# Optimizing a Trainium2 kernel written in Bass

```python
import jax
import jax.numpy as jnp
from jax import lax
import numpy as np

D_MODEL = 2048
BATCH = 1
SEQ = 512
DEPTH = 1

HEAD_DIM = 128
MOBA_HEADS = 8
MOBA_WIDTH = MOBA_HEADS * HEAD_DIM
MOBA_BLOCK = 256
MOBA_TOPK = 3
MOBA_QROWS = 128
ROPE_THETA = 500000.0
ROPE_DIM = HEAD_DIM // 4

DN_HEADS = 8
DN_KEY_DIM = 128
DN_VAL_DIM = 128
DN_QK_WIDTH = DN_HEADS * DN_KEY_DIM
DN_V_WIDTH = DN_HEADS * DN_VAL_DIM
DN_CONV_WIDTH = 4
DN_CHUNK = 64

MOE_GROUPS = 4
MOE_EXPERTS_PER_GROUP = 8
MOE_EXPERTS = MOE_GROUPS * MOE_EXPERTS_PER_GROUP
MOE_TOPK = 2
MOE_FF = 512
MOE_ROWS = 128

NORM_EPS = 1e-6
N_MOD = 6

IN_SPLITS = (MOBA_WIDTH, MOBA_WIDTH, MOBA_WIDTH, 2 * DN_QK_WIDTH + DN_V_WIDTH, DN_V_WIDTH,
             DN_HEADS, DN_HEADS, D_MODEL, D_MODEL)
IN_WIDTH = 3 * MOBA_WIDTH + 2 * DN_QK_WIDTH + 2 * DN_V_WIDTH + 2 * DN_HEADS + 2 * D_MODEL

kernel_name = "hybrid_moba_gdn_hmoe_block"

def _rms_norm(x, gain):
    x32 = x.astype(jnp.float32)
    y = x32 * lax.rsqrt(jnp.mean(x32 * x32, axis=-1, keepdims=True) + NORM_EPS)
    return y.astype(x.dtype) * gain

def _l2_normalize(x):
    return x * lax.rsqrt(jnp.sum(x * x, axis=-1, keepdims=True) + NORM_EPS)

def _partial_rotary(x, positions):
    half = ROPE_DIM // 2
    inv_freq = jnp.power(ROPE_THETA, -jnp.arange(half, dtype=jnp.float32) * (2.0 / ROPE_DIM))
    ang = positions.astype(jnp.float32)[..., None] * inv_freq
    cos = jnp.cos(ang)[:, :, None, :]
    sin = jnp.sin(ang)[:, :, None, :]
    x1 = x[..., :half]
    x2 = x[..., half:ROPE_DIM]
    rot = jnp.concatenate([x1 * cos - x2 * sin, x2 * cos + x1 * sin], axis=-1).astype(x.dtype)
    return jnp.concatenate([rot, x[..., ROPE_DIM:]], axis=-1)

def _padded_rows(n_valid, n_groups, rows):
    total = n_valid + n_groups * (rows - 1)
    return -(-total // rows) * rows

def _group_rows(group_id, valid, n_groups, n_rows, rows):
    key = jnp.where(valid, group_id, n_groups)
    order = jnp.argsort(key).astype(jnp.int32)
    skey = key[order]
    counts = jnp.bincount(key, length=n_groups + 1)[:n_groups]
    padded = (counts + rows - 1) // rows * rows
    start = jnp.cumsum(counts) - counts
    pad_end = jnp.cumsum(padded)
    pad_start = pad_end - padded
    gc = jnp.minimum(skey, n_groups - 1)
    rank = jnp.arange(key.shape[0], dtype=jnp.int32) - start[gc]
    dest = jnp.where(skey < n_groups, pad_start[gc] + rank, n_rows)
    row_src = jnp.zeros((n_rows,), jnp.int32).at[dest].set(order, mode="drop")
    row_valid = jnp.zeros((n_rows,), bool).at[dest].set(True, mode="drop")
    block_start = jnp.arange(n_rows // rows, dtype=pad_end.dtype) * rows
    block_group = jnp.minimum(jnp.searchsorted(pad_end, block_start, side="right"), n_groups - 1)
    return row_src, row_valid, block_group

def _moba_single(q, k, v):
    s_pad, dh = q.shape
    nblk = s_pad // MOBA_BLOCK
    scale = dh ** -0.5
    qb = q.reshape(nblk, MOBA_BLOCK, dh)
    kb = k.reshape(nblk, MOBA_BLOCK, dh)
    vb = v.reshape(nblk, MOBA_BLOCK, dh)
    causal = jnp.tril(jnp.ones((MOBA_BLOCK, MOBA_BLOCK), dtype=bool))
    s_own = jnp.where(causal, jnp.einsum("nqd,nkd->nqk", qb, kb) * scale, -jnp.inf)
    lse_own = jax.nn.logsumexp(s_own, axis=-1)
    o_own = jnp.einsum("nqk,nkd->nqd", jnp.exp(s_own - lse_own[..., None]), vb).reshape(s_pad, dh)
    lse_own = lse_own.reshape(s_pad)
    k_sel = min(MOBA_TOPK, nblk - 1)
    if k_sel == 0:
        return o_own
    q_blk = jnp.arange(s_pad) // MOBA_BLOCK
    k_mean = kb.mean(axis=1)
    gate = jnp.where(jnp.arange(nblk)[None, :] < q_blk[:, None], q @ k_mean.T, -jnp.inf)
    _, sel_blk = lax.top_k(gate, k_sel)
    sel_valid = jnp.arange(k_sel)[None, :] < q_blk[:, None]
    n_valid = sum(MOBA_BLOCK * min(k_sel, j) for j in range(nblk))
    n_rows = _padded_rows(n_valid, nblk, MOBA_QROWS)
    row_src, row_valid, block_of = _group_rows(sel_blk.reshape(-1), sel_valid.reshape(-1),
                                               nblk, n_rows, MOBA_QROWS)
    row_q = row_src // k_sel

    def attend_block(args):
        rq, blk = args
        s = (q[rq] @ kb[blk].T) * scale
        lse = jax.nn.logsumexp(s, axis=-1)
        return jnp.exp(s - lse[:, None]) @ vb[blk], lse

    o_sel, lse_sel = lax.map(attend_block, (row_q.reshape(-1, MOBA_QROWS), block_of))
    o_sel = o_sel.reshape(n_rows, dh)
    lse_sel = jnp.where(row_valid, lse_sel.reshape(n_rows), -jnp.inf)
    m = jnp.maximum(lse_own, jax.ops.segment_max(lse_sel, row_q, num_segments=s_pad))
    w_sel = jnp.where(row_valid, jnp.exp(lse_sel - m[row_q]), 0.0)
    w_own = jnp.exp(lse_own - m)
    num = w_own[:, None] * o_own + jax.ops.segment_sum(w_sel[:, None] * o_sel, row_q, num_segments=s_pad)
    den = w_own + jax.ops.segment_sum(w_sel, row_q, num_segments=s_pad)
    return num / den[:, None]

def _moba_branch(q, k, v, positions):
    b, s, _ = q.shape
    q = _partial_rotary(q.reshape(b, s, MOBA_HEADS, HEAD_DIM), positions)
    k = _partial_rotary(k.reshape(b, s, MOBA_HEADS, HEAD_DIM), positions)
    v = v.reshape(b, s, MOBA_HEADS, HEAD_DIM)
    pad = (-s) % MOBA_BLOCK

    def prep(t):
        t = t.astype(jnp.float32).transpose(0, 2, 1, 3)
        return jnp.pad(t, ((0, 0), (0, 0), (0, pad), (0, 0)))

    o = jax.vmap(jax.vmap(_moba_single))(prep(q), prep(k), prep(v))
    return o[:, :, :s].transpose(0, 2, 1, 3).reshape(b, s, MOBA_WIDTH)

def _causal_short_conv(x, w):
    return lax.conv_general_dilated(
        x, w[:, None, :].astype(x.dtype), window_strides=(1,),
        padding=[(DN_CONV_WIDTH - 1, 0)], dimension_numbers=("NWC", "WIO", "NWC"),
        feature_group_count=x.shape[-1])

def _chunk_gated_delta(q, k, v, g, beta):
    b, h, s, dk = q.shape
    dv = v.shape[-1]
    c = DN_CHUNK
    n = s // c
    q = (q * dk ** -0.5).reshape(b, h, n, c, dk)
    k = k.reshape(b, h, n, c, dk)
    v = v.reshape(b, h, n, c, dv)
    beta = beta.reshape(b, h, n, c)
    big_g = jnp.cumsum(g.reshape(b, h, n, c), axis=-1)
    lower = jnp.tril(jnp.ones((c, c), dtype=bool))
    strict = jnp.tril(jnp.ones((c, c), dtype=bool), -1)
    diff = big_g[..., :, None] - big_g[..., None, :]
    decay = jnp.where(lower, jnp.exp(jnp.where(lower, diff, 0.0)), 0.0)
    k_beta = k * beta[..., None]
    v_beta = v * beta[..., None]
    kk = jnp.where(strict, jnp.einsum("bhnid,bhnjd->bhnij", k_beta, k) * decay, 0.0)
    a_mat = kk + jnp.eye(c, dtype=kk.dtype)
    u = lax.linalg.triangular_solve(a_mat, v_beta, left_side=True, lower=True, unit_diagonal=True)
    w = lax.linalg.triangular_solve(a_mat, k_beta * jnp.exp(big_g)[..., None],
                                    left_side=True, lower=True, unit_diagonal=True)
    qk = jnp.einsum("bhnid,bhnjd->bhnij", q, k) * decay
    q_dec = q * jnp.exp(big_g)[..., None]
    g_last = big_g[..., -1]
    k_tail = k * jnp.exp(g_last[..., None] - big_g)[..., None]
    xs = tuple(jnp.moveaxis(t, 2, 0) for t in (q_dec, qk, u, w, k_tail, g_last))

    def step(state, chunk):
        q_c, qk_c, u_c, w_c, kt_c, gl_c = chunk
        v_new = u_c - jnp.einsum("bhcd,bhdv->bhcv", w_c, state)
        o_c = jnp.einsum("bhcd,bhdv->bhcv", q_c, state) + jnp.einsum("bhij,bhjv->bhiv", qk_c, v_new)
        state = state * jnp.exp(gl_c)[..., None, None] + jnp.einsum("bhcd,bhcv->bhdv", kt_c, v_new)
        return state, o_c

    state0 = jnp.zeros((b, h, dk, dv), jnp.float32)
    _, o = lax.scan(step, state0, xs)
    return jnp.moveaxis(o, 0, 2).reshape(b, h, s, dv)

def _deltanet_branch(qkv, z, beta_raw, a_raw, conv_w, a_log, dt_bias, out_gain):
    b, s, _ = qkv.shape
    qkv = jax.nn.silu(_causal_short_conv(qkv, conv_w)).astype(jnp.float32)
    q, k, v = jnp.split(qkv, [DN_QK_WIDTH, 2 * DN_QK_WIDTH], axis=-1)
    q = _l2_normalize(q.reshape(b, s, DN_HEADS, DN_KEY_DIM))
    k = _l2_normalize(k.reshape(b, s, DN_HEADS, DN_KEY_DIM))
    v = v.reshape(b, s, DN_HEADS, DN_VAL_DIM)
    beta = jax.nn.sigmoid(beta_raw.astype(jnp.float32))
    g = -jnp.exp(a_log.astype(jnp.float32)) * jax.nn.softplus(
        a_raw.astype(jnp.float32) + dt_bias.astype(jnp.float32))
    o = _chunk_gated_delta(q.transpose(0, 2, 1, 3), k.transpose(0, 2, 1, 3), v.transpose(0, 2, 1, 3),
                           g.transpose(0, 2, 1), beta.transpose(0, 2, 1))
    o = o.transpose(0, 2, 1, 3)
    o = _rms_norm(o, out_gain.astype(jnp.float32)) * jax.nn.silu(
        z.reshape(b, s, DN_HEADS, DN_VAL_DIM).astype(jnp.float32))
    return o.reshape(b, s, DN_V_WIDTH)

def _mixer(u, positions, w_in, conv_w, a_log, dt_bias, dn_out_norm, w_branch_moba, w_branch_delta, w_out):
    proj = u @ w_in
    split_at = np.cumsum(IN_SPLITS)[:-1].tolist()
    qa, ka, va, qkv_d, z_d, beta_raw, a_raw, gate_a, gate_b = jnp.split(proj, split_at, axis=-1)
    y_a = _moba_branch(qa, ka, va, positions).astype(u.dtype)
    y_b = _deltanet_branch(qkv_d, z_d, beta_raw, a_raw, conv_w, a_log, dt_bias, dn_out_norm).astype(u.dtype)
    merged = jax.nn.sigmoid(gate_a) * (y_a @ w_branch_moba) + jax.nn.sigmoid(gate_b) * (y_b @ w_branch_delta)
    return merged @ w_out

def _hier_moe(h, w_rg, b_rg, w_re, b_re, w_gate, w_up, w_down):
    b, s, d = h.shape
    t = b * s
    tok = h.reshape(t, d)
    g_logits = (tok @ w_rg + b_rg).astype(jnp.float32)
    p_group = jax.nn.softmax(g_logits, axis=-1)
    g_sel = jnp.argmax(g_logits, axis=-1)
    e_logits = (tok @ w_re + b_re).astype(jnp.float32).reshape(t, MOE_GROUPS, MOE_EXPERTS_PER_GROUP)
    e_logits = jnp.take_along_axis(e_logits, g_sel[:, None, None], axis=1)[:, 0]
    top_p, top_e = lax.top_k(jax.nn.softmax(e_logits, axis=-1), MOE_TOPK)
    weights = jnp.take_along_axis(p_group, g_sel[:, None], axis=1) * top_p / jnp.sum(top_p, axis=-1, keepdims=True)
    expert_id = g_sel[:, None] * MOE_EXPERTS_PER_GROUP + top_e
    n_rows = _padded_rows(t * MOE_TOPK, MOE_EXPERTS, MOE_ROWS)
    row_src, row_valid, block_expert = _group_rows(
        expert_id.reshape(-1), jnp.ones((t * MOE_TOPK,), bool), MOE_EXPERTS, n_rows, MOE_ROWS)
    row_tok = row_src // MOE_TOPK
    row_w = jnp.where(row_valid, weights.reshape(-1)[row_src], 0.0)

    def expert_block(args):
        rt, e = args
        xb = tok[rt]
        return (jax.nn.silu(xb @ w_gate[e]) * (xb @ w_up[e])) @ w_down[e]

    yb = lax.map(expert_block, (row_tok.reshape(-1, MOE_ROWS), block_expert)).reshape(n_rows, d)
    y = jax.ops.segment_sum(yb * row_w[:, None].astype(yb.dtype), row_tok, num_segments=t)
    return y.reshape(b, s, d)

def setup_inputs(seed: int = 0) -> dict:
    key = jax.random.key(seed)
    ks = jax.random.split(key, 24)
    nrm = jax.random.normal
    f32 = jnp.float32
    x = nrm(ks[0], (BATCH, SEQ, D_MODEL), f32)
    c = nrm(ks[1], (BATCH, D_MODEL), f32)
    offset = jax.random.randint(ks[2], (BATCH, 1), 0, 4096, dtype=jnp.int32)
    positions = (offset + jnp.arange(SEQ, dtype=jnp.int32)[None, :]).astype(jnp.int32)

    def gain(k):
        return 1.0 + 0.05 * nrm(k, (DEPTH, D_MODEL), f32)

    gk = jax.random.split(ks[3], 5)
    dt = jnp.exp(jax.random.uniform(ks[4], (DEPTH, DN_HEADS), f32, np.log(1e-3), np.log(1e-1)))
    return {
        "x": x,
        "c": c,
        "positions": positions,
        "w_ada": nrm(ks[5], (DEPTH, D_MODEL, N_MOD * D_MODEL), f32) * (0.5 * D_MODEL ** -0.5),
        "b_ada": 0.02 * nrm(ks[6], (DEPTH, N_MOD * D_MODEL), f32),
        "norm_mix_pre": gain(gk[0]),
        "norm_mix_post": gain(gk[1]),
        "norm_ffn_pre": gain(gk[2]),
        "norm_ffn_post": gain(gk[3]),
        "w_in": nrm(ks[7], (DEPTH, D_MODEL, IN_WIDTH), f32) * D_MODEL ** -0.5,
        "conv_w": nrm(ks[8], (DEPTH, DN_CONV_WIDTH, 2 * DN_QK_WIDTH + DN_V_WIDTH), f32) * DN_CONV_WIDTH ** -0.5,
        "dn_a_log": jnp.log(jax.random.uniform(ks[9], (DEPTH, DN_HEADS), f32, 1.0, 16.0)),
        "dn_dt_bias": dt + jnp.log(-jnp.expm1(-dt)),
        "dn_out_norm": 1.0 + 0.05 * nrm(gk[4], (DEPTH, DN_VAL_DIM), f32),
        "w_branch_moba": nrm(ks[10], (DEPTH, MOBA_WIDTH, D_MODEL), f32) * MOBA_WIDTH ** -0.5,
        "w_branch_delta": nrm(ks[11], (DEPTH, DN_V_WIDTH, D_MODEL), f32) * DN_V_WIDTH ** -0.5,
        "w_out": nrm(ks[12], (DEPTH, D_MODEL, D_MODEL), f32) * D_MODEL ** -0.5,
        "router_group_w": nrm(ks[13], (DEPTH, D_MODEL, MOE_GROUPS), f32) * D_MODEL ** -0.5,
        "router_group_b": 0.01 * nrm(ks[14], (DEPTH, MOE_GROUPS), f32),
        "router_expert_w": nrm(ks[15], (DEPTH, D_MODEL, MOE_EXPERTS), f32) * D_MODEL ** -0.5,
        "router_expert_b": 0.01 * nrm(ks[16], (DEPTH, MOE_EXPERTS), f32),
        "expert_w_gate": nrm(ks[17], (DEPTH, MOE_EXPERTS, D_MODEL, MOE_FF), f32) * D_MODEL ** -0.5,
        "expert_w_up": nrm(ks[18], (DEPTH, MOE_EXPERTS, D_MODEL, MOE_FF), f32) * D_MODEL ** -0.5,
        "expert_w_down": nrm(ks[19], (DEPTH, MOE_EXPERTS, MOE_FF, D_MODEL), f32) * MOE_FF ** -0.5,
    }

def reference(x, c, positions, w_ada, b_ada, norm_mix_pre, norm_mix_post, norm_ffn_pre, norm_ffn_post,
              w_in, conv_w, dn_a_log, dn_dt_bias, dn_out_norm, w_branch_moba, w_branch_delta, w_out,
              router_group_w, router_group_b, router_expert_w, router_expert_b,
              expert_w_gate, expert_w_up, expert_w_down):
    cond = jax.nn.silu(c)
    for layer in range(DEPTH):
        mod = cond @ w_ada[layer] + b_ada[layer]
        sh1, sc1, gt1, sh2, sc2, gt2 = [m[:, None, :] for m in jnp.split(mod, N_MOD, axis=-1)]
        u = _rms_norm(x, norm_mix_pre[layer]) * (1.0 + sc1) + sh1
        y = _mixer(u, positions, w_in[layer], conv_w[layer], dn_a_log[layer], dn_dt_bias[layer],
                   dn_out_norm[layer], w_branch_moba[layer], w_branch_delta[layer], w_out[layer])
        x = x + gt1 * _rms_norm(y, norm_mix_post[layer])
        u = _rms_norm(x, norm_ffn_pre[layer]) * (1.0 + sc2) + sh2
        y = _hier_moe(u, router_group_w[layer], router_group_b[layer], router_expert_w[layer],
                      router_expert_b[layer], expert_w_gate[layer], expert_w_up[layer], expert_w_down[layer])
        x = x + gt2 * _rms_norm(y, norm_ffn_post[layer])
    return x


_drawn_inputs = setup_inputs


def setup_inputs(seed=0):
    import zlib

    import numpy as np

    out = dict(_drawn_inputs(seed))
    spreads = {}
    factors = {'norm_ffn_post': 3.917, 'router_expert_b': 2.953}
    for name, (base, spread) in spreads.items():
        noise = np.random.default_rng([zlib.crc32(name.encode()), seed]).standard_normal(out[name].shape)
        drawn = base * np.exp(spread * noise) if base else spread * noise
        out[name] = jnp.asarray(drawn.astype(out[name].dtype))
    for name, factor in factors.items():
        out[name] = (out[name] * factor).astype(out[name].dtype)
    return out
```

```python
from contextlib import ExitStack, contextmanager

import numpy as np

import concourse.bass as bass
from concourse import mybir

F32 = mybir.dt.float32
F32R = mybir.dt.float32r
I32 = mybir.dt.int32
ALU = mybir.AluOpType
ACT = mybir.ActivationFunctionType
AX = mybir.AxisListType.X

P = 128
SEQ = 512
D = 2048
ND = D // P
NT = SEQ // P
HD = 128
HEADS = 8
WIDTH = HEADS * HD
ROPE = HD // 4
HALF = ROPE // 2
ROPE_THETA = 500000.0
CHUNK = 64
CONV = 4
GROUPS, PER_GROUP = 4, 8
EXPERTS = GROUPS * PER_GROUP
FF = 512
NF = FF // P
ROWS = 128
MAX_OVER = (SEQ * 2) // (ROWS + 1)
COLS = 512
SLOT = 4 * COLS
EPS = 1e-6
NEG = -1.0e30
IN_QA, IN_KA, IN_VA, IN_DN, IN_Z = 0, WIDTH, 2 * WIDTH, 3 * WIDTH, 6 * WIDTH
IN_BETA = 7 * WIDTH
IN_GA = IN_BETA + 2 * HEADS
IN_GB = IN_GA + D
LEVELS = (1, 2, 4, 8, 16, 32)

TWO_PI_1 = 6.28125
TWO_PI_2 = float(np.float32(np.round((2 * np.pi - 6.28125) * 2.0 ** 20) / 2.0 ** 20))
TWO_PI_3 = float(np.float32(2 * np.pi - 6.28125 - TWO_PI_2))
ROUND = 1.5 * 2.0 ** 23
PI_BELOW = 3.1415925

(C_ID, C_ONES, C_CUM, C_TAIL, C_DEC, C_CAUSAL, C_RANK, C_ROT, C_LEV) = (0, 1, 2, 3, 4, 5, 6, 7, 8)
N_CONST = C_LEV + len(LEVELS)


def shape_constants():
    c = np.zeros((N_CONST, P, P), np.float32)
    k, i = np.meshgrid(np.arange(P), np.arange(P), indexing="ij")
    same = (k // CHUNK) == (i // CHUNK)
    c[C_ID] = np.eye(P)
    c[C_ONES] = 1.0
    c[C_CUM] = same & (k <= i)
    c[C_TAIL] = same & (k > i)
    c[C_DEC] = np.where(same & (i >= k), 0.0, NEG)
    c[C_CAUSAL] = np.where(i <= k, 0.0, NEG)
    c[C_RANK] = k < i
    for a in range(HALF):
        c[C_ROT, a + HALF, a] = -1.0
        c[C_ROT, a, a + HALF] = 1.0
    for n, s in enumerate(LEVELS):
        c[C_LEV + n] = (k // (2 * s) == i // (2 * s)) & (k % (2 * s) < s) & (i % (2 * s) >= s)
    planes = np.ascontiguousarray(c.transpose(1, 0, 2))
    small = np.zeros((P, 64), np.float32)
    small[:, 0:32] = np.arange(32)
    small[:, 32] = np.arange(P)
    f = np.power(np.float64(ROPE_THETA), -np.arange(HALF) * (2.0 / ROPE)).astype(np.float32)
    small[0:ROPE, 33] = np.concatenate([f, f])
    small[:, 40:40 + MAX_OVER] = EXPERTS + np.arange(MAX_OVER)
    return planes, small


class Chain:

    def __init__(self, eng, sem):
        self.eng, self.sem, self.base, self.off = eng, sem, 0, 0

    def do(self, ins):
        ins.then_inc(self.sem, 1)
        self.off += 1
        return ins

    def sync(self):
        self.eng.wait_ge(self.sem, self.base + self.off)

    def link(self, ins):
        self.do(ins)
        self.sync()

    @contextmanager
    def loop(self, n, per):
        base, off = self.base, self.off
        with self.eng.Fori(0, n) as i:
            self.base, self.off = i * per + (base + off), 0
            yield i
            assert self.off == per, f"this loop signals {self.off} times a turn"
        self.base, self.off = base, off + n * per


class Carve:

    def __init__(self, *areas):
        self.areas = [[x, 0] for x in areas]

    def take(self, shape):
        n = int(np.prod(shape[1:]))
        for area in self.areas:
            x, at = area
            if at + n <= x.shape[1]:
                area[1] += n
                part = x[:, at:at + n]
                if len(shape) == 3:
                    part = part.rearrange("p (a b) -> p a b", a=shape[1])
                return part
        raise ValueError("the areas are full")


def build(nc, a, out, dram):
    ctx = ExitStack()
    with ctx:
        starts = {}

        def sb(name, shape, dt=F32):
            starts[name] = -(-nc.sbuf_base // 32) * 32
            return ctx.enter_context(nc.sbuf_tensor(name, shape, dt))

        def rounded(name, shape):
            return nc.alloc_sbuf_tensor_at(name + "_r", shape, F32R, offset=starts[name])

        def sem(name):
            return ctx.enter_context(nc.semaphore(name))

        proj_t = dram("proj_t", [18, NT, P, SEQ])
        proj_n = dram("proj_n", [NT, P, 4 * COLS])
        mod_rows = dram("mod_rows", [16, COLS])
        T_QA, T_KA, T_DN, T_GA, T_GB = 0, 2, 4, 10, 14

        planes = sb("planes", [P, N_CONST, P])
        small = sb("small", [P, 64])
        half_pi = sb("half_pi", [P, 1])
        eps = sb("eps", [P, 1])
        cond = sb("cond", [P, ND])
        g_pre = sb("g_pre", [P, 2, ND])
        b_col = sb("b_col", [P, 6 * ND])
        conv_col = sb("conv_col", [P, CONV * 3 * HEADS])
        mod_col = sb("mod_col", [P, 6 * ND])
        a_col = sb("a_col", [P, 2, ND])
        row_out = sb("row_out", [1, 2, COLS])
        cos_t = sb("cos_t", [ROPE, SEQ])
        sin_t = sb("sin_t", [ROPE, SEQ])
        ba = sb("ba", [P, NT, 2 * HEADS])
        raw = [sb(f"raw{i}", [P, SLOT]) for i in range(4)]
        raw_r = [rounded(f"raw{i}", [P, SLOT]) for i in range(4)]
        hi = [sb(f"hi{i}", [P, SLOT], F32R) for i in range(2)]
        area = sb("area", [P, 2 * ND, SEQ])
        area_r = rounded("area", [P, 2 * ND, SEQ])
        u_hi, u_lo = area_r[:, 0:ND, :], area_r[:, ND:2 * ND, :]
        area_1, area_2 = area[:, 0:ND, :], area[:, ND:2 * ND, :]
        stage = sb("stage", [P, 4, COLS])
        acc = sb("acc", [P, 2, COLS])
        x_all = sb("x_all", [P, NT, D])
        x_all_r = rounded("x_all", [P, NT, D])
        stage_r = rounded("stage", [P, 4, COLS])
        ada_ring = [x_all[:, s, :] for s in range(NT)]
        vecs = stage[:, 0, 0:3 * P].rearrange("p (v c) -> p v c", v=3)
        u_tmp = acc
        ssq = sb("ssq", [P, NT])
        rstd = sb("rstd", [P, NT])
        w_ba = sb("w_ba", [P, ND, 2 * HEADS])
        cond_raw = sb("cond_raw", [P, ND])
        cond_sig = sb("cond_sig", [P, ND])
        ba_hi = sb("ba_hi", [P, ND, 2 * HEADS], F32R)
        ba_lo = sb("ba_lo", [P, ND, 2 * HEADS], F32R)
        ang_mem = sb("ang_mem", [P, SLOT])
        ang_r = rounded("ang_mem", [P, SLOT])
        ang = ang_mem[0:ROPE, :].rearrange("p (a n) -> p a n", a=4)
        pos_i = sb("pos_i", [ROPE, SEQ], I32)

        ps = [ctx.enter_context(nc.psum_tensor(f"ps{i}", [P, 512], F32)) for i in range(8)]
        ident = planes[:, C_ID, :]
        ones = planes[:, C_ONES, :]

        s_const = sem("s_const")
        s_x = sem("s_x")
        s_slot = [sem(f"s_slot{i}") for i in range(4)]
        s_ada_slot = [sem(f"s_ada_slot{i}") for i in range(4)]
        s_hi = sem("s_hi")
        s_lo = sem("s_lo")
        s_used = sem("s_used")
        s_ada1_used = sem("s_ada1_used")
        s_ada_used = sem("s_ada_used")
        s_acc = sem("s_acc")
        s_mod = sem("s_mod")
        s_xn = sem("s_xn")
        s_ut = sem("s_ut")
        s_uhi = sem("s_uhi")
        s_ulo = sem("s_ulo")
        s_ba_split = sem("s_ba_split")
        s_bank = sem("s_bank")
        s_ev_a = sem("s_ev_a")
        s_ev_v = sem("s_ev_v")
        s_stored = [sem(f"s_stored{i}") for i in range(4)]
        s_row = sem("s_row")
        s_row_out = sem("s_row_out")
        s_prep_pe = sem("s_prep_pe")
        s_prep_a = sem("s_prep_a")
        s_prep_v = sem("s_prep_v")
        s_act = sem("s_act")
        s_dve = sem("s_dve")
        s_pool = sem("s_pool")

        w_in, w_ada = a["w_in"][0], a["w_ada"][0]
        w_in_v = w_in.rearrange("(t p) n -> p t n", p=P)
        w_ada_v = w_ada.rearrange("(t p) n -> p t n", p=P)
        x_v = a["x"][0].rearrange("(t p) d -> p t d", p=P)


        yb_t = dram("yb_t", [HEADS, P, SEQ])
        dtb_row = sb("dtb_row", [P, HEADS])
        alog_row = sb("alog_row", [P, HEADS])
        og_row = sb("og_row", [P, HD])
        dec_in = sb("dec_in", [P, 4, NT, HEADS])
        g_nat = sb("g_nat", [P, NT, HEADS])
        beta = sb("beta", [P, NT, HEADS])
        gcum = sb("gcum", [P, NT, HEADS])
        tail = sb("tail", [P, NT, HEADS])
        beta_g = sb("beta_g", [P, NT, HEADS])
        PAD = CONV - 1
        dn = Carve(area_1.rearrange("p a b -> p (a b)"), area_2.rearrange("p a b -> p (a b)"))
        xin = dn.take([P, 3, PAD + SEQ])
        cv = dn.take([P, 3, SEQ])
        kb = dn.take([P, SEQ])
        e_g = dn.take([P, SEQ])
        q_dec = dn.take([P, SEQ])
        dec = dn.take([P, SEQ])
        n_t = dn.take([P, SEQ])
        qk_t = dn.take([P, SEQ])
        k_bg = dn.take([P, NT, HD])
        k_tail = dn.take([P, NT, HD])
        v_b = dn.take([P, NT, HD])
        inv = dn.take([P, SEQ])
        inv_t = dn.take([P, SEQ])
        z_in = dn.take([P, NT, HD])
        state = dn.take([P, HD])
        v_new = dn.take([P, HD])
        g_last = dn.take([P, SEQ // CHUNK])
        o_ms = dn.take([P, NT])
        w_t, u_sol, x_sb = e_g, kb, dec
        sq = dn.take([P, 2, SEQ])
        z_sig = k_bg
        c_lev = [cv[:, 1, :], cv[:, 2, :]]
        o_sb = cv[:, 0, :]

        s_rows = sem("s_rows")
        s_dn_in = sem("s_dn_in")
        s_dn_z = sem("s_dn_z")
        s_conv = sem("s_conv")
        s_sig = sem("s_sig")
        s_silu = sem("s_silu")
        s_sq = sem("s_sq")
        s_ss = sem("s_ss")
        s_nroot = sem("s_nroot")
        s_unit = sem("s_unit")
        s_gb = sem("s_gb")
        s_gbc = sem("s_gbc")
        s_bbc = sem("s_bbc")
        s_eg = sem("s_eg")
        s_darg = sem("s_darg")
        s_dec = sem("s_dec")
        s_kb = sem("s_kb")
        s_gram = sem("s_gram")
        s_knat = sem("s_knat")
        s_vnat = sem("s_vnat")
        s_nt = sem("s_nt")
        s_qkt = sem("s_qkt")
        s_first = sem("s_first")
        s_kfac = sem("s_kfac")
        s_vb = sem("s_vb")
        s_inv1 = sem("s_inv1")
        s_inv1_out = sem("s_inv1_out")
        s_clev = sem("s_clev")
        s_xm = sem("s_xm")
        s_xc = sem("s_xc")
        s_corr = sem("s_corr")
        s_inv = sem("s_inv")
        s_uw = sem("s_uw")
        s_u = sem("s_u")
        s_w = sem("s_w")
        s_ws = sem("s_ws")
        s_vn = sem("s_vn")
        s_sd = sem("s_sd")
        s_state = sem("s_state")
        s_osq = sem("s_osq")
        s_oms = sem("s_oms")
        s_oroot = sem("s_oroot")
        s_zsig = sem("s_zsig")
        s_on = sem("s_on")
        s_ot = sem("s_ot")
        s_ot_out = sem("s_ot_out")
        s_yb = sem("s_yb")
        NL = len(LEVELS) - 1
        NC = SEQ // CHUNK
        TB, SB_, XB = ps[4], ps[5], ps[6]

        def tiles(x):
            return x.rearrange("p (t c) -> p t c", t=NT)

        def column(x, h):
            return x[:, :, bass.ds(h, 1)].broadcast_to([P, NT, HD])

        def plane(c):
            return planes[:, c:c + 1, :].broadcast_to([P, NT, P])

        PARTS = [
            (IN_DN, T_DN, 4, False, 12), (IN_DN + 4 * COLS, T_DN + 4, 2, False, None),
            (IN_Z, 2, 2, True, None), (IN_VA, 0, 2, True, None),
            (IN_QA, T_QA, 4, False, 16), (IN_GA, T_GA, 4, False, 8), (IN_GB, T_GB, 4, False, 20),
        ]
        N_ADA1 = 8

        ya_t = dram("ya_t", [HEADS, P, SEQ])
        SCALE = HD ** -0.5
        at = Carve(area_1.rearrange("p a b -> p (a b)"), area_2.rearrange("p a b -> p (a b)"))
        at_q = [at.take([P, SEQ]) for _ in range(2)]
        at_k = [at.take([P, SEQ]) for _ in range(2)]
        at_v = [at.take([P, NT, HD]) for _ in range(2)]
        rot = at.take([P, SEQ])
        prob = at.take([P, NT, SEQ])
        prob_t = at.take([P, NT, SEQ])
        at_o = at.take([P, SEQ])
        at_raw = sb("at_raw", [P, NT])
        at_max = sb("at_max", [P, NT])
        at_sum = sb("at_sum", [P, NT])
        s_at_in = [sem(f"s_at_in{i}") for i in range(2)]
        s_rot = sem("s_rot")
        s_roped = sem("s_roped")
        s_sc = sem("s_sc")
        s_nmax = sem("s_nmax")
        s_exp = sem("s_exp")
        s_prob = sem("s_prob")
        s_pt = sem("s_pt")
        s_pt_out = sem("s_pt_out")
        s_av = sem("s_av")
        s_av_out = sem("s_av_out")
        s_ya = sem("s_ya")

        N_IN = sum(p[2] for p in PARTS)
        yh = u_hi[:, :, :]
        yl = u_lo[:, :, :]
        merged = x_all[:, :, :].rearrange("p m (k n) -> p (m k) n", n=SEQ)
        y_nat = x_all
        gate_in = sb("gate_in", [P, 4, SEQ])
        s_yl = sem("s_yl")
        s_yh = sem("s_yh")
        s_ysplit = sem("s_ysplit")
        s_gate = [sem(f"s_gate{i}") for i in range(2)]
        s_gsig = sem("s_gsig")
        s_merged = sem("s_merged")

        rows4 = dram("rows4", [4, D])
        x1_s = dram("x1_s", [SEQ, D])
        u2_s = dram("u2_s", [SEQ, D])
        yb_s = dram("yb_s", [2 * SEQ, D])
        NB = EXPERTS + MAX_OVER
        table = dram("table", [P * (NB + 1), 1], I32)
        mr = sb("mr", [ND, 4, P])
        br = sb("br", [ND, 4, P])
        gr = sb("gr", [ND, 3, P])
        ra = Carve(area_2.rearrange("p a b -> p (a b)"))
        row_g1, row_a2, row_s2 = ra.take([P, D]), ra.take([P, D]), ra.take([P, D])
        x_in = ra.take([P, D])
        u2_t = area_1
        w_r = sb("w_r", [P, ND, GROUPS + EXPERTS])
        NR = GROUPS + EXPERTS
        b_r = sb("b_r", [P, NR])
        ss2 = sb("ss2", [P, 2, NT])
        s_mr = sem("s_mr")
        s_rows4 = sem("s_rows4")
        s_rowb = sem("s_rowb")
        s_xin2 = sem("s_xin2")
        s_res = sem("s_res")
        s_rooty = sem("s_rooty")
        s_x1 = sem("s_x1")
        s_root1 = sem("s_root1")
        s_u2 = sem("s_u2")
        s_x1_out = sem("s_x1_out")
        s_u2_out = sem("s_u2_out")
        s_u2t = sem("s_u2t")
        s_u2t_out = sem("s_u2t_out")
        s_route_v = sem("s_route_v")
        s_route_a = sem("s_route_a")
        s_route_pe = sem("s_route_pe")
        s_table = sem("s_table")
        s_logit = sem("s_logit")

        rt = Carve(stage[:, :, :].rearrange("p a b -> p (a b)"))
        logit = rt.take([P, NT, NR])
        e_log = rt.take([P, NT, EXPERTS])
        tmp32 = rt.take([P, NT, EXPERTS])
        oh1 = rt.take([P, NT, EXPERTS])
        oh2 = rt.take([P, NT, EXPERTS])
        both = rt.take([P, NT, EXPERTS])
        rank = rt.take([P, NT, EXPERTS])
        oh_g = rt.take([P, NT, GROUPS])
        tmp4 = rt.take([P, NT, GROUPS])
        r1 = rt.take([P, 16, NT])
        cnt = rt.take([P, 4, EXPERTS])
        tmp7 = rt.take([P, MAX_OVER, EXPERTS])
        over_t = rt.take([P, P])
        place = rt.take([P, 2, NT])
        wts = sb("wts", [P, 2, NT])
        place_i = sb("place_i", [P, 2 * NT], I32)
        id_i = sb("id_i", [P, 2 * NT], I32)
        plan_f = sb("plan_f", [P, MAX_OVER + 1])
        plan = sb("plan", [P, MAX_OVER + 1], I32)
        fill = sb("fill", [P, NB + 1], I32)
        row_i = sb("row_i", [P, NB + 1], I32)
        row_f = sb("row_f", [P, NB + 1])
        tok_f = sb("tok_f", [P, NB + 1])
        tok_i = sb("tok_i", [P, NB + 1], I32)
        NO_ROW = 1 << 20

        mo = Carve(area_2.rearrange("p a b -> p (a b)"), area_1.rearrange("p a b -> p (a b)"))
        mo_r = Carve(u_lo.rearrange("p a b -> p (a b)"), u_hi.rearrange("p a b -> p (a b)"))
        m_raw = [raw[i][:, :] for i in range(4)] + [mo.take([P, SLOT]) for _ in range(8)]
        m_raw_r = [raw_r[i][:, :] for i in range(4)] + [mo_r.take([P, SLOT]) for _ in range(8)]
        m_hi = [hi[i][:, :] for i in range(2)] + [
            ang_r[:, :], stage_r[:, :, :].rearrange("p a b -> p (a b)")]
        mx = Carve(x_all[:, :, :].rearrange("p a b -> p (a b)"))
        xg = mx.take([P, D])
        y_e = mx.take([P, D])
        mx_r = Carve(x_all_r[:, 2:4, :].rearrange("p a b -> p (a b)"))
        xe_hi = mx_r.take([P, ND, P])
        xe_lo = mx_r.take([P, ND, P])
        me = Carve(gate_in[:, :, :].rearrange("p a b -> p (a b)"))
        h_sig, h_e = me.take([P, FF]), me.take([P, FF])
        gate_in_r = rounded("gate_in", [P, 4, SEQ])
        ht_hi = gate_in_r[:, 2, :].rearrange("p (a b) -> p a b", a=NF)
        ht_lo = gate_in_r[:, 3, :].rearrange("p (a b) -> p a b", a=NF)
        g_idx = sb("g_idx", [P, 1], I32)
        y_idx = sb("y_idx", [P, 1], I32)
        s_mslot = s_slot + s_ada_slot + [sem(f"s_mslot{i}") for i in range(4)]
        mslot_base = [16 * (N_ADA1 + N_IN + 8)] * 4 + [16 * 16] * 4 + [0] * 4
        s_mhi = sem("s_mhi")
        s_mlo = sem("s_mlo")
        s_mused = sem("s_mused")
        s_gi = sem("s_gi")
        s_yi = sem("s_yi")
        s_xg = sem("s_xg")
        s_xt = sem("s_xt")
        s_xehi = sem("s_xehi")
        s_xelo = sem("s_xelo")
        s_hsig = sem("s_hsig")
        s_h = sem("s_h")
        s_ht = sem("s_ht")
        s_hthi = sem("s_hthi")
        s_htlo = sem("s_htlo")
        s_ybank = sem("s_ybank")
        s_ye_a = sem("s_ye_a")
        s_ye_v = sem("s_ye_v")
        s_ysc = sem("s_ysc")

        fi = Carve(*m_raw)
        row_g2 = fi.take([P, D])
        f_y = [[fi.take([P, D]) for _ in range(2)] for _ in range(2)]
        f_x = [fi.take([P, D]) for _ in range(2)]
        f_sq = fi.take([P, D])
        ss_f = sb("ss_f", [P, NT])
        s_g2 = sem("s_g2")
        s_f_y = sem("s_f_y")
        s_f_ss = sem("s_f_ss")
        s_f_out = sem("s_f_out")
        s_out = [sem(f"s_out{i}") for i in range(2)]

        def split3(eng, bank, l_hi, l_lo, r_hi, r_lo, first, last):
            eng.matmul(bank, l_hi, r_hi, start=first, stop=False)
            eng.matmul(bank, l_hi, r_lo, start=False, stop=False)
            return eng.matmul(bank, l_lo, r_hi, start=False, stop=last)

        block = ctx.enter_context(nc.Block())

        @block.sync
        def _(sp):
            sp.dma_start(planes[:, :, :], a["planes"]).then_inc(s_const, 16)
            sp.dma_start(small[:, :], a["small"]).then_inc(s_const, 16)
            sp.dma_start(vecs[0:ND, 0, :], a["c"][0].rearrange("(t p) -> t p", p=P)).then_inc(s_const, 16)
            sp.dma_start(vecs[ND:2 * ND, 0, :], a["norm_mix_pre"][0].rearrange("(t p) -> t p", p=P)).then_inc(s_const, 16)
            sp.dma_start(vecs[2 * ND:3 * ND, 0, :], a["norm_ffn_pre"][0].rearrange("(t p) -> t p", p=P)).then_inc(s_const, 16)
            sp.dma_start(vecs[0:96, 1, :], a["b_ada"][0].rearrange("(t p) -> t p", p=P)).then_inc(s_const, 16)
            sp.dma_start(vecs[0:96, 2, :], a["conv_w"][0].rearrange("k (t p) -> (k t) p", p=P)).then_inc(s_const, 16)
            sp.dma_start(pos_i[:, :], a["positions"].broadcast_to([ROPE, SEQ])).then_inc(s_const, 16)
            with sp.Fori(0, N_ADA1) as c:
                for s in range(4):
                    sp.wait_ge(s_ada1_used, c * 4 + (s + 1))
                    sp.dma_start(raw[s][:, :].rearrange("p (t n) -> p t n", t=4),
                                 w_ada_v[:, 4 * s:4 * s + 4, bass.ds(c * COLS, COLS)]).then_inc(s_slot[s], 16)
            for t in range(NT):
                sp.dma_start(x_all[:, t, :], x_v[:, t, :]).then_inc(s_x, 16)
            sp.dma_start(w_ba[:, :, :], w_in_v[:, :, IN_BETA:IN_BETA + 2 * HEADS]).then_inc(s_x, 16)
            sp.wait_ge(s_ada1_used, 4 + 4 * N_ADA1)
            done = ada_done = 0
            for col0, row0, n, natural, ada0 in PARTS:
                with sp.Fori(0, n) as c:
                    for s in range(4):
                        sp.wait_ge(s_used, (c + done) * 4 + (s + 1))
                        sp.dma_start(raw[s][:, :].rearrange("p (t n) -> p t n", t=4),
                                     w_in_v[:, 4 * s:4 * s + 4, bass.ds(c * COLS + col0, COLS)]).then_inc(s_slot[s], 16)
                    if ada0 is not None:
                        for s in range(4):
                            if s == 0 and ada_done == 0:
                                sp.wait_ge(s_ut, ND)
                            sp.wait_ge(s_ada_used, (c + ada_done) * 4 + (s + 1))
                            sp.dma_start(ada_ring[s].rearrange("p (t n) -> p t n", t=4),
                                         w_ada_v[:, 4 * s:4 * s + 4, bass.ds((c + ada0) * COLS, COLS)]).then_inc(s_ada_slot[s], 16)
                done += n
                if ada0 is not None:
                    ada_done += n
            w_moba = a["w_branch_moba"][0].rearrange("(t p) n -> p t n", p=P)
            w_delta = a["w_branch_delta"][0].rearrange("(t p) n -> p t n", p=P)
            w_out = a["w_out"][0].rearrange("(t p) n -> p t n", p=P)

            def merge_slot(c, s):
                sp.wait_ge(s_used, (c + N_IN) * 4 + (s + 1))
                sp.dma_start(raw[s][:, :].rearrange("p (t n) -> p t n", t=4),
                             (w_moba, w_delta)[s // 2][:, 4 * (s % 2):4 * (s % 2) + 4, bass.ds(c * COLS, COLS)]).then_inc(s_slot[s], 16)

            for s in range(4):
                merge_slot(0, s)
            for b in range(4):
                sp.wait_ge(s_stored[b], 16 * N_IN)
            sp.wait_ge(s_ot_out, HEADS)
            sp.wait_ge(s_yb, 16 * HEADS)
            tq = proj_t.rearrange("c b p n -> (c b) p n")
            with sp.Fori(0, HEADS // 2) as i:
                for par in range(2):
                    sp.wait_ge(s_av, i * 2 + (par + 1))
                    for dst, first in ((at_q[par], T_QA * 4), (at_k[par], T_KA * 4)):
                        sp.dma_start(dst, tq[bass.ds(i * 2 + (par + first), 1)].rearrange("a p n -> (a p) n")).then_inc(s_at_in[par], 16)
                    sp.dma_start(at_v[par], proj_n[:, :, bass.ds((i * 2 + par) * HD, HD)].rearrange("b p n -> p b n")).then_inc(s_at_in[par], 16)
            sp.wait_ge(s_ya, 16 * HEADS)
            sp.dma_start(area_2[:, 0:HEADS, :], ya_t.rearrange("h p n -> p h n")).then_inc(s_yl, 16)
            sp.dma_start(area_2[:, HEADS:2 * HEADS, :], yb_t.rearrange("h p n -> p h n")).then_inc(s_yl, 16)
            with sp.Fori(1, 4) as c:
                for s in range(4):
                    merge_slot(c, s)
            with sp.Fori(0, 4) as c:
                for s in range(4):
                    sp.wait_ge(s_used, (c + (N_IN + 4)) * 4 + (s + 1))
                    sp.dma_start(raw[s][:, :].rearrange("p (t n) -> p t n", t=4),
                                 w_out[:, 4 * s:4 * s + 4, bass.ds(c * COLS, COLS)]).then_inc(s_slot[s], 16)
            sp.dma_start(w_r[:, :, 0:GROUPS], a["router_group_w"][0].rearrange("(t p) n -> p t n", p=P)).then_inc(s_rowb, 16)
            sp.dma_start(w_r[:, :, GROUPS:NR], a["router_expert_w"][0].rearrange("(t p) n -> p t n", p=P)).then_inc(s_rowb, 16)
            sp.dma_start(b_r[:, 0:GROUPS], a["router_group_b"].broadcast_to([P, GROUPS])).then_inc(s_rowb, 16)
            sp.dma_start(b_r[:, GROUPS:NR], a["router_expert_b"].broadcast_to([P, EXPERTS])).then_inc(s_rowb, 16)
            sp.wait_ge(s_used, 4 + 4 * (N_IN + 8))
            sp.wait_ge(s_rows4, 16)
            for n, dst in enumerate((row_g1, row_s2, row_a2)):
                sp.dma_start(dst, rows4[n:n + 1, :].broadcast_to([P, D])).then_inc(s_rowb, 16)
            for m in range(NT):
                if m:
                    sp.wait_ge(s_x1, m)
                sp.dma_start(x_in, x_v[:, m, :]).then_inc(s_xin2, 16)

            def expert_slot(e, j, s):
                sp.wait_ge(s_mused, j * 12 + (s + 1))
                if s < 8:
                    src = a[("expert_w_gate", "expert_w_up")[s // 4]][0, bass.ds(e, 1), (s % 4) * 4 * P:(s % 4 + 1) * 4 * P, :]
                    sp.dma_start(m_raw[s].rearrange("p (t n) -> p t n", t=4),
                                 src.rearrange("a (t p) n -> p (a t) n", p=P)).then_inc(s_mslot[s], 16)
                else:
                    src = a["expert_w_down"][0, bass.ds(e, 1), (s - 8) * P:(s - 7) * P, :]
                    sp.dma_start(m_raw[s], src.rearrange("a p n -> (a p) n")).then_inc(s_mslot[s], 16)

            for s in range(4):
                expert_slot(0, 0, s)
            sp.wait_ge(s_u2, NT)
            sp.wait_ge(s_logit, 1)
            for s in range(4, 12):
                expert_slot(0, 0, s)
            with sp.Fori(1, EXPERTS) as j:
                for s in range(12):
                    expert_slot(j, j, s)
            sp.wait_ge(s_route_v, 6)
            n_blocks = sp.value_load(plan[0:1, MAX_OVER:MAX_OVER + 1], min_val=EXPERTS, max_val=NB)
            with sp.If(n_blocks > EXPERTS):
                with sp.Fori(EXPERTS, n_blocks) as j:
                    e = sp.value_load(plan[0:1, bass.ds(j - EXPERTS, 1)], min_val=0, max_val=EXPERTS - 1)
                    for s in range(12):
                        expert_slot(e, j, s)
            for s in range(3):
                expert_slot(0, n_blocks, s)
            sp.wait_ge(s_mused, n_blocks * 12 + 12)
            sp.wait_ge(s_mlo, n_blocks * 12 + 3)
            sp.dma_start(row_g2, rows4[3:4, :].broadcast_to([P, D])).then_inc(s_g2, 16)
            sp.wait_ge(s_ysc, n_blocks * 16)
            for m in range(NT):
                if m >= 2:
                    sp.wait_ge(s_f_out, m - 1)
                    sp.wait_ge(s_out[m % 2], (m // 2) * 16)
                for k in range(2):
                    sp.dma_start(f_y[m % 2][k], yb_s[k * SEQ + m * P:k * SEQ + (m + 1) * P, :]).then_inc(s_at_in[m % 2], 16)
                sp.dma_start(f_x[m % 2], x1_s[m * P:(m + 1) * P, :]).then_inc(s_at_in[m % 2], 16)

        @block.gpsimd
        def _(pool):
            done = ada_done = 0
            for col0, row0, n, natural, ada0 in PARTS:
                with pool.Fori(0, n) as c:
                    for b in range(4):
                        pool.wait_ge((s_ev_a, s_ev_v)[b // 2], (c + done) * 2 + (b % 2 + 3))
                        dst = (proj_n[b, :, bass.ds((c + row0) * COLS, COLS)] if natural else
                               proj_t[bass.ds(c + row0, 1), b].rearrange("a p n -> (a p) n"))
                        pool.dma_start(dst,
                                     stage[:, b, :]).then_inc(s_stored[b], 16)
                    if ada0 is not None:
                        pool.wait_ge(s_row, c + (ada_done + 2))
                        pool.dma_start(mod_rows[bass.ds(c + (ada0 - N_ADA1), 1), :], row_out[:, 0, :]).then_inc(s_row_out, 16)
                done += n
                if ada0 is not None:
                    ada_done += n
            for b in range(4):
                pool.wait_ge(s_stored[b], 16 * done)

            pool.dma_start(dtb_row[:, :], a["dn_dt_bias"].broadcast_to([P, HEADS])).then_inc(s_rows, 16)
            pool.dma_start(alog_row[:, :], a["dn_a_log"].broadcast_to([P, HEADS])).then_inc(s_rows, 16)
            pool.dma_start(og_row[:, :], a["dn_out_norm"].broadcast_to([P, HD])).then_inc(s_rows, 16)
            pool.memset(xin[:, :, 0:PAD], 0.0).then_inc(s_pool, 1)
            pool.wait_ge(s_pool, 1)
            blocks = proj_t.rearrange("c b p n -> (c b) p n")[T_DN * 4:(T_DN + 6) * 4].rearrange("(j h) p n -> h p j n", j=3)
            with pool.Fori(0, HEADS) as h:
                pool.wait_ge(s_unit, h * 2)
                pool.dma_start(xin[:, :, PAD:PAD + SEQ], blocks[bass.ds(h, 1)].rearrange("a p j n -> (a p) j n")).then_inc(s_dn_in, 16)
                pool.wait_ge(s_on, h)
                pool.dma_start(z_in[:, :, :], proj_n[:, :, bass.ds(h * HD + WIDTH, HD)].rearrange("b p n -> p b n")).then_inc(s_dn_z, 16)
                for n in range(NL):
                    if n == 0:
                        pool.wait_ge(s_vnat, h + 1)
                        pool.wait_ge(s_gram, h * 2 + 2)
                        pool.wait_ge(s_nt, h + 1)
                    if n >= 2:
                        pool.wait_ge(s_xm, h * NL + (n - 1))
                    pool.tensor_tensor(tiles(c_lev[n % 2]), tiles(n_t[:, :]), plane(C_LEV + 1 + n), ALU.mult).then_inc(s_clev, 1)
                pool.wait_ge(s_ot_out, h + 1)
                pool.dma_start(yb_t[bass.ds(h, 1)].rearrange("a p n -> (a p) n"), o_sb).then_inc(s_yb, 16)
            pool.wait_ge(s_yb, 16 * HEADS)
            with pool.Fori(0, HEADS) as h:
                pool.wait_ge(s_av_out, h + 1)
                pool.dma_start(ya_t[bass.ds(h, 1)].rearrange("a p n -> (a p) n"), at_o).then_inc(s_ya, 16)
            tg = proj_t.rearrange("c b p n -> (c b) p n")
            with pool.Fori(0, 4) as c:
                for b in range(4):
                    pool.wait_ge(s_merged, c * 4 + (b + 3))
                    for k, first in enumerate((T_GA * 4, T_GB * 4)):
                        pool.dma_start(gate_in[:, (b % 2) * 2 + k, :],
                                       tg[bass.ds(c * 4 + (b + first), 1)].rearrange("a p n -> (a p) n")).then_inc(s_gate[b % 2], 16)
            pool.wait_ge(s_row_out, 16 * 16)
            flat = mod_rows.rearrange("c n -> (c n)")
            pool.dma_start(mr[:, :, :], flat.rearrange("(v t p) -> t v p", v=4, p=P)).then_inc(s_mr, 16)
            pool.dma_start(br[:, :, :], a["b_ada"][0, 2 * D:6 * D].rearrange("(v t p) -> t v p", v=4, p=P)).then_inc(s_mr, 16)
            for n, g in enumerate(("norm_mix_post", "norm_ffn_pre", "norm_ffn_post")):
                pool.dma_start(gr[:, n, :], a[g][0].rearrange("(t p) -> t p", p=P)).then_inc(s_mr, 16)
            pool.wait_ge(s_res, 1)
            pool.dma_start(rows4.rearrange("v (t p) -> t v p", p=P), mr[:, :, :]).then_inc(s_rows4, 16)
            for m in range(NT):
                pool.wait_ge(s_x1, m + 1)
                pool.dma_start(x1_s[m * P:(m + 1) * P, :], y_nat[:, m, :]).then_inc(s_x1_out, 16)
            for m in range(NT):
                pool.wait_ge(s_u2, m + 1)
                pool.dma_start(u2_s[m * P:(m + 1) * P, :], y_nat[:, m, :]).then_inc(s_u2_out, 16)
            pool.memset(fill[:, :], NO_ROW).then_inc(s_pool, 1)
            pool.wait_ge(s_pool, 2)
            pool.dma_start(table.rearrange("(p b) a -> p (b a)", p=P), fill[:, :]).then_inc(s_table, 16)
            pool.wait_ge(s_table, 16)
            pool.wait_ge(s_route_v, 8)
            for n in range(2 * NT):
                pool.indirect_dma_start(out=table, out_offset=bass.IndirectOffsetOnAxis(ap=place_i[:, n:n + 1], axis=0),
                                        in_=id_i[:, n:n + 1], in_offset=None,
                                        bounds_check=P * (NB + 1) - 1, oob_is_err=False).then_inc(s_table, 16)
            pool.wait_ge(s_table, 16 + 16 * 2 * NT)
            pool.dma_start(row_i[:, :], table.rearrange("(p b) a -> p (b a)", p=P)).then_inc(s_table, 16)
            pool.wait_ge(s_u2_out, 16 * NT)
            pool.wait_ge(s_u2t, ND)
            pool.memset(xg, 0.0).then_inc(s_pool, 1)
            pool.wait_ge(s_pool, 3)
            pool.wait_ge(s_route_v, 9)
            pool.wait_ge(s_route_v, 6)
            n_blocks = pool.value_load(plan[0:1, MAX_OVER:MAX_OVER + 1], min_val=EXPERTS, max_val=NB)

            def gather(j, n):
                pool.tensor_copy(g_idx[:, :], tok_i[:, bass.ds(j, 1)]).then_inc(s_gi, 1)
                pool.wait_ge(s_gi, n)
                pool.nop(nofuse=True)
                pool.indirect_dma_start(out=xg, out_offset=None, in_=u2_s,
                                        in_offset=bass.IndirectOffsetOnAxis(ap=g_idx[:, :], axis=0),
                                        bounds_check=SEQ - 1, oob_is_err=False).then_inc(s_xg, 16)

            gather(0, 1)
            with pool.Fori(0, n_blocks) as j:
                pool.wait_ge(s_xt, j * 4 + 4)
                pool.wait_ge(s_xg, j * 16 + 16)
                gather(j + 1, j + 2)
                pool.wait_ge(s_ysc, j * 16)
                pool.tensor_copy(y_idx[:, :], row_i[:, bass.ds(j, 1)]).then_inc(s_yi, 1)
                pool.wait_ge(s_yi, j + 1)
                pool.wait_ge(s_ye_a, j * 2 + 2)
                pool.wait_ge(s_ye_v, j * 2 + 2)
                pool.nop(nofuse=True)
                pool.indirect_dma_start(out=yb_s, out_offset=bass.IndirectOffsetOnAxis(ap=y_idx[:, :], axis=0),
                                        in_=y_e, in_offset=None,
                                        bounds_check=2 * SEQ - 1, oob_is_err=False).then_inc(s_ysc, 16)
            pool.wait_ge(s_xg, n_blocks * 16 + 16)
            pool.wait_ge(s_ysc, n_blocks * 16)
            pool.nop(nofuse=True)
            for m in range(NT):
                pool.wait_ge(s_f_out, m + 1)
                pool.dma_start(out[0, m * P:(m + 1) * P, :], f_x[m % 2]).then_inc(s_out[m % 2], 16)
            for par in range(2):
                pool.wait_ge(s_out[par], 16 * NT // 2)

        @block.tensor
        def _(pe):
            pe.sem_inc(s_used, 4)
            pe.wait_ge(s_const, 16 * 8)
            pe.transpose(ps[7][:, 0:48], vecs[0:48, 0, :], ident[0:48, 0:48])
            pe.transpose(ps[7][:, 64:160], vecs[0:96, 1, :], ident[0:96, 0:96])
            pe.transpose(ps[7][:, 192:288], vecs[0:96, 2, :], ident[0:96, 0:96]).then_inc(s_prep_pe, 1)

            def mod_columns(c, n, par):
                pe.wait_ge(s_acc, n)
                for j in range(4):
                    mm = pe.matmul(ps[6][:, bass.ds(c * 4 + j, 1)], acc[:, par, j * P:(j + 1) * P],
                                   ones[:, 0:1], start=True, stop=True)
                mm.then_inc(s_mod, 1)

            with pe.Fori(0, N_ADA1 // 2) as i:
                for par in range(2):
                    mod_columns(i * 2 + par, i * 2 + (par + 1), par)
            pe.wait_ge(s_xn, NT)
            for t in range(ND):
                if t >= 4:
                    pe.wait_ge(s_uhi, t - 3)
                for m in range(NT):
                    tr = pe.transpose(ps[t % 4][:, m * P:(m + 1) * P], x_all[:, m, t * P:(t + 1) * P], ident)
                tr.then_inc(s_ut, 1)
            pe.wait_ge(s_ulo, ND)
            pe.wait_ge(s_ba_split, 2)
            for m in range(NT):
                tok = slice(m * P, (m + 1) * P)
                for t in range(ND):
                    mm = split3(pe, ps[5][:, m * 16:(m + 1) * 16], u_hi[:, t, tok], u_lo[:, t, tok],
                                ba_hi[:, t, :], ba_lo[:, t, :], t == 0, t == ND - 1)
            mm.then_inc(s_prep_pe, 1)
            pe.wait_ge(s_uhi, ND)
            pe.wait_ge(s_prep_a, 5)

            done = ada_done = 0
            for col0, row0, n, natural, ada0 in PARTS:
                with pe.Fori(0, n) as c:
                    for s in range(4):
                        pe.wait_ge(s_lo, (c + done) * 4 + (s + 1))
                        for b in range(4):
                            if s == 0:
                                pe.wait_ge((s_ev_a, s_ev_v)[b // 2], (c + done) * 2 + (b % 2 + 1))
                            for t in range(4):
                                cols = slice(t * COLS, (t + 1) * COLS)
                                part = slice(t * COLS + b * P, t * COLS + (b + 1) * P)
                                w_lo = raw_r[s]
                                k = 4 * s + t
                                first, last = k == 0, k == ND - 1
                                if natural:
                                    tok = slice(b * P, (b + 1) * P)
                                    mm = split3(pe, ps[b][:, :], u_hi[:, k, tok], u_lo[:, k, tok],
                                                hi[s % 2][:, cols], w_lo[:, cols], first, last)
                                else:
                                    mm = split3(pe, ps[b][:, :], hi[s % 2][:, part], w_lo[:, part],
                                                u_hi[:, k, :], u_lo[:, k, :], first, last)
                            if s == 3 and b < 3:
                                mm.then_inc(s_bank, 1)
                        mm.then_inc(s_used, 1)
                    if ada0 is not None:
                        pe.wait_ge(s_acc, c + (N_ADA1 + ada_done + 1))
                        pe.wait_ge(s_row, c + (ada_done + 1))
                        pe.matmul(ps[7][0:1, :], ones[:, 0:1], acc[:, 0, :], start=True, stop=True).then_inc(s_mod, 1)
                done += n
                if ada0 is not None:
                    ada_done += n

            pe.wait_ge(s_prep_v, 4)
            for t in range(NT):
                pe.matmul(ps[5][:, t * HEADS:(t + 1) * HEADS], planes[:, C_CUM, :], g_nat[:, t, :], start=True, stop=True)
                mm = pe.matmul(ps[5][:, (NT + t) * HEADS:(NT + t + 1) * HEADS], planes[:, C_TAIL, :], g_nat[:, t, :], start=True, stop=True)
            mm.then_inc(s_prep_pe, 1)

            def per_tile(bank, lhs, rhs):
                for t in range(NT):
                    c = slice(t * P, (t + 1) * P)
                    mm = pe.matmul(bank[:, c], lhs[:, c], rhs if rhs.shape[1] == P else rhs[:, c], start=True, stop=True)
                return mm

            def per_tile_t(bank, x):
                for t in range(NT):
                    c = slice(t * P, (t + 1) * P)
                    mm = pe.transpose(bank[:, c], x[:, c], ident)
                return mm

            def dn_norms(h):
                for j, bank in ((1, TB), (0, SB_)):
                    pe.wait_ge(s_sq, h * 2 + (2 - j))
                    if j == 1:
                        pe.wait_ge(s_state, h * NC)
                        pe.wait_ge(s_on, h)
                        pe.wait_ge(s_ot_out, h)
                    pe.matmul(bank[:, :], ones, sq[:, j, :], start=True, stop=True).then_inc(s_ss, 1)

            def dn_decay(h):
                pe.wait_ge(s_gb, h + 1)
                per_tile(XB, inv, planes[:, C_CUM, :]).then_inc(s_gbc, 1)
                pe.wait_ge(s_nroot, h * 2 + 1)
                per_tile(TB, inv_t, ident).then_inc(s_bbc, 1)

            def dn_gram(h):
                pe.wait_ge(s_kb, h + 1)
                pe.wait_ge(s_nroot, h * 2 + 2)
                per_tile(SB_, cv[:, 1, :], kb[:, :]).then_inc(s_gram, 1)
                pe.wait_ge(s_unit, h * 2 + 2)
                per_tile(TB, cv[:, 1, :], cv[:, 0, :]).then_inc(s_gram, 1)

            def dn_naturals(h):
                pe.wait_ge(s_darg, h + 1)
                per_tile_t(XB, cv[:, 1, :]).then_inc(s_knat, 1)
                pe.wait_ge(s_silu, h * 3 + 3)
                pe.wait_ge(s_qkt, h + 1)
                per_tile_t(TB, cv[:, 2, :]).then_inc(s_vnat, 1)
                pe.wait_ge(s_first, h + 1)
                per_tile_t(SB_, inv_t[:, :]).then_inc(s_inv1, 1)

            def dn_level_x(h, n):
                if n == 0:
                    pe.wait_ge(s_inv1_out, h + 1)
                    pe.wait_ge(s_kfac, h * 2 + 2)
                else:
                    pe.wait_ge(s_inv, h * (2 * NL - 1) + 2 * n)
                pe.wait_ge(s_clev, h * NL + (n + 1))
                per_tile(XB, c_lev[n % 2], inv[:, :]).then_inc(s_xm, 1)

            def dn_level_corr(h, n):
                pe.wait_ge(s_xc, h * NL + (n + 1))
                if n == 0:
                    pe.wait_ge(s_vb, h + 1)
                mm = per_tile(TB, x_sb, inv_t[:, :])
                if n < NL - 1:
                    mm = per_tile(SB_, inv_t, x_sb[:, :])
                mm.then_inc(s_corr, 1)

            def dn_solve(h):
                pe.wait_ge(s_inv, (h + 1) * (2 * NL - 1))
                per_tile(TB, inv_t, v_b[:, :, :].rearrange("p t c -> p (t c)"))
                per_tile(SB_, k_bg[:, :, :].rearrange("p t c -> p (t c)"), inv_t[:, :]).then_inc(s_uw, 1)

            def rows_of(c):
                return slice((c % 2) * CHUNK, (c % 2 + 1) * CHUNK), c // 2

            def dn_scan_w(h, c):
                r, t = rows_of(c)
                if c == 1:
                    pe.wait_ge(s_w, h + 1)
                pe.wait_ge(s_state, h * NC + c)
                pe.nop(nofuse=True)
                pe.matmul(XB[r, 0:HD], w_t[:, c * CHUNK:(c + 1) * CHUNK], state[:, :], start=True, stop=True).then_inc(s_ws, 1)

            def dn_scan_o(h, c):
                r, t = rows_of(c)
                vn = u_sol[r, t * HD:(t + 1) * HD] if c == 0 else v_new[r, :]
                if c == 0:
                    pe.wait_ge(s_u, h + 1)
                    pe.wait_ge(s_w, h + 1)
                else:
                    pe.matmul(TB[r, t * HD:(t + 1) * HD], q_dec[:, c * CHUNK:(c + 1) * CHUNK], state[:, :], start=True, stop=False)
                    pe.wait_ge(s_vn, h * (NC - 1) + c)
                pe.nop(nofuse=True)
                pe.matmul(TB[r, t * HD:(t + 1) * HD], qk_t[r, c * CHUNK:(c + 1) * CHUNK], vn, start=c == 0, stop=True)
                pe.matmul(SB_[:, 0:HD], k_tail[r, t, :], vn, start=True, stop=True).then_inc(s_sd, 1)

            def dn_out(h):
                pe.wait_ge(s_on, h + 1)
                per_tile_t(XB, o_sb).then_inc(s_ot, 1)

            with pe.Fori(0, HEADS) as h:
                dn_norms(h)
                dn_decay(h)
                dn_gram(h)
                dn_naturals(h)
                for n in range(NL):
                    dn_level_x(h, n)
                    dn_level_corr(h, n)
                dn_solve(h)
                for c in range(NC):
                    if c:
                        dn_scan_w(h, c)
                    dn_scan_o(h, c)
                dn_out(h)
            pe.sem_inc(s_av, 2)
            with pe.Fori(0, HEADS // 2) as i:
                for par in range(2):
                    h = i * 2 + par
                    pe.wait_ge(s_at_in[par], i * 48 + 48)
                    pe.wait_ge(s_pt_out, h * NT)
                    pe.nop(nofuse=True)
                    pe.matmul(ps[4][0:ROPE, :], planes[0:ROPE, C_ROT, 0:ROPE], at_q[par][0:ROPE, :], start=True, stop=True).then_inc(s_rot, 1)
                    pe.matmul(ps[5][0:ROPE, :], planes[0:ROPE, C_ROT, 0:ROPE], at_k[par][0:ROPE, :], start=True, stop=True).then_inc(s_rot, 1)
                    pe.wait_ge(s_roped, h * 2 + 2)
                    pe.wait_ge(s_av_out, h)
                    for m in range(NT):
                        pe.matmul(ps[m][:, 0:(m + 1) * P], at_q[par][:, m * P:(m + 1) * P], at_k[par][:, 0:(m + 1) * P],
                                  start=True, stop=True).then_inc(s_sc, 1)
                    for m in range(NT):
                        pe.wait_ge(s_prob, h * NT + (m + 1))
                        for k in range(m + 1):
                            tr = pe.transpose(ps[4 + k][:, m * P:(m + 1) * P], prob[:, m, k * P:(k + 1) * P], ident)
                    tr.then_inc(s_pt, 1)
                    for k in range(NT):
                        pe.wait_ge(s_pt_out, h * NT + (k + 1))
                        mm = pe.matmul(ps[0][:, k * P:SEQ], at_v[par][:, k, :], prob_t[:, k, k * P:SEQ],
                                       start=k == 0, stop=k == NT - 1)
                    mm.then_inc(s_av, 1)

            pe.wait_ge(s_ysplit, 4)
            pe.wait_ge(s_av_out, HEADS)
            with pe.Fori(0, 4) as c:
                for s in range(4):
                    pe.wait_ge(s_lo, (c + N_IN) * 4 + (s + 1))
                    for b in range(4):
                        if s == 0:
                            pe.wait_ge(s_merged, c * 4 + (b + 1))
                        for t in range(4):
                            part = slice(t * COLS + b * P, t * COLS + (b + 1) * P)
                            k = (s % 2) * 4 + t
                            y = (s // 2) * HEADS + k
                            mm = split3(pe, ps[b + 4 * (s // 2)][:, :], hi[s % 2][:, part], raw_r[s][:, part],
                                        yh[:, y, :], yl[:, y, :], k == 0, k == HEADS - 1)
                        if s == 3 and b < 3:
                            mm.then_inc(s_bank, 1)
                    mm.then_inc(s_used, 1)

            pe.wait_ge(s_ysplit, 8)
            pe.wait_ge(s_merged, 4 + 16)

            with pe.Fori(0, 4) as c:
                for s in range(4):
                    pe.wait_ge(s_lo, (c + (N_IN + 4)) * 4 + (s + 1))
                    for b in range(4):
                        if s == 0:
                            pe.wait_ge((s_ev_a, s_ev_v)[b // 2], (c + N_IN) * 2 + (b % 2 + 1))
                        tok = slice(b * P, (b + 1) * P)
                        for t in range(4):
                            cols = slice(t * COLS, (t + 1) * COLS)
                            k = 4 * s + t
                            mm = split3(pe, ps[b][:, :], yh[:, k, tok], yl[:, k, tok],
                                        hi[s % 2][:, cols], raw_r[s][:, cols], k == 0, k == ND - 1)
                        if s == 3 and b < 3:
                            mm.then_inc(s_bank, 1)
                    mm.then_inc(s_used, 1)

            pe.sem_inc(s_mused, 12)
            pe.wait_ge(s_u2, NT)
            pe.wait_ge(s_ev_a, 2 + 2 * (N_IN + 4))
            pe.wait_ge(s_ev_v, 2 + 2 * (N_IN + 4))
            for t in range(ND):
                if t >= 4:
                    pe.wait_ge(s_u2t_out, t - 3)
                for m in range(NT):
                    tr = pe.transpose(ps[t % 4][:, m * P:(m + 1) * P], y_nat[:, m, t * P:(t + 1) * P], ident)
                tr.then_inc(s_u2t, 1)
            pe.wait_ge(s_u2t_out, ND)
            pe.wait_ge(s_rowb, 16 * 7)
            for m in range(NT):
                for t in range(ND):
                    mm = pe.matmul(ps[4][:, m * NR:(m + 1) * NR], u2_t[:, t, m * P:(m + 1) * P], w_r[:, t, :],
                                   start=t == 0, stop=t == ND - 1)
            mm.then_inc(s_logit, 1)
            pe.wait_ge(s_route_v, 3)
            for m in range(NT):
                for k in range(m):
                    pe.matmul(ps[5][:, m * EXPERTS:(m + 1) * EXPERTS], ones, both[:, k, :], start=k == 0, stop=False)
                pe.matmul(ps[5][:, m * EXPERTS:(m + 1) * EXPERTS], planes[:, C_RANK, :], both[:, m, :], start=m == 0, stop=True)
            for m in range(NT):
                mm = pe.matmul(ps[6][:, 0:EXPERTS], ones, both[:, m, :], start=m == 0, stop=m == NT - 1)
            mm.then_inc(s_route_pe, 1)
            pe.wait_ge(s_route_v, 4)
            pe.transpose(ps[7][0:EXPERTS, 0:P], cnt[:, 1, :], ident).then_inc(s_route_pe, 1)
            pe.wait_ge(s_route_v, 5)
            pe.matmul(ps[5][:, 256:256 + EXPERTS], over_t[0:EXPERTS, :], planes[0:EXPERTS, C_RANK, 0:EXPERTS],
                      start=True, stop=True).then_inc(s_route_pe, 1)

            def block_transposes(n):
                for q in range(4):
                    if q >= 2:
                        pe.wait_ge(s_xelo, n + (q - 1))
                    for t in range(4):
                        tr = pe.transpose(ps[2 + q % 2][:, t * P:(t + 1) * P], xg[:, (4 * q + t) * P:(4 * q + t + 1) * P], ident)
                    tr.then_inc(s_xt, 1)

            pe.wait_ge(s_route_v, 6)
            n_blocks = pe.value_load(plan[0:1, MAX_OVER:MAX_OVER + 1], min_val=EXPERTS, max_val=NB)
            pe.wait_ge(s_xg, 16)
            block_transposes(0)
            with pe.Fori(0, n_blocks) as j:
                for s in range(8):
                    if s % 4 == 0:
                        pe.wait_ge(s_xelo, j * 4 + 4)
                        pe.wait_ge((s_htlo, s_h)[s // 4], j)
                    pe.wait_ge(s_mlo, j * 12 + (s + 1))
                    for t in range(4):
                        cols = slice(t * COLS, (t + 1) * COLS)
                        k = 4 * (s % 4) + t
                        mm = split3(pe, ps[s // 4][:, :], xe_hi[:, k, :], xe_lo[:, k, :],
                                    m_hi[s % 4][:, cols], m_raw_r[s][:, cols], k == 0, k == ND - 1)
                    mm.then_inc(s_mused, 1)
                pe.wait_ge(s_xg, j * 16 + 32)
                block_transposes(j * 4 + 4)
                pe.wait_ge(s_h, j + 1)
                for t in range(NF):
                    tr = pe.transpose(ps[0][:, t * P:(t + 1) * P], h_e[:, t * P:(t + 1) * P], ident)
                tr.then_inc(s_ht, 1)
                pe.wait_ge(s_htlo, j + 1)
                for s in range(8, 12):
                    pe.wait_ge(s_mlo, j * 12 + (s + 1))
                    for b in range(4):
                        if s == 8:
                            pe.wait_ge((s_ye_a, s_ye_v)[b // 2], j * 2)
                        cols = slice(b * COLS, (b + 1) * COLS)
                        mm = split3(pe, ps[4 + b][:, :], ht_hi[:, s - 8, :], ht_lo[:, s - 8, :],
                                    m_hi[s % 4][:, cols], m_raw_r[s][:, cols], s == 8, s == 11)
                        if s == 11 and b < 3:
                            mm.then_inc(s_ybank, 1)
                    mm.then_inc(s_mused, 1)

        @block.scalar
        def _(act):
            ch = Chain(act, s_act)
            act.sem_inc(s_ev_a, 2)
            act.wait_ge(s_prep_pe, 1)
            ch.do(act.copy(cond_raw[:, :], ps[7][:, 0:ND]))
            ch.do(act.activation(cond_sig[:, :], ps[7][:, 0:ND], ACT.Sigmoid))
            ch.do(act.copy(g_pre[:, :, :].rearrange("p a t -> p (a t)"), ps[7][:, ND:3 * ND]))
            ch.do(act.copy(b_col[:, :], ps[7][:, 64:160]))
            ch.link(act.copy(conv_col[:, :], ps[7][:, 192:288]))
            act.sem_inc(s_row, 1)
            act.sem_inc(s_prep_a, 1)
            act.wait_ge(s_prep_v, 1)
            act.activation(sin_t[:, :], ang[:, 2, :], ACT.Sin).then_inc(s_prep_a, 1)
            act.activation(cos_t[:, :], ang[:, 3, :], ACT.Sin, scale=-1.0, bias=half_pi[0:ROPE, :]).then_inc(s_prep_a, 1)
            for m in range(NT):
                act.wait_ge(s_x, 16 * (NT + 1))
                ch.do(act.activation(area_1[:, m * 4:(m + 1) * 4, :].rearrange("p a b -> p (a b)"),
                                     x_all[:, m, :], ACT.Square, accum_out=ssq[:, m:m + 1]))
            ch.sync()
            act.activation(rstd[:, :], ssq[:, :], ACT.Sqrt, scale=1.0 / D, bias=eps[:, :]).then_inc(s_prep_a, 1)
            act.wait_ge(s_mod, N_ADA1)
            act.copy(mod_col[:, 0:2 * ND], ps[6][:, 0:2 * ND]).then_inc(s_prep_a, 1)
            act.wait_ge(s_prep_v, 2)
            for t in range(ND):
                act.wait_ge(s_ut, t + 1)
                if t >= 2:
                    act.wait_ge(s_ulo, t - 1)
                ch.do(act.activation(u_tmp[:, t % 2, :], ps[t % 4][:, :], ACT.Identity, scale=a_col[:, 0, t:t + 1],
                               bias=mod_col[:, t:t + 1]))
                act.activation(u_hi[:, t, :], ps[t % 4][:, :], ACT.Identity, scale=a_col[:, 0, t:t + 1],
                               bias=mod_col[:, t:t + 1]).then_inc(s_uhi, 1)
            act.wait_ge(s_x, 16 * (NT + 1))
            act.copy(ba_hi[:, :, :], w_ba[:, :, :]).then_inc(s_ba_split, 1)
            act.wait_ge(s_prep_pe, 2)
            act.copy(ba[:, :, :].rearrange("p a b -> p (a b)"), ps[5][:, 0:NT * 16]).then_inc(s_prep_a, 1)

            def act_split(s, loaded, free):
                act.wait_ge(s_slot[s], loaded)
                act.wait_ge(s_used, free)
                act.copy(hi[s % 2][:, :], raw[s][:, :]).then_inc(s_hi, 1)

            act_split(0, N_ADA1 * 16 + 16, 3)
            done = ada_done = 0
            for col0, row0, n, natural, ada0 in PARTS:
                with act.Fori(0, n) as c:
                    for s in range(1, 5):
                        act_split(s % 4, (c + (N_ADA1 + done + s // 4)) * 16 + 16, (c + done) * 4 + (s + 3))
                    for b in range(2):
                        act.wait_ge(s_bank, (c + done) * 3 + (b + 1))
                        act.wait_ge(s_stored[b], (c + done) * 16)
                        act.copy(stage[:, b, :], ps[b][:, :]).then_inc(s_ev_a, 1)
                    if ada0 is not None:
                        act.wait_ge(s_mod, c + (N_ADA1 + ada_done + 1))
                        act.wait_ge(s_row_out, (c + ada_done) * 16)
                        act.copy(row_out[:, 0, :], ps[7][0:1, :]).then_inc(s_row, 1)
                done += n
                if ada0 is not None:
                    ada_done += n

            act.wait_ge(s_prep_v, 3)
            ch.link(act.activation(dec_in[:, 1, :, :], dec_in[:, 2, :, :], ACT.Exp))
            ch.link(act.activation(alog_row[:, :], alog_row[:, :], ACT.Exp))
            act.activation(dec_in[:, 2, :, :], dec_in[:, 1, :, :], ACT.Ln, bias=planes[:, C_ONES, 0:1]).then_inc(s_prep_a, 1)
            act.activation(beta[:, :, :], ba[:, :, 0:HEADS], ACT.Sigmoid).then_inc(s_prep_a, 1)
            act.wait_ge(s_prep_pe, 3)
            sums = ps[5][:, 0:2 * NT * HEADS].rearrange("p (a t h) -> p a t h", a=2, t=NT)
            ch.do(act.copy(gcum[:, :, :], sums[:, 0]))
            ch.do(act.activation(beta_g[:, :, :], sums[:, 0], ACT.Exp))
            act.activation(tail[:, :, :], sums[:, 1], ACT.Exp).then_inc(s_prep_a, 1)

            with act.Fori(0, HEADS) as h:
                for n, j in enumerate((1, 0, 2)):
                    act.wait_ge(s_conv, h * 3 + (n + 1))
                    act.activation(xin[:, j, PAD:PAD + SEQ], cv[:, j, :], ACT.Sigmoid).then_inc(s_sig, 1)
                for n, j in enumerate((1, 0)):
                    act.wait_ge(s_silu, h * 3 + (n + 1))
                    act.activation(sq[:, j, :], cv[:, j, :], ACT.Square).then_inc(s_sq, 1)
                for n, (j, bank) in enumerate(((1, TB), (0, SB_))):
                    act.wait_ge(s_ss, h * 2 + (n + 1))
                    act.activation(sq[:, j, :], bank[:, :], ACT.Sqrt, bias=eps[:, :]).then_inc(s_nroot, 1)
                act.wait_ge(s_gbc, h + 1)
                act.activation(e_g[:, :], XB[:, :], ACT.Exp).then_inc(s_eg, 1)
                act.wait_ge(s_darg, h + 1)
                act.activation(dec[:, :], dec[:, :], ACT.Exp).then_inc(s_dec, 1)
                act.wait_ge(s_inv1, h + 1)
                act.copy(inv[:, :], SB_[:, :]).then_inc(s_inv1_out, 1)
                for n in range(NL):
                    act.wait_ge(s_xm, h * NL + (n + 1))
                    if n == 0:
                        act.wait_ge(s_qkt, h + 1)
                    act.copy(x_sb[:, :], XB[:, :]).then_inc(s_xc, 1)
                act.wait_ge(s_uw, h + 1)
                act.copy(u_sol[:, :], TB[:, :]).then_inc(s_u, 1)
                act.wait_ge(s_dn_z, (h + 1) * 16)
                act.activation(z_sig[:, :, :], z_in[:, :, :], ACT.Sigmoid).then_inc(s_zsig, 1)
                act.wait_ge(s_sd, (h + 1) * NC)
                act.activation(n_t[:, :], TB[:, :], ACT.Square).then_inc(s_osq, 1)
                act.wait_ge(s_oms, h + 1)
                act.activation(o_ms[:, :], o_ms[:, :], ACT.Sqrt, scale=1.0 / HD, bias=eps[:, :]).then_inc(s_oroot, 1)
                act.wait_ge(s_ot, h + 1)
                act.copy(o_sb, XB[:, :]).then_inc(s_ot_out, 1)
            with act.Fori(0, HEADS) as h:
                for m in range(NT):
                    act.wait_ge(s_nmax, h * NT + (m + 1))
                    act.wait_ge(s_pt, h)
                    act.activation(prob[:, m, 0:(m + 1) * P], ps[m][:, 0:(m + 1) * P], ACT.Exp, scale=SCALE,
                                   bias=at_max[:, m:m + 1], accum_out=at_sum[:, m:m + 1]).then_inc(s_exp, 1)
                act.wait_ge(s_pt, h + 1)
                for k in range(NT):
                    act.copy(prob_t[:, k, k * P:SEQ], ps[4 + k][:, k * P:SEQ]).then_inc(s_pt_out, 1)
                act.wait_ge(s_av, h + 3)
                act.wait_ge(s_ya, h * 16)
                act.copy(at_o, ps[0][:, :]).then_inc(s_av_out, 1)

            def sigmoid_row(c, b):
                act.wait_ge(s_gate[b % 2], (c * 2 + b // 2) * 32 + 32)
                g = gate_in[:, (b % 2) * 2:(b % 2) * 2 + 2, :]
                act.activation(g, g, ACT.Sigmoid).then_inc(s_gsig, 1)

            act.wait_ge(s_yl, 32)
            for q in range(4):
                act.copy(yh[:, 4 * q:4 * q + 4, :], area_2[:, 4 * q:4 * q + 4, :]).then_inc(s_yh, 1)
            with act.Fori(0, 4) as c:
                for s in range(1, 5):
                    act_split(s % 4, (c + (N_ADA1 + N_IN + s // 4)) * 16 + 16, (c + N_IN) * 4 + (s + 3))
                    if s <= 2:
                        sigmoid_row(c, s - 1)
                for b in (2, 3):
                    sigmoid_row(c, b)
            act.wait_ge(s_used, 4 + 4 * (N_IN + 4))
            act.wait_ge(s_merged, 4 + 16)
            for q in range(4):
                act.copy(yh[:, 4 * q:4 * q + 4, :], merged[:, 4 * q:4 * q + 4, :]).then_inc(s_yh, 1)

            def project_out(c, last):
                for s in range(1, 4 if last else 5):
                    act_split(s % 4, (c + (N_ADA1 + N_IN + 4 + s // 4)) * 16 + 16, (c + (N_IN + 4)) * 4 + (s + 3))
                for b in range(2):
                    act.wait_ge(s_bank, (c + (N_IN + 4)) * 3 + (b + 1))
                    act.copy(y_nat[:, b, bass.ds(c * COLS, COLS)], ps[b][:, :]).then_inc(s_ev_a, 1)

            with act.Fori(0, 3) as c:
                project_out(c, False)
            project_out(3, True)
            act.wait_ge(s_ev_a, 2 + 2 * (N_IN + 4))
            act.wait_ge(s_ev_v, 2 + 2 * (N_IN + 4))
            junk = stage[:, :, :].rearrange("p a b -> p (a b)")
            for m in range(NT):
                ch.link(act.activation(junk, y_nat[:, m, :], ACT.Square, accum_out=ss2[:, 0, m:m + 1]))
            act.activation(ss2[:, 0, :], ss2[:, 0, :], ACT.Sqrt, scale=1.0 / D, bias=eps[:, :]).then_inc(s_rooty, 1)
            for m in range(NT):
                act.wait_ge(s_x1, m + 1)
                ch.link(act.activation(junk, y_nat[:, m, :], ACT.Square, accum_out=ss2[:, 1, m:m + 1]))
            act.activation(ss2[:, 1, :], ss2[:, 1, :], ACT.Sqrt, scale=1.0 / D, bias=eps[:, :]).then_inc(s_root1, 1)
            for t in range(ND):
                act.wait_ge(s_u2t, t + 1)
                act.copy(u2_t[:, t, :], ps[t % 4][:, :]).then_inc(s_u2t_out, 1)
            act.wait_ge(s_route_v, 1)
            act.activation(tmp4, tmp4, ACT.Exp).then_inc(s_route_a, 1)
            act.wait_ge(s_route_v, 2)
            act.activation(r1[:, 4, :], r1[:, 4, :], ACT.Exp).then_inc(s_route_a, 1)

            def expert_hi(j, x):
                act.wait_ge(s_mslot[x % 12], j * 16 + (mslot_base[x % 12] + 16 * (x // 12) + 16))
                act.wait_ge(s_mused, j * 12 + (x + 9))
                act.copy(m_hi[x % 4], m_raw[x % 12]).then_inc(s_mhi, 1)

            def rows_hi(n):
                for q in range(4):
                    act.wait_ge(s_xt, n + (q + 1))
                    act.copy(xe_hi[:, 4 * q:4 * q + 4, :].rearrange("p a b -> p (a b)"), ps[2 + q % 2][:, :]).then_inc(s_xehi, 1)

            act.wait_ge(s_ysplit, 8)
            for x in range(3):
                expert_hi(0, x)
            act.wait_ge(s_route_v, 6)
            n_blocks = act.value_load(plan[0:1, MAX_OVER:MAX_OVER + 1], min_val=EXPERTS, max_val=NB)
            rows_hi(0)
            with act.Fori(0, n_blocks) as j:
                for x in range(3, 8):
                    expert_hi(j, x)
                act.wait_ge(s_mused, j * 12 + 16)
                act.activation(h_sig, ps[0][:, :], ACT.Sigmoid).then_inc(s_hsig, 1)
                for x in range(8, 11):
                    expert_hi(j, x)
                rows_hi(j * 4 + 4)
                act.wait_ge(s_ht, j + 1)
                act.copy(ht_hi.rearrange("p a b -> p (a b)"), ps[0][:, :]).then_inc(s_hthi, 1)
                for x in range(11, 15):
                    expert_hi(j, x)
                act.wait_ge(s_ysc, j * 16)
                for b in range(2):
                    act.wait_ge(s_ybank, j * 3 + (b + 1))
                    act.copy(y_e[:, b * COLS:(b + 1) * COLS], ps[4 + b][:, :]).then_inc(s_ye_a, 1)
            for m in range(NT):
                act.wait_ge(s_f_y, m + 1)
                ch.link(act.activation(f_sq, f_y[m % 2][0], ACT.Square, accum_out=ss_f[:, m:m + 1]))
                act.activation(ss_f[:, m:m + 1], ss_f[:, m:m + 1], ACT.Sqrt, scale=1.0 / D, bias=eps[:, :]).then_inc(s_f_ss, 1)

        @block.vector
        def _(dve):
            ch = Chain(dve, s_dve)
            dve.sem_inc(s_ev_v, 2)
            dve.sem_inc(s_ada1_used, 4)
            dve.sem_inc(s_ada_used, 4)
            ch.do(dve.memset(half_pi[:, :], float(np.pi / 2)))
            ch.do(dve.memset(eps[:, :], EPS))
            dve.wait_ge(s_const, 16 * 8)
            ch.link(dve.tensor_copy(ang[:, 0, :], pos_i[:, :]))
            ch.link(dve.tensor_scalar(ang[:, 0, :], ang[:, 0, :], small[0:ROPE, 33:34], None, ALU.mult))
            ch.link(dve.tensor_scalar(ang[:, 1, :], ang[:, 0, :], float(1 / (2 * np.pi)), None, ALU.mult))
            ch.link(dve.tensor_scalar(ang[:, 1, :], ang[:, 1, :], ROUND, None, ALU.add))
            ch.link(dve.tensor_scalar(ang[:, 1, :], ang[:, 1, :], -ROUND, None, ALU.add))
            for part in (TWO_PI_1, TWO_PI_2, TWO_PI_3):
                ch.link(dve.scalar_tensor_tensor(ang[:, 0, :], ang[:, 1, :], -part, ang[:, 0, :], ALU.mult, ALU.add))
            ch.link(dve.tensor_scalar(ang[:, 2, :], ang[:, 0, :], -PI_BELOW, PI_BELOW, ALU.max, ALU.min))
            ch.link(dve.tensor_scalar(ang[:, 1, :], ang[:, 2, :], -1.0, None, ALU.mult))
            dve.tensor_tensor(ang[:, 3, :], ang[:, 1, :], ang[:, 2, :], ALU.max).then_inc(s_prep_v, 1)
            dve.wait_ge(s_prep_a, 1)
            ch.link(dve.tensor_tensor(cond[:, :], cond_raw[:, :], cond_sig[:, :], ALU.mult))

            def accumulate(ring, s, par, slot_done, used):
                for t in range(4):
                    w = ring[s][:, t * COLS:(t + 1) * COLS]
                    k = 4 * s + t
                    if k == 0:
                        ins = dve.tensor_scalar(acc[:, par, :], w, cond[:, 0:1], None, ALU.mult)
                    else:
                        ins = dve.scalar_tensor_tensor(acc[:, par, :], w, cond[:, k:k + 1], acc[:, par, :], ALU.mult, ALU.add)
                    if t < 3:
                        ch.link(ins)
                    else:
                        ins.then_inc(used, 1)
                        dve.wait_ge(used, slot_done)

            with ch.loop(N_ADA1 // 2, 24) as i:
                for par in range(2):
                    for s in range(4):
                        dve.wait_ge(s_slot[s], (i * 2 + par) * 16 + 16)
                        accumulate([r[:, :] for r in raw], s, par, (i * 2 + par) * 4 + (s + 5), s_ada1_used)
                    dve.sem_inc(s_acc, 1)
                    dve.wait_ge(s_mod, i * 2 + par)
            dve.wait_ge(s_prep_a, 5)
            ch.link(dve.tensor_tensor(mod_col[:, 0:2 * ND], mod_col[:, 0:2 * ND], b_col[:, 0:2 * ND], ALU.add))
            dve.scalar_tensor_tensor(a_col[:, 0, :], mod_col[:, ND:2 * ND], 1.0, g_pre[:, 0, :], ALU.add, ALU.mult).then_inc(s_prep_v, 1)
            dve.wait_ge(s_prep_a, 4)
            ch.link(dve.reciprocal(rstd[:, :], rstd[:, :]))
            for m in range(NT):
                dve.tensor_scalar(x_all[:, m, :], x_all[:, m, :], rstd[:, m:m + 1], None, ALU.mult).then_inc(s_xn, 1)
            for t in range(ND):
                dve.wait_ge(s_uhi, t + 1)
                dve.tensor_tensor(u_lo[:, t, :], u_tmp[:, t % 2, :], u_hi[:, t, :].bitcast(F32), ALU.subtract).then_inc(s_ulo, 1)
            dve.wait_ge(s_ba_split, 1)
            dve.tensor_tensor(ba_lo[:, :, :], w_ba[:, :, :], ba_hi[:, :, :].bitcast(F32), ALU.subtract).then_inc(s_ba_split, 1)
            dve.wait_ge(s_ulo, ND)

            def dve_split(s, ready):
                dve.wait_ge(s_hi, ready)
                dve.tensor_tensor(raw_r[s][:, :], raw[s][:, :], hi[s % 2][:, :].bitcast(F32),
                                  ALU.subtract).then_inc(s_lo, 1)

            dve_split(0, 1)
            done = ada_done = 0
            for col0, row0, n, natural, ada0 in PARTS:
                with ch.loop(n, 12 if ada0 is not None else 0) as c:
                    for s in range(4):
                        dve_split((s + 1) % 4, (c + done) * 4 + (s + 2))
                        if ada0 is not None:
                            if s == 0:
                                dve.wait_ge(s_mod, c + (N_ADA1 + ada_done))
                            dve.wait_ge(s_ada_slot[s], (c + ada_done) * 16 + 16)
                            accumulate(ada_ring, s, 0, (c + ada_done) * 4 + (s + 5), s_ada_used)
                    if ada0 is not None:
                        dve.sem_inc(s_acc, 1)
                    for b in range(2, 4):
                        if b == 2:
                            dve.wait_ge(s_bank, (c + done) * 3 + 3)
                        else:
                            dve.wait_ge(s_used, (c + done) * 4 + 8)
                        dve.wait_ge(s_stored[b], (c + done) * 16)
                        dve.tensor_copy(stage[:, b, :], ps[b][:, :]).then_inc(s_ev_v, 1)
                done += n
                if ada0 is not None:
                    ada_done += n

            dve.wait_ge(s_rows, 16 * 3)
            dve.wait_ge(s_prep_a, 6)
            ch.link(dve.tensor_tensor(dec_in[:, 0, :, :], ba[:, :, HEADS:2 * HEADS],
                                      dtb_row[:, :].rearrange("p (a h) -> p a h", a=1).broadcast_to([P, NT, HEADS]), ALU.add))
            ch.link(dve.tensor_scalar(dec_in[:, 1, :, :], dec_in[:, 0, :, :], -1.0, None, ALU.mult))
            dve.tensor_tensor(dec_in[:, 2, :, :], dec_in[:, 0, :, :], dec_in[:, 1, :, :], ALU.min).then_inc(s_prep_v, 1)
            dve.wait_ge(s_prep_a, 8)
            ch.link(dve.scalar_tensor_tensor(dec_in[:, 3, :, :], dec_in[:, 0, :, :], 0.0, dec_in[:, 2, :, :], ALU.max, ALU.add))
            ch.link(dve.tensor_scalar(dec_in[:, 3, :, :], dec_in[:, 3, :, :], -1.0, None, ALU.mult))
            dve.tensor_tensor(g_nat[:, :, :], dec_in[:, 3, :, :],
                              alog_row[:, :].rearrange("p (a h) -> p a h", a=1).broadcast_to([P, NT, HEADS]), ALU.mult).then_inc(s_prep_v, 1)
            dve.wait_ge(s_prep_a, 9)
            ch.link(dve.tensor_tensor(beta_g[:, :, :], beta_g[:, :, :], beta[:, :, :], ALU.mult))

            with ch.loop(HEADS, 22) as h:
                dve.wait_ge(s_dn_in, (h + 1) * 16)
                for j in (1, 0, 2):
                    for k in range(CONV):
                        w = conv_col[:, bass.ds(h + (k * 3 * HEADS + j * HEADS), 1)]
                        src = xin[:, j, k:k + SEQ]
                        if k == 0:
                            ch.link(dve.tensor_scalar(cv[:, j, :], src, w, None, ALU.mult))
                        else:
                            ins = dve.scalar_tensor_tensor(cv[:, j, :], src, w, cv[:, j, :], ALU.mult, ALU.add)
                            if k < CONV - 1:
                                ch.link(ins)
                            else:
                                ins.then_inc(s_conv, 1)
                for n, j in enumerate((1, 0, 2)):
                    dve.wait_ge(s_sig, h * 3 + (n + 1))
                    dve.tensor_tensor(cv[:, j, :], cv[:, j, :], xin[:, j, PAD:PAD + SEQ], ALU.mult).then_inc(s_silu, 1)
                ch.do(dve.tensor_copy(tiles(inv[:, :]), column(g_nat, h)))
                dve.tensor_copy(tiles(inv_t[:, :]), column(beta, h)).then_inc(s_gb, 1)
                for n, j in enumerate((1, 0)):
                    dve.wait_ge(s_nroot, h * 2 + (n + 1))
                    ch.link(dve.reciprocal(sq[:, j, :], sq[:, j, :]))
                    dve.scalar_tensor_tensor(cv[:, j, :], cv[:, j, :], 1.0 if j else HD ** -0.5, sq[:, j, :],
                                             ALU.mult, ALU.mult).then_inc(s_unit, 1)
                dve.wait_ge(s_bbc, h + 1)
                dve.wait_ge(s_unit, h * 2 + 1)
                dve.tensor_tensor(kb[:, :], cv[:, 1, :], TB[:, :], ALU.mult).then_inc(s_kb, 1)
                dve.wait_ge(s_eg, h + 1)
                for t in range(NT):
                    c = slice(t * P, (t + 1) * P)
                    ins = dve.scalar_tensor_tensor(dec[:, c], XB[:, c], gcum[:, t, bass.ds(h, 1)], planes[:, C_DEC, :],
                                                   ALU.subtract, ALU.add)
                    ins.then_inc(s_darg, 1) if t == NT - 1 else ch.do(ins)
                dve.wait_ge(s_unit, h * 2 + 2)
                ch.do(dve.tensor_tensor(q_dec[:, :], cv[:, 0, :], e_g[:, :], ALU.mult))
                ch.do(dve.tensor_copy(g_last[:, :], e_g[:, CHUNK - 1::CHUNK]))
                dve.wait_ge(s_dec, h + 1)
                dve.wait_ge(s_gram, h * 2 + 1)
                dve.tensor_tensor(n_t[:, :], SB_[:, :], dec[:, :], ALU.mult).then_inc(s_nt, 1)
                dve.wait_ge(s_gram, h * 2 + 2)
                dve.tensor_tensor(qk_t[:, :], TB[:, :], dec[:, :], ALU.mult).then_inc(s_qkt, 1)
                dve.wait_ge(s_nt, h + 1)
                dve.wait_ge(s_gbc, h + 1)
                dve.wait_ge(s_bbc, h + 1)
                ch.link(dve.tensor_tensor(tiles(inv_t[:, :]), tiles(n_t[:, :]), plane(C_LEV), ALU.mult))
                dve.tensor_tensor(tiles(inv_t[:, :]), plane(C_ID), tiles(inv_t[:, :]), ALU.subtract).then_inc(s_first, 1)
                dve.wait_ge(s_knat, h + 1)
                dve.tensor_tensor(k_bg[:, :, :], tiles(XB[:, :]), column(beta_g, h), ALU.mult).then_inc(s_kfac, 1)
                dve.tensor_tensor(k_tail[:, :, :], tiles(XB[:, :]), column(tail, h), ALU.mult).then_inc(s_kfac, 1)
                dve.wait_ge(s_vnat, h + 1)
                dve.tensor_tensor(v_b[:, :, :], tiles(TB[:, :]), column(beta, h), ALU.mult).then_inc(s_vb, 1)
                for n in range(NL):
                    dve.wait_ge(s_corr, h * NL + (n + 1))
                    if n < NL - 1:
                        dve.tensor_tensor(inv_t[:, :], inv_t[:, :], TB[:, :], ALU.subtract).then_inc(s_inv, 1)
                        dve.tensor_tensor(inv[:, :], inv[:, :], SB_[:, :], ALU.subtract).then_inc(s_inv, 1)
                        dve.wait_ge(s_inv, h * (2 * NL - 1) + (2 * n + 2))
                    else:
                        dve.tensor_tensor(inv_t[:, :], inv_t[:, :], TB[:, :], ALU.subtract).then_inc(s_inv, 1)
                dve.wait_ge(s_uw, h + 1)
                dve.tensor_copy(w_t[:, :], SB_[:, :]).then_inc(s_w, 1)
                for c in range(NC):
                    r, t = slice((c % 2) * CHUNK, (c % 2 + 1) * CHUNK), c // 2
                    if c:
                        dve.wait_ge(s_ws, h * (NC - 1) + c)
                        if c == 1:
                            dve.wait_ge(s_u, h + 1)
                        dve.tensor_tensor(v_new[r, :], u_sol[r, t * HD:(t + 1) * HD], XB[r, 0:HD], ALU.subtract).then_inc(s_vn, 1)
                    dve.wait_ge(s_sd, h * NC + (c + 1))
                    if c == 0:
                        dve.tensor_copy(state[:, :], SB_[:, 0:HD]).then_inc(s_state, 1)
                    else:
                        dve.wait_ge(s_state, h * NC + c)
                        dve.scalar_tensor_tensor(state[:, :], state[:, :], g_last[:, c:c + 1], SB_[:, 0:HD],
                                                 ALU.mult, ALU.add).then_inc(s_state, 1)
                dve.wait_ge(s_osq, h + 1)
                dve.tensor_reduce(o_ms[:, :], tiles(n_t[:, :]), AX, ALU.add).then_inc(s_oms, 1)
                dve.wait_ge(s_zsig, h + 1)
                ch.link(dve.tensor_tensor(z_sig[:, :, :], z_sig[:, :, :], z_in[:, :, :], ALU.mult))
                ch.link(dve.tensor_tensor(z_sig[:, :, :], z_sig[:, :, :],
                                          og_row[:, :].rearrange("p (a c) -> p a c", a=1).broadcast_to([P, NT, HD]), ALU.mult))
                dve.wait_ge(s_oroot, h + 1)
                ch.link(dve.reciprocal(o_ms[:, :], o_ms[:, :]))
                dve.wait_ge(s_yb, h * 16)
                ch.link(dve.tensor_tensor(tiles(o_sb), tiles(TB[:, :]), o_ms[:, :].rearrange("p (t a) -> p t a", a=1).broadcast_to([P, NT, HD]), ALU.mult))
                dve.tensor_tensor(tiles(o_sb), tiles(o_sb), z_sig[:, :, :], ALU.mult).then_inc(s_on, 1)

            with ch.loop(HEADS // 2, 2 * 16) as i:
                for par in range(2):
                    h = i * 2 + par
                    for n, x in enumerate((at_q[par], at_k[par])):
                        dve.wait_ge(s_rot, h * 2 + (n + 1))
                        ch.link(dve.tensor_tensor(rot[0:ROPE, :], ps[4 + n][0:ROPE, :], sin_t[:, :], ALU.mult))
                        if n == 0:
                            dve.wait_ge(s_rot, h * 2 + 2)
                        ch.link(dve.tensor_tensor(x[0:ROPE, :], x[0:ROPE, :], cos_t[:, :], ALU.mult))
                        dve.tensor_tensor(x[0:ROPE, :], x[0:ROPE, :], rot[0:ROPE, :], ALU.add).then_inc(s_roped, 1)
                        dve.wait_ge(s_roped, h * 2 + (n + 1))
                    for m in range(NT):
                        dve.wait_ge(s_sc, h * NT + (m + 1))
                        diag = ps[m][:, m * P:(m + 1) * P]
                        ch.link(dve.tensor_tensor(diag, diag, planes[:, C_CAUSAL, :], ALU.add))
                        ch.link(dve.reduce_max(at_raw[:, m:m + 1], ps[m][:, 0:(m + 1) * P], AX))
                        dve.tensor_scalar(at_max[:, m:m + 1], at_raw[:, m:m + 1], -SCALE, None, ALU.mult).then_inc(s_nmax, 1)
                    for m in range(NT):
                        dve.wait_ge(s_exp, h * NT + (m + 1))
                        ch.link(dve.reciprocal(at_sum[:, m:m + 1], at_sum[:, m:m + 1]))
                        dve.tensor_scalar(prob[:, m, 0:(m + 1) * P], prob[:, m, 0:(m + 1) * P], at_sum[:, m:m + 1], None,
                                          ALU.mult).then_inc(s_prob, 1)

            for q in range(4):
                dve.wait_ge(s_yh, q + 1)
                dve.tensor_tensor(yl[:, 4 * q:4 * q + 4, :], area_2[:, 4 * q:4 * q + 4, :],
                                  yh[:, 4 * q:4 * q + 4, :].bitcast(F32), ALU.subtract).then_inc(s_ysplit, 1)
            dve.sem_inc(s_merged, 4)
            with ch.loop(4, 8) as c:
                for s in range(4):
                    dve_split((s + 1) % 4, (c + N_IN) * 4 + (s + 2))
                for b in range(4):
                    g = gate_in[:, (b % 2) * 2, :], gate_in[:, (b % 2) * 2 + 1, :]
                    dve.wait_ge(s_gsig, c * 4 + (b + 1))
                    if b < 3:
                        dve.wait_ge(s_bank, (c + N_IN) * 3 + (b + 1))
                    else:
                        dve.wait_ge(s_used, (c + N_IN) * 4 + 8)
                    ch.do(dve.tensor_tensor(g[0], g[0], ps[b][:, :], ALU.mult))
                    ch.link(dve.tensor_tensor(g[1], g[1], ps[4 + b][:, :], ALU.mult))
                    dve.tensor_tensor(merged[:, bass.ds(c * 4 + b, 1), :].rearrange("p a n -> p (a n)"), g[0], g[1],
                                      ALU.add).then_inc(s_merged, 1)
            for q in range(4):
                dve.wait_ge(s_yh, q + 5)
                dve.tensor_tensor(yl[:, 4 * q:4 * q + 4, :], merged[:, 4 * q:4 * q + 4, :],
                                  yh[:, 4 * q:4 * q + 4, :].bitcast(F32), ALU.subtract).then_inc(s_ysplit, 1)

            def project_out(c, last):
                for s in range(3 if last else 4):
                    dve_split((s + 1) % 4, (c + (N_IN + 4)) * 4 + (s + 2))
                for b in range(2, 4):
                    if b == 2:
                        dve.wait_ge(s_bank, (c + (N_IN + 4)) * 3 + 3)
                    else:
                        dve.wait_ge(s_used, (c + (N_IN + 4)) * 4 + 8)
                    dve.tensor_copy(y_nat[:, b, bass.ds(c * COLS, COLS)], ps[b][:, :]).then_inc(s_ev_v, 1)

            with dve.Fori(0, 3) as c:
                project_out(c, False)
            project_out(3, True)

            dve.wait_ge(s_mr, 16 * 5)
            ch.link(dve.tensor_tensor(mr[:, :, :], mr[:, :, :], br[:, :, :], ALU.add))
            ch.do(dve.tensor_tensor(mr[:, 0, :], mr[:, 0, :], gr[:, 0, :], ALU.mult))
            ch.do(dve.scalar_tensor_tensor(mr[:, 2, :], mr[:, 2, :], 1.0, gr[:, 1, :], ALU.add, ALU.mult))
            dve.tensor_tensor(mr[:, 3, :], mr[:, 3, :], gr[:, 2, :], ALU.mult).then_inc(s_res, 1)

            dve.wait_ge(s_rooty, 1)
            ch.link(dve.reciprocal(ss2[:, 0, :], ss2[:, 0, :]))
            dve.wait_ge(s_rowb, 16 * 7)
            for m in range(NT):
                ch.link(dve.scalar_tensor_tensor(y_nat[:, m, :], y_nat[:, m, :], ss2[:, 0, m:m + 1], row_g1, ALU.mult, ALU.mult))
                dve.wait_ge(s_xin2, (m + 1) * 16)
                dve.tensor_tensor(y_nat[:, m, :], y_nat[:, m, :], x_in, ALU.add).then_inc(s_x1, 1)
            dve.wait_ge(s_root1, 1)
            ch.link(dve.reciprocal(ss2[:, 1, :], ss2[:, 1, :]))
            for m in range(NT):
                dve.wait_ge(s_x1_out, 16 * NT)
                ch.link(dve.scalar_tensor_tensor(y_nat[:, m, :], y_nat[:, m, :], ss2[:, 1, m:m + 1], row_a2, ALU.mult, ALU.mult))
                dve.tensor_tensor(y_nat[:, m, :], y_nat[:, m, :], row_s2, ALU.add).then_inc(s_u2, 1)

            def over_tiles(x, n):
                return x.rearrange("p (t a) -> p t a", a=1).broadcast_to([P, NT, n])

            def numbers(n):
                return small[:, 0:n].rearrange("p (a e) -> p a e", a=1).broadcast_to([P, NT, n])

            def first_of_max(x, best, one_hot, scratch, index, n):
                ch.link(dve.tensor_reduce(best, x, AX, ALU.max))
                ch.link(dve.tensor_tensor(scratch, x, over_tiles(best, n), ALU.is_equal))
                ch.link(dve.tensor_scalar(scratch, scratch, -1000.0, 1000.0, ALU.mult, ALU.add))
                ch.link(dve.tensor_tensor(scratch, scratch, numbers(n), ALU.add))
                ch.link(dve.tensor_reduce(index, scratch, AX, ALU.min))
                ch.link(dve.tensor_tensor(one_hot, numbers(n), over_tiles(index, n), ALU.is_equal))

            def look_up(dst, values, one_hot, n):
                ch.link(dve.tensor_tensor(tmp32, values, one_hot, ALU.mult))
                ch.link(dve.tensor_reduce(dst, tmp32, AX, ALU.add))

            dve.wait_ge(s_logit, 1)
            ch.link(dve.tensor_tensor(logit, ps[4][:, 0:NT * NR].rearrange("p (t n) -> p t n", t=NT),
                                      b_r[:, :].rearrange("p (a n) -> p a n", a=1).broadcast_to([P, NT, NR]), ALU.add))
            g_log = logit[:, :, 0:GROUPS]
            first_of_max(g_log, r1[:, 0, :], oh_g, tmp4, r1[:, 1, :], GROUPS)
            dve.tensor_tensor(tmp4, g_log, over_tiles(r1[:, 0, :], GROUPS), ALU.subtract).then_inc(s_route_v, 1)
            ch.link(dve.tensor_scalar(oh_g, oh_g, -NEG, NEG, ALU.mult, ALU.add))
            for g in range(GROUPS):
                ch.do(dve.tensor_tensor(e_log[:, :, g * PER_GROUP:(g + 1) * PER_GROUP],
                                        logit[:, :, GROUPS + g * PER_GROUP:GROUPS + (g + 1) * PER_GROUP],
                                        oh_g[:, :, g:g + 1].broadcast_to([P, NT, PER_GROUP]), ALU.add))
            ch.sync()
            first_of_max(e_log, r1[:, 2, :], oh1, tmp32, r1[:, 5, :], EXPERTS)
            ch.link(dve.tensor_scalar(tmp32, oh1, 2 * NEG, None, ALU.mult))
            ch.link(dve.tensor_tensor(e_log, e_log, tmp32, ALU.add))
            first_of_max(e_log, r1[:, 3, :], oh2, tmp32, r1[:, 6, :], EXPERTS)
            dve.tensor_tensor(r1[:, 4, :], r1[:, 3, :], r1[:, 2, :], ALU.subtract).then_inc(s_route_v, 1)
            dve.tensor_tensor(both, oh1, oh2, ALU.add).then_inc(s_route_v, 1)
            dve.wait_ge(s_route_a, 1)
            ch.link(dve.tensor_reduce(r1[:, 7, :], tmp4, AX, ALU.add))
            dve.wait_ge(s_route_a, 2)
            ch.link(dve.tensor_scalar(r1[:, 8, :], r1[:, 4, :], 1.0, None, ALU.add))
            ch.link(dve.tensor_tensor(r1[:, 8, :], r1[:, 8, :], r1[:, 7, :], ALU.mult))
            ch.link(dve.reciprocal(wts[:, 0, :], r1[:, 8, :]))
            ch.link(dve.tensor_tensor(wts[:, 1, :], wts[:, 0, :], r1[:, 4, :], ALU.mult))
            dve.wait_ge(s_route_pe, 1)
            ch.do(dve.tensor_copy(rank, ps[5][:, 0:NT * EXPERTS].rearrange("p (t e) -> p t e", t=NT)))
            ch.link(dve.tensor_copy(cnt[:, 0, :], ps[6][:, 0:EXPERTS]))
            ch.link(dve.tensor_scalar(cnt[:, 1, :], cnt[:, 0, :], float(ROWS), None, ALU.is_gt))
            for q in (2, 3):
                ch.link(dve.tensor_scalar(cnt[:, 2, :], cnt[:, 0, :], float(q * ROWS), None, ALU.is_gt))
                ins = dve.tensor_tensor(cnt[:, 1, :], cnt[:, 1, :], cnt[:, 2, :], ALU.add)
                ch.link(ins) if q == 2 else ins.then_inc(s_route_v, 1)
            dve.wait_ge(s_route_pe, 2)
            dve.tensor_copy(over_t[0:EXPERTS, :], ps[7][0:EXPERTS, 0:P]).then_inc(s_route_v, 1)
            dve.wait_ge(s_route_pe, 3)
            ch.link(dve.tensor_scalar(cnt[:, 2, :], ps[5][:, 256:256 + EXPERTS], float(EXPERTS), None, ALU.add))
            ch.link(dve.tensor_tensor(cnt[:, 3, :], cnt[:, 2, :], cnt[:, 1, :], ALU.add))
            ch.link(dve.tensor_tensor(tmp7, cnt[:, 3:4, :].broadcast_to([P, MAX_OVER, EXPERTS]),
                                      small[:, 40:40 + MAX_OVER].rearrange("p (n a) -> p n a", a=1).broadcast_to([P, MAX_OVER, EXPERTS]),
                                      ALU.is_le))
            ch.link(dve.tensor_reduce(plan_f[:, 0:MAX_OVER], tmp7, AX, ALU.add))
            ch.link(dve.tensor_scalar(plan_f[:, 0:MAX_OVER], plan_f[:, 0:MAX_OVER], float(EXPERTS - 1), None, ALU.min))
            ch.link(dve.tensor_copy(plan_f[:, MAX_OVER:MAX_OVER + 1], cnt[:, 3, EXPERTS - 1:EXPERTS]))
            ch.do(dve.tensor_copy(plan[:, :], plan_f[:, :]))
            ch.sync()
            dve.sem_inc(s_route_v, 1)
            base = cnt[:, 2:3, :].broadcast_to([P, NT, EXPERTS])
            for k, one_hot in enumerate((oh1, oh2)):
                look_up(r1[:, 9, :], rank, one_hot, EXPERTS)
                look_up(r1[:, 10, :], base, one_hot, EXPERTS)
                ch.link(dve.tensor_scalar(r1[:, 11, :], r1[:, 9, :], float(ROWS), None, ALU.is_ge))
                ch.link(dve.tensor_copy(r1[:, 12, :], r1[:, 11, :]))
                for q in (2, 3):
                    ch.link(dve.tensor_scalar(r1[:, 13, :], r1[:, 9, :], float(q * ROWS), None, ALU.is_ge))
                    ch.link(dve.tensor_tensor(r1[:, 12, :], r1[:, 12, :], r1[:, 13, :], ALU.add))
                ch.link(dve.tensor_tensor(r1[:, 10, :], r1[:, 10, :], r1[:, 12, :], ALU.add))
                ch.link(dve.scalar_tensor_tensor(r1[:, 10, :], r1[:, 10, :], -1.0, r1[:, 5 + k, :], ALU.add, ALU.subtract))
                ch.link(dve.tensor_tensor(r1[:, 10, :], r1[:, 10, :], r1[:, 11, :], ALU.mult))
                ch.link(dve.tensor_tensor(r1[:, 10, :], r1[:, 10, :], r1[:, 5 + k, :], ALU.add))
                ch.link(dve.scalar_tensor_tensor(r1[:, 9, :], r1[:, 12, :], -float(ROWS), r1[:, 9, :], ALU.mult, ALU.add))
                ch.link(dve.scalar_tensor_tensor(place[:, k, :], r1[:, 9, :], float(NB + 1), r1[:, 10, :], ALU.mult, ALU.add))
                for m in range(NT):
                    ch.do(dve.tensor_scalar(r1[:, 14 + k, m:m + 1], small[:, 32:33], float(m * P + k * SEQ), None, ALU.add))
                ch.sync()
            dve.tensor_copy(place_i[:, :], place.rearrange("p k t -> p (k t)")).then_inc(s_route_v, 1)
            dve.tensor_copy(id_i[:, :], r1[:, 14:16, :].rearrange("p k t -> p (k t)")).then_inc(s_route_v, 1)
            dve.wait_ge(s_table, 32 + 16 * 2 * NT)
            ch.link(dve.tensor_copy(row_f[:, :], row_i[:, :]))
            ch.link(dve.tensor_scalar(tok_f[:, :], row_f[:, :], float(SEQ), -float(SEQ), ALU.is_ge, ALU.mult))
            ch.link(dve.tensor_tensor(tok_f[:, :], tok_f[:, :], row_f[:, :], ALU.add))
            dve.tensor_copy(tok_i[:, :], tok_f[:, :]).then_inc(s_route_v, 1)

            def expert_lo(j, x):
                dve.wait_ge(s_mhi, j * 12 + (x + 1))
                dve.tensor_tensor(m_raw_r[x % 12], m_raw[x % 12], m_hi[x % 4].bitcast(F32),
                                  ALU.subtract).then_inc(s_mlo, 1)

            def rows_lo(n):
                for q in range(4):
                    dve.wait_ge(s_xehi, n + (q + 1))
                    dve.tensor_tensor(xe_lo[:, 4 * q:4 * q + 4, :].rearrange("p a b -> p (a b)"), ps[2 + q % 2][:, :],
                                      xe_hi[:, 4 * q:4 * q + 4, :].bitcast(F32).rearrange("p a b -> p (a b)"),
                                      ALU.subtract).then_inc(s_xelo, 1)

            for x in range(3):
                expert_lo(0, x)
            n_blocks = dve.value_load(plan[0:1, MAX_OVER:MAX_OVER + 1], min_val=EXPERTS, max_val=NB)
            rows_lo(0)
            with ch.loop(n_blocks, 1) as j:
                for x in range(3, 11):
                    expert_lo(j, x)
                dve.wait_ge(s_hsig, j + 1)
                ch.link(dve.tensor_tensor(h_e, h_sig, ps[0][:, :], ALU.mult))
                dve.wait_ge(s_mused, j * 12 + 20)
                dve.tensor_tensor(h_e, h_e, ps[1][:, :], ALU.mult).then_inc(s_h, 1)
                rows_lo(j * 4 + 4)
                dve.wait_ge(s_hthi, j + 1)
                dve.tensor_tensor(ht_lo.rearrange("p a b -> p (a b)"), ps[0][:, :],
                                  ht_hi.bitcast(F32).rearrange("p a b -> p (a b)"), ALU.subtract).then_inc(s_htlo, 1)
                for x in range(11, 15):
                    expert_lo(j, x)
                dve.wait_ge(s_ysc, j * 16)
                for b in range(2, 4):
                    if b == 2:
                        dve.wait_ge(s_ybank, j * 3 + 3)
                    else:
                        dve.wait_ge(s_mused, j * 12 + 24)
                    dve.tensor_copy(y_e[:, b * COLS:(b + 1) * COLS], ps[4 + b][:, :]).then_inc(s_ye_v, 1)

            dve.wait_ge(s_g2, 16)
            for m in range(NT):
                dve.wait_ge(s_at_in[m % 2], HEADS // 2 * 48 + (m // 2 + 1) * 48)
                y0, y1, x1 = f_y[m % 2][0], f_y[m % 2][1], f_x[m % 2]
                ch.link(dve.tensor_scalar(y0, y0, wts[:, 0, m:m + 1], None, ALU.mult))
                dve.scalar_tensor_tensor(y0, y1, wts[:, 1, m:m + 1], y0, ALU.mult, ALU.add).then_inc(s_f_y, 1)
                dve.wait_ge(s_f_ss, m + 1)
                ch.link(dve.reciprocal(ss_f[:, m:m + 1], ss_f[:, m:m + 1]))
                ch.link(dve.scalar_tensor_tensor(y0, y0, ss_f[:, m:m + 1], row_g2, ALU.mult, ALU.mult))
                dve.tensor_tensor(x1, x1, y0, ALU.add).then_inc(s_f_out, 1)


def kernel(**inputs):
    import numpy as _np
    import concourse.bacc as _bacc
    from concourse import mybir as _mybir
    from concourse.bass_utils import run_bass_kernel_spmd as _run

    nc = _bacc.Bacc("TRN2", target_bir_lowering=False, num_devices=1)
    planes, small = shape_constants()
    arrays, aps = {}, {}
    for name, x in {**inputs, "planes": planes, "small": small}.items():
        x = _np.ascontiguousarray(x)
        arrays[f"in_{name}_dram"] = x
        aps[name] = nc.dram_tensor(f"in_{name}_dram", x.shape, _mybir.dt.from_np(x.dtype), kind="ExternalInput").ap()
    out = nc.dram_tensor("out_dram", (1, SEQ, D), F32, kind="ExternalOutput").ap()

    def dram(name, shape, dt=F32):
        return nc.dram_tensor(f"{name}_dram", shape, dt).ap()

    build(nc, aps, out, dram)
    r = _run(nc, [arrays], core_ids=[0])
    return r.results[0]["out_dram"]
```

```python
from contextlib import ExitStack, contextmanager

import numpy as np

import concourse.bass as bass
from concourse import mybir

F32 = mybir.dt.float32
F32R = mybir.dt.float32r
I32 = mybir.dt.int32
ALU = mybir.AluOpType
ACT = mybir.ActivationFunctionType
AX = mybir.AxisListType.X

P = 128
SEQ = 512
D = 2048
ND = D // P
NT = SEQ // P
HD = 128
HEADS = 8
WIDTH = HEADS * HD
ROPE = HD // 4
HALF = ROPE // 2
ROPE_THETA = 500000.0
CHUNK = 64
CONV = 4
GROUPS, PER_GROUP = 4, 8
EXPERTS = GROUPS * PER_GROUP
FF = 512
NF = FF // P
ROWS = 128
MAX_OVER = (SEQ * 2) // (ROWS + 1)
COLS = 512
SLOT = 4 * COLS
EPS = 1e-6
NEG = -1.0e30
IN_QA, IN_KA, IN_VA, IN_DN, IN_Z = 0, WIDTH, 2 * WIDTH, 3 * WIDTH, 6 * WIDTH
IN_BETA = 7 * WIDTH
IN_GA = IN_BETA + 2 * HEADS
IN_GB = IN_GA + D
LEVELS = (1, 2, 4, 8, 16, 32)

TWO_PI_1 = 6.28125
TWO_PI_2 = float(np.float32(np.round((2 * np.pi - 6.28125) * 2.0 ** 20) / 2.0 ** 20))
TWO_PI_3 = float(np.float32(2 * np.pi - 6.28125 - TWO_PI_2))
ROUND = 1.5 * 2.0 ** 23
PI_BELOW = 3.1415925

(C_ID, C_ONES, C_CUM, C_TAIL, C_DEC, C_CAUSAL, C_RANK, C_ROT, C_LEV) = (0, 1, 2, 3, 4, 5, 6, 7, 8)
N_CONST = C_LEV + len(LEVELS)


def shape_constants():
    c = np.zeros((N_CONST, P, P), np.float32)
    k, i = np.meshgrid(np.arange(P), np.arange(P), indexing="ij")
    same = (k // CHUNK) == (i // CHUNK)
    c[C_ID] = np.eye(P)
    c[C_ONES] = 1.0
    c[C_CUM] = same & (k <= i)
    c[C_TAIL] = same & (k > i)
    c[C_DEC] = np.where(same & (i >= k), 0.0, NEG)
    c[C_CAUSAL] = np.where(i <= k, 0.0, NEG)
    c[C_RANK] = k < i
    for a in range(HALF):
        c[C_ROT, a + HALF, a] = -1.0
        c[C_ROT, a, a + HALF] = 1.0
    for n, s in enumerate(LEVELS):
        c[C_LEV + n] = (k // (2 * s) == i // (2 * s)) & (k % (2 * s) < s) & (i % (2 * s) >= s)
    planes = np.ascontiguousarray(c.transpose(1, 0, 2))
    small = np.zeros((P, 64), np.float32)
    small[:, 0:32] = np.arange(32)
    small[:, 32] = np.arange(P)
    f = np.power(np.float64(ROPE_THETA), -np.arange(HALF) * (2.0 / ROPE)).astype(np.float32)
    small[0:ROPE, 33] = np.concatenate([f, f])
    small[:, 40:40 + MAX_OVER] = EXPERTS + np.arange(MAX_OVER)
    return planes, small


class Chain:

    def __init__(self, eng, sem):
        self.eng, self.sem, self.base, self.off = eng, sem, 0, 0

    def do(self, ins):
        ins.then_inc(self.sem, 1)
        self.off += 1
        return ins

    def sync(self, but=0):
        self.eng.wait_ge(self.sem, self.base + (self.off - but))

    def link(self, ins):
        self.do(ins)
        self.sync()

    @contextmanager
    def loop(self, n, per):
        base, off = self.base, self.off
        with self.eng.Fori(0, n) as i:
            self.base, self.off = i * per + (base + off), 0
            yield i
            assert self.off == per, f"this loop signals {self.off} times a turn"
        self.base, self.off = base, off + n * per


class Carve:

    def __init__(self, *areas):
        self.areas = [[x, 0] for x in areas]

    def take(self, shape):
        n = int(np.prod(shape[1:]))
        for area in self.areas:
            x, at = area
            if at + n <= x.shape[1]:
                area[1] += n
                part = x[:, at:at + n]
                if len(shape) == 3:
                    part = part.rearrange("p (a b) -> p a b", a=shape[1])
                return part
        raise ValueError("the areas are full")


def count(i, k, n, par):
    return i * (2 * k) + (2 * n + par + 1)


class DeltaHead:

    def __init__(self, mem, banks, xin, z_in):
        self.tb, self.sb, self.xb = banks
        self.xin = xin
        self.z_in = z_in
        self.cv = mem.take([P, 3, SEQ])
        self.kb = mem.take([P, SEQ])
        self.e_g = mem.take([P, SEQ])
        self.q_dec = mem.take([P, SEQ])
        self.dec = mem.take([P, SEQ])
        self.n_t = mem.take([P, SEQ])
        self.qk_t = mem.take([P, SEQ])
        self.k_bg = mem.take([P, NT, HD])
        self.k_tail = mem.take([P, NT, HD])
        self.v_b = mem.take([P, NT, HD])
        self.inv = mem.take([P, SEQ])
        self.inv_t = mem.take([P, SEQ])
        self.state = mem.take([P, HD])
        self.v_new = mem.take([P, HD])
        self.g_last = mem.take([P, SEQ // CHUNK])
        self.o_ms = mem.take([P, NT])
        self.sq = mem.take([P, 2, SEQ])
        self.w_t, self.u_sol, self.x_sb = self.e_g, self.kb, self.dec
        self.z_sig = self.k_bg
        self.c_lev = [self.cv[:, 1, :], self.cv[:, 2, :]]
        self.o_out = self.sq[:, 0, :]


def build(nc, a, out, dram):
    ctx = ExitStack()
    with ctx:
        starts = {}

        def sb(name, shape, dt=F32):
            starts[name] = -(-nc.sbuf_base // 32) * 32
            return ctx.enter_context(nc.sbuf_tensor(name, shape, dt))

        def rounded(name, shape):
            return nc.alloc_sbuf_tensor_at(name + "_r", shape, F32R, offset=starts[name])

        def sem(name):
            return ctx.enter_context(nc.semaphore(name))

        proj_t = dram("proj_t", [18, NT, P, SEQ])
        proj_n = dram("proj_n", [NT, P, 4 * COLS])
        mod_rows = dram("mod_rows", [16, COLS])
        T_QA, T_KA, T_DN, T_GA, T_GB = 0, 2, 4, 10, 14

        planes = sb("planes", [P, N_CONST, P])
        small = sb("small", [P, 64])
        half_pi = sb("half_pi", [P, 1])
        eps = sb("eps", [P, 1])
        cond = sb("cond", [P, ND])
        g_pre = sb("g_pre", [P, 2, ND])
        b_col = sb("b_col", [P, 6 * ND])
        conv_col = sb("conv_col", [P, CONV * 3 * HEADS])
        mod_col = sb("mod_col", [P, 6 * ND])
        a_col = sb("a_col", [P, 2, ND])
        row_out = sb("row_out", [1, 2, COLS])
        cos_t = sb("cos_t", [ROPE, SEQ])
        sin_t = sb("sin_t", [ROPE, SEQ])
        ba = sb("ba", [P, NT, 2 * HEADS])
        raw = [sb(f"raw{i}", [P, SLOT]) for i in range(4)]
        raw_r = [rounded(f"raw{i}", [P, SLOT]) for i in range(4)]
        hi = [sb(f"hi{i}", [P, SLOT], F32R) for i in range(2)]
        area = sb("area", [P, 2 * ND, SEQ])
        area_r = rounded("area", [P, 2 * ND, SEQ])
        u_hi, u_lo = area_r[:, 0:ND, :], area_r[:, ND:2 * ND, :]
        area_1, area_2 = area[:, 0:ND, :], area[:, ND:2 * ND, :]
        stage = sb("stage", [P, 4, COLS])
        acc = sb("acc", [P, 2, COLS])
        x_all = sb("x_all", [P, NT, D])
        x_all_r = rounded("x_all", [P, NT, D])
        stage_r = rounded("stage", [P, 4, COLS])
        ada_ring = [x_all[:, s, :] for s in range(NT)]
        vecs = stage[:, 0, 0:3 * P].rearrange("p (v c) -> p v c", v=3)
        u_tmp = acc
        ssq = sb("ssq", [P, NT])
        rstd = sb("rstd", [P, NT])
        w_ba = sb("w_ba", [P, ND, 2 * HEADS])
        cond_raw = sb("cond_raw", [P, ND])
        cond_sig = sb("cond_sig", [P, ND])
        ba_hi = sb("ba_hi", [P, ND, 2 * HEADS], F32R)
        ba_lo = sb("ba_lo", [P, ND, 2 * HEADS], F32R)
        ang_mem = sb("ang_mem", [P, SLOT])
        ang_r = rounded("ang_mem", [P, SLOT])
        ang = ang_mem[0:ROPE, :].rearrange("p (a n) -> p a n", a=4)
        pos_i = sb("pos_i", [ROPE, SEQ], I32)

        ps = [ctx.enter_context(nc.psum_tensor(f"ps{i}", [P, 512], F32)) for i in range(8)]
        ident = planes[:, C_ID, :]
        ones = planes[:, C_ONES, :]

        s_const = sem("s_const")
        s_x = sem("s_x")
        s_slot = [sem(f"s_slot{i}") for i in range(4)]
        s_ada_slot = [sem(f"s_ada_slot{i}") for i in range(4)]
        s_hi = sem("s_hi")
        s_lo = sem("s_lo")
        s_used = sem("s_used")
        s_ada1_used = sem("s_ada1_used")
        s_ada_used = sem("s_ada_used")
        s_acc = sem("s_acc")
        s_mod = sem("s_mod")
        s_xn = sem("s_xn")
        s_ut = sem("s_ut")
        s_uhi = sem("s_uhi")
        s_ulo = sem("s_ulo")
        s_ba_split = sem("s_ba_split")
        s_bank = sem("s_bank")
        s_ev_a = sem("s_ev_a")
        s_ev_v = sem("s_ev_v")
        s_stored = [sem(f"s_stored{i}") for i in range(4)]
        s_row = sem("s_row")
        s_row_out = sem("s_row_out")
        s_prep_pe = sem("s_prep_pe")
        s_prep_a = sem("s_prep_a")
        s_prep_v = sem("s_prep_v")
        s_act = sem("s_act")
        s_dve = sem("s_dve")
        s_pool = sem("s_pool")

        w_in, w_ada = a["w_in"][0], a["w_ada"][0]
        w_in_v = w_in.rearrange("(t p) n -> p t n", p=P)
        w_ada_v = w_ada.rearrange("(t p) n -> p t n", p=P)
        x_v = a["x"][0].rearrange("(t p) d -> p t d", p=P)


        yb_t = dram("yb_t", [HEADS, P, SEQ])
        dtb_row = sb("dtb_row", [P, HEADS])
        alog_row = sb("alog_row", [P, HEADS])
        og_row = sb("og_row", [P, HD])
        dec_in = sb("dec_in", [P, 4, NT, HEADS])
        g_nat = sb("g_nat", [P, NT, HEADS])
        beta = sb("beta", [P, NT, HEADS])
        gcum = sb("gcum", [P, NT, HEADS])
        tail = sb("tail", [P, NT, HEADS])
        beta_g = sb("beta_g", [P, NT, HEADS])
        PAD = CONV - 1
        dn = Carve(area_1.rearrange("p a b -> p (a b)"), area_2.rearrange("p a b -> p (a b)"),
                   x_all[:, :, :].rearrange("p a b -> p (a b)"))
        dn_xin = [dn.take([P, 3, PAD + SEQ]) for _ in range(2)]
        dn_z = [dn.take([P, NT, HD]) for _ in range(2)]
        dn_heads = [DeltaHead(dn, banks, dn_xin[par], dn_z[par])
                    for par, banks in enumerate(((ps[4], ps[5], ps[6]), (ps[0], ps[1], ps[7])))]

        s_rows = sem("s_rows")
        s_dn_in = sem("s_dn_in")
        s_dn_z = sem("s_dn_z")
        s_conv = sem("s_conv")
        s_sig = sem("s_sig")
        s_silu = sem("s_silu")
        s_sq = sem("s_sq")
        s_ss = sem("s_ss")
        s_nroot = sem("s_nroot")
        s_unit = sem("s_unit")
        s_gb = sem("s_gb")
        s_gbc = sem("s_gbc")
        s_bbc = sem("s_bbc")
        s_eg = sem("s_eg")
        s_darg = sem("s_darg")
        s_dec = sem("s_dec")
        s_kb = sem("s_kb")
        s_gram = sem("s_gram")
        s_knat = sem("s_knat")
        s_vnat = sem("s_vnat")
        s_nt = sem("s_nt")
        s_qkt = sem("s_qkt")
        s_first = sem("s_first")
        s_kfac = sem("s_kfac")
        s_vb = sem("s_vb")
        s_inv1 = sem("s_inv1")
        s_inv1_out = sem("s_inv1_out")
        s_clev = sem("s_clev")
        s_xm = sem("s_xm")
        s_xc = sem("s_xc")
        s_corr = sem("s_corr")
        s_inv = sem("s_inv")
        s_uw = sem("s_uw")
        s_u = sem("s_u")
        s_w = sem("s_w")
        s_ws = sem("s_ws")
        s_vn = sem("s_vn")
        s_sd = sem("s_sd")
        s_state = sem("s_state")
        s_osq = sem("s_osq")
        s_oms = sem("s_oms")
        s_oroot = sem("s_oroot")
        s_zsig = sem("s_zsig")
        s_on = sem("s_on")
        s_ot = sem("s_ot")
        s_ot_out = sem("s_ot_out")
        s_yb = sem("s_yb")
        NL = len(LEVELS) - 1
        NC = SEQ // CHUNK

        def tiles(x):
            return x.rearrange("p (t c) -> p t c", t=NT)

        def column(x, h):
            return x[:, :, bass.ds(h, 1)].broadcast_to([P, NT, HD])

        def plane(c):
            return planes[:, c:c + 1, :].broadcast_to([P, NT, P])

        PARTS = [
            (IN_DN, T_DN, 4, False, 12), (IN_DN + 4 * COLS, T_DN + 4, 2, False, None),
            (IN_Z, 2, 2, True, None), (IN_VA, 0, 2, True, None),
            (IN_QA, T_QA, 4, False, 16), (IN_GA, T_GA, 4, False, 8), (IN_GB, T_GB, 4, False, 20),
        ]
        N_ADA1 = 8

        ya_t = dram("ya_t", [HEADS, P, SEQ])
        SCALE = HD ** -0.5
        at = Carve(area_1.rearrange("p a b -> p (a b)"), area_2.rearrange("p a b -> p (a b)"))
        at_q = [at.take([P, SEQ]) for _ in range(2)]
        at_k = [at.take([P, SEQ]) for _ in range(2)]
        at_v = [at.take([P, NT, HD]) for _ in range(2)]
        rot = at.take([P, SEQ])
        prob = at.take([P, NT, SEQ])
        prob_t = at.take([P, NT, SEQ])
        at_o = at.take([P, SEQ])
        at_raw = sb("at_raw", [P, NT])
        at_max = sb("at_max", [P, NT])
        at_sum = sb("at_sum", [P, NT])
        s_at_in = [sem(f"s_at_in{i}") for i in range(2)]
        s_rot = sem("s_rot")
        s_roped = sem("s_roped")
        s_sc = sem("s_sc")
        s_nmax = sem("s_nmax")
        s_exp = sem("s_exp")
        s_prob = sem("s_prob")
        s_pt = sem("s_pt")
        s_pt_out = sem("s_pt_out")
        s_av = sem("s_av")
        s_av_out = sem("s_av_out")
        s_ya = sem("s_ya")

        N_IN = sum(p[2] for p in PARTS)
        yh = u_hi[:, :, :]
        yl = u_lo[:, :, :]
        merged = x_all[:, :, :].rearrange("p m (k n) -> p (m k) n", n=SEQ)
        y_nat = x_all
        gate_in = sb("gate_in", [P, 4, SEQ])
        s_yl = sem("s_yl")
        s_yh = sem("s_yh")
        s_ysplit = sem("s_ysplit")
        s_gate = [sem(f"s_gate{i}") for i in range(2)]
        s_gsig = sem("s_gsig")
        s_merged = sem("s_merged")

        rows4 = dram("rows4", [4, D])
        x1_s = dram("x1_s", [SEQ, D])
        u2_s = dram("u2_s", [SEQ, D])
        yb_s = dram("yb_s", [2 * SEQ, D])
        NB = EXPERTS + MAX_OVER
        table = dram("table", [P * (NB + 1), 1], I32)
        mr = sb("mr", [ND, 4, P])
        br = sb("br", [ND, 4, P])
        gr = sb("gr", [ND, 3, P])
        ra = Carve(area_2.rearrange("p a b -> p (a b)"))
        row_g1, row_a2, row_s2 = ra.take([P, D]), ra.take([P, D]), ra.take([P, D])
        x_in = ra.take([P, D])
        u2_t = area_1
        w_r = sb("w_r", [P, ND, GROUPS + EXPERTS])
        NR = GROUPS + EXPERTS
        b_r = sb("b_r", [P, NR])
        ss2 = sb("ss2", [P, 2, NT])
        s_mr = sem("s_mr")
        s_rows4 = sem("s_rows4")
        s_rowb = sem("s_rowb")
        s_xin2 = sem("s_xin2")
        s_res = sem("s_res")
        s_rooty = sem("s_rooty")
        s_x1 = sem("s_x1")
        s_root1 = sem("s_root1")
        s_u2 = sem("s_u2")
        s_x1_out = sem("s_x1_out")
        s_u2_out = sem("s_u2_out")
        s_u2t = sem("s_u2t")
        s_u2t_out = sem("s_u2t_out")
        s_route_v = sem("s_route_v")
        s_route_a = sem("s_route_a")
        s_route_pe = sem("s_route_pe")
        s_table = sem("s_table")
        s_logit = sem("s_logit")

        rt = Carve(stage[:, :, :].rearrange("p a b -> p (a b)"))
        logit = rt.take([P, NT, NR])
        e_log = rt.take([P, NT, EXPERTS])
        tmp32 = rt.take([P, NT, EXPERTS])
        oh1 = rt.take([P, NT, EXPERTS])
        oh2 = rt.take([P, NT, EXPERTS])
        both = rt.take([P, NT, EXPERTS])
        rank = rt.take([P, NT, EXPERTS])
        oh_g = rt.take([P, NT, GROUPS])
        tmp4 = rt.take([P, NT, GROUPS])
        r1 = rt.take([P, 16, NT])
        cnt = rt.take([P, 4, EXPERTS])
        tmp7 = rt.take([P, MAX_OVER, EXPERTS])
        over_t = rt.take([P, P])
        place = rt.take([P, 2, NT])
        wts = sb("wts", [P, 2, NT])
        place_i = sb("place_i", [P, 2 * NT], I32)
        id_i = sb("id_i", [P, 2 * NT], I32)
        plan_f = sb("plan_f", [P, MAX_OVER + 1])
        plan = sb("plan", [P, MAX_OVER + 1], I32)
        fill = sb("fill", [P, NB + 1], I32)
        row_i = sb("row_i", [P, NB + 1], I32)
        row_f = sb("row_f", [P, NB + 1])
        tok_f = sb("tok_f", [P, NB + 1])
        tok_i = sb("tok_i", [P, NB + 1], I32)
        NO_ROW = 1 << 20

        mo = Carve(area_2.rearrange("p a b -> p (a b)"), area_1.rearrange("p a b -> p (a b)"))
        mo_r = Carve(u_lo.rearrange("p a b -> p (a b)"), u_hi.rearrange("p a b -> p (a b)"))
        m_raw = [raw[i][:, :] for i in range(4)] + [mo.take([P, SLOT]) for _ in range(8)]
        m_raw_r = [raw_r[i][:, :] for i in range(4)] + [mo_r.take([P, SLOT]) for _ in range(8)]
        m_hi = [hi[i][:, :] for i in range(2)] + [
            ang_r[:, :], stage_r[:, :, :].rearrange("p a b -> p (a b)")]
        mx = Carve(x_all[:, :, :].rearrange("p a b -> p (a b)"))
        xg = mx.take([P, D])
        y_e = mx.take([P, D])
        mx_r = Carve(x_all_r[:, 2:4, :].rearrange("p a b -> p (a b)"))
        xe_hi = mx_r.take([P, ND, P])
        xe_lo = mx_r.take([P, ND, P])
        me = Carve(gate_in[:, :, :].rearrange("p a b -> p (a b)"))
        h_sig, h_e = me.take([P, FF]), me.take([P, FF])
        gate_in_r = rounded("gate_in", [P, 4, SEQ])
        ht_hi = gate_in_r[:, 2, :].rearrange("p (a b) -> p a b", a=NF)
        ht_lo = gate_in_r[:, 3, :].rearrange("p (a b) -> p a b", a=NF)
        g_idx = sb("g_idx", [P, 1], I32)
        y_idx = sb("y_idx", [P, 1], I32)
        s_mslot = s_slot + s_ada_slot + [sem(f"s_mslot{i}") for i in range(4)]
        mslot_base = [16 * (N_ADA1 + N_IN + 8)] * 4 + [16 * 16] * 4 + [0] * 4
        s_mhi = sem("s_mhi")
        s_mlo = sem("s_mlo")
        s_mused = sem("s_mused")
        s_gi = sem("s_gi")
        s_yi = sem("s_yi")
        s_xg = sem("s_xg")
        s_xt = sem("s_xt")
        s_xehi = sem("s_xehi")
        s_xelo = sem("s_xelo")
        s_hsig = sem("s_hsig")
        s_h = sem("s_h")
        s_ht = sem("s_ht")
        s_hthi = sem("s_hthi")
        s_htlo = sem("s_htlo")
        s_ybank = sem("s_ybank")
        s_ye_a = sem("s_ye_a")
        s_ye_v = sem("s_ye_v")
        s_ysc = sem("s_ysc")

        fi = Carve(*m_raw)
        row_g2 = fi.take([P, D])
        f_y = [[fi.take([P, D]) for _ in range(2)] for _ in range(2)]
        f_x = [fi.take([P, D]) for _ in range(2)]
        f_sq = fi.take([P, D])
        ss_f = sb("ss_f", [P, NT])
        s_g2 = sem("s_g2")
        s_f_y = sem("s_f_y")
        s_f_ss = sem("s_f_ss")
        s_f_out = sem("s_f_out")
        s_out = [sem(f"s_out{i}") for i in range(2)]

        def split3(eng, bank, l_hi, l_lo, r_hi, r_lo, first, last):
            eng.matmul(bank, l_hi, r_hi, start=first, stop=False)
            eng.matmul(bank, l_hi, r_lo, start=False, stop=False)
            return eng.matmul(bank, l_lo, r_hi, start=False, stop=last)

        block = ctx.enter_context(nc.Block())

        @block.sync
        def _(sp):
            sp.dma_start(planes[:, :, :], a["planes"]).then_inc(s_const, 16)
            sp.dma_start(small[:, :], a["small"]).then_inc(s_const, 16)
            sp.dma_start(vecs[0:ND, 0, :], a["c"][0].rearrange("(t p) -> t p", p=P)).then_inc(s_const, 16)
            sp.dma_start(vecs[ND:2 * ND, 0, :], a["norm_mix_pre"][0].rearrange("(t p) -> t p", p=P)).then_inc(s_const, 16)
            sp.dma_start(vecs[2 * ND:3 * ND, 0, :], a["norm_ffn_pre"][0].rearrange("(t p) -> t p", p=P)).then_inc(s_const, 16)
            sp.dma_start(vecs[0:96, 1, :], a["b_ada"][0].rearrange("(t p) -> t p", p=P)).then_inc(s_const, 16)
            sp.dma_start(vecs[0:96, 2, :], a["conv_w"][0].rearrange("k (t p) -> (k t) p", p=P)).then_inc(s_const, 16)
            sp.dma_start(pos_i[:, :], a["positions"].broadcast_to([ROPE, SEQ])).then_inc(s_const, 16)
            with sp.Fori(0, N_ADA1) as c:
                for s in range(4):
                    sp.wait_ge(s_ada1_used, c * 4 + (s + 1))
                    sp.dma_start(raw[s][:, :].rearrange("p (t n) -> p t n", t=4),
                                 w_ada_v[:, 4 * s:4 * s + 4, bass.ds(c * COLS, COLS)]).then_inc(s_slot[s], 16)
            for t in range(NT):
                sp.dma_start(x_all[:, t, :], x_v[:, t, :]).then_inc(s_x, 16)
            sp.dma_start(w_ba[:, :, :], w_in_v[:, :, IN_BETA:IN_BETA + 2 * HEADS]).then_inc(s_x, 16)
            sp.wait_ge(s_ada1_used, 4 + 4 * N_ADA1)
            done = ada_done = 0
            for col0, row0, n, natural, ada0 in PARTS:
                with sp.Fori(0, n) as c:
                    for s in range(4):
                        sp.wait_ge(s_used, (c + done) * 4 + (s + 1))
                        sp.dma_start(raw[s][:, :].rearrange("p (t n) -> p t n", t=4),
                                     w_in_v[:, 4 * s:4 * s + 4, bass.ds(c * COLS + col0, COLS)]).then_inc(s_slot[s], 16)
                    if ada0 is not None:
                        for s in range(4):
                            if s == 0 and ada_done == 0:
                                sp.wait_ge(s_ut, ND)
                            sp.wait_ge(s_ada_used, (c + ada_done) * 4 + (s + 1))
                            sp.dma_start(ada_ring[s].rearrange("p (t n) -> p t n", t=4),
                                         w_ada_v[:, 4 * s:4 * s + 4, bass.ds((c + ada0) * COLS, COLS)]).then_inc(s_ada_slot[s], 16)
                done += n
                if ada0 is not None:
                    ada_done += n
            w_moba = a["w_branch_moba"][0].rearrange("(t p) n -> p t n", p=P)
            w_delta = a["w_branch_delta"][0].rearrange("(t p) n -> p t n", p=P)
            w_out = a["w_out"][0].rearrange("(t p) n -> p t n", p=P)

            def merge_slot(c, s):
                sp.wait_ge(s_used, (c + N_IN) * 4 + (s + 1))
                sp.dma_start(raw[s][:, :].rearrange("p (t n) -> p t n", t=4),
                             (w_moba, w_delta)[s // 2][:, 4 * (s % 2):4 * (s % 2) + 4, bass.ds(c * COLS, COLS)]).then_inc(s_slot[s], 16)

            for s in range(4):
                merge_slot(0, s)
            for b in range(4):
                sp.wait_ge(s_stored[b], 16 * N_IN)
            sp.wait_ge(s_pool, 1)
            blocks = proj_t.rearrange("c b p n -> (c b) p n")[T_DN * 4:(T_DN + 6) * 4].rearrange("(j h) p n -> h p j n", j=3)
            with sp.Fori(0, HEADS // 2) as i:
                sp.wait_ge(s_silu, i * 6)
                for par in range(2):
                    sp.dma_start(dn_xin[par][:, :, PAD:PAD + SEQ],
                                 blocks[bass.ds(i * 2 + par, 1)].rearrange("a p j n -> (a p) j n")).then_inc(s_dn_in, 16)
                sp.wait_ge(s_on, i * 2)
                for par in range(2):
                    sp.dma_start(dn_z[par], proj_n[:, :, bass.ds((i * 2 + par) * HD + WIDTH, HD)].rearrange("b p n -> p b n")).then_inc(s_dn_z, 16)
            sp.wait_ge(s_ot_out, HEADS)
            sp.wait_ge(s_yb, 16 * HEADS)
            tq = proj_t.rearrange("c b p n -> (c b) p n")
            with sp.Fori(0, HEADS // 2) as i:
                for par in range(2):
                    sp.wait_ge(s_av, i * 2 + (par + 1))
                    for dst, first in ((at_q[par], T_QA * 4), (at_k[par], T_KA * 4)):
                        sp.dma_start(dst, tq[bass.ds(i * 2 + (par + first), 1)].rearrange("a p n -> (a p) n")).then_inc(s_at_in[par], 16)
                    sp.dma_start(at_v[par], proj_n[:, :, bass.ds((i * 2 + par) * HD, HD)].rearrange("b p n -> p b n")).then_inc(s_at_in[par], 16)
            sp.wait_ge(s_ya, 16 * HEADS)
            sp.dma_start(area_2[:, 0:HEADS, :], ya_t.rearrange("h p n -> p h n")).then_inc(s_yl, 16)
            sp.dma_start(area_2[:, HEADS:2 * HEADS, :], yb_t.rearrange("h p n -> p h n")).then_inc(s_yl, 16)
            with sp.Fori(1, 4) as c:
                for s in range(4):
                    merge_slot(c, s)
            with sp.Fori(0, 4) as c:
                for s in range(4):
                    sp.wait_ge(s_used, (c + (N_IN + 4)) * 4 + (s + 1))
                    sp.dma_start(raw[s][:, :].rearrange("p (t n) -> p t n", t=4),
                                 w_out[:, 4 * s:4 * s + 4, bass.ds(c * COLS, COLS)]).then_inc(s_slot[s], 16)
            sp.dma_start(w_r[:, :, 0:GROUPS], a["router_group_w"][0].rearrange("(t p) n -> p t n", p=P)).then_inc(s_rowb, 16)
            sp.dma_start(w_r[:, :, GROUPS:NR], a["router_expert_w"][0].rearrange("(t p) n -> p t n", p=P)).then_inc(s_rowb, 16)
            sp.dma_start(b_r[:, 0:GROUPS], a["router_group_b"].broadcast_to([P, GROUPS])).then_inc(s_rowb, 16)
            sp.dma_start(b_r[:, GROUPS:NR], a["router_expert_b"].broadcast_to([P, EXPERTS])).then_inc(s_rowb, 16)
            sp.wait_ge(s_used, 4 + 4 * (N_IN + 8))
            sp.wait_ge(s_rows4, 16)
            for n, dst in enumerate((row_g1, row_s2, row_a2)):
                sp.dma_start(dst, rows4[n:n + 1, :].broadcast_to([P, D])).then_inc(s_rowb, 16)
            for m in range(NT):
                if m:
                    sp.wait_ge(s_x1, m)
                sp.dma_start(x_in, x_v[:, m, :]).then_inc(s_xin2, 16)

            def expert_slot(e, j, s):
                sp.wait_ge(s_mused, j * 12 + (s + 1))
                if s < 8:
                    src = a[("expert_w_gate", "expert_w_up")[s // 4]][0, bass.ds(e, 1), (s % 4) * 4 * P:(s % 4 + 1) * 4 * P, :]
                    sp.dma_start(m_raw[s].rearrange("p (t n) -> p t n", t=4),
                                 src.rearrange("a (t p) n -> p (a t) n", p=P)).then_inc(s_mslot[s], 16)
                else:
                    src = a["expert_w_down"][0, bass.ds(e, 1), (s - 8) * P:(s - 7) * P, :]
                    sp.dma_start(m_raw[s], src.rearrange("a p n -> (a p) n")).then_inc(s_mslot[s], 16)

            for s in range(4):
                expert_slot(0, 0, s)
            sp.wait_ge(s_u2, NT)
            sp.wait_ge(s_logit, 1)
            for s in range(4, 12):
                expert_slot(0, 0, s)
            with sp.Fori(1, EXPERTS) as j:
                for s in range(12):
                    expert_slot(j, j, s)
            sp.wait_ge(s_route_v, 6)
            n_blocks = sp.value_load(plan[0:1, MAX_OVER:MAX_OVER + 1], min_val=EXPERTS, max_val=NB)
            with sp.If(n_blocks > EXPERTS):
                with sp.Fori(EXPERTS, n_blocks) as j:
                    e = sp.value_load(plan[0:1, bass.ds(j - EXPERTS, 1)], min_val=0, max_val=EXPERTS - 1)
                    for s in range(12):
                        expert_slot(e, j, s)
            for s in range(3):
                expert_slot(0, n_blocks, s)
            sp.wait_ge(s_mused, n_blocks * 12 + 12)
            sp.wait_ge(s_mlo, n_blocks * 12 + 3)
            sp.dma_start(row_g2, rows4[3:4, :].broadcast_to([P, D])).then_inc(s_g2, 16)
            sp.wait_ge(s_ysc, n_blocks * 16)
            for m in range(NT):
                if m >= 2:
                    sp.wait_ge(s_f_out, m - 1)
                    sp.wait_ge(s_out[m % 2], (m // 2) * 16)
                for k in range(2):
                    sp.dma_start(f_y[m % 2][k], yb_s[k * SEQ + m * P:k * SEQ + (m + 1) * P, :]).then_inc(s_at_in[m % 2], 16)
                sp.dma_start(f_x[m % 2], x1_s[m * P:(m + 1) * P, :]).then_inc(s_at_in[m % 2], 16)

        @block.gpsimd
        def _(pool):
            done = ada_done = 0
            for col0, row0, n, natural, ada0 in PARTS:
                with pool.Fori(0, n) as c:
                    for b in range(4):
                        pool.wait_ge((s_ev_a, s_ev_v)[b // 2], (c + done) * 2 + (b % 2 + 3))
                        dst = (proj_n[b, :, bass.ds((c + row0) * COLS, COLS)] if natural else
                               proj_t[bass.ds(c + row0, 1), b].rearrange("a p n -> (a p) n"))
                        pool.dma_start(dst,
                                     stage[:, b, :]).then_inc(s_stored[b], 16)
                    if ada0 is not None:
                        pool.wait_ge(s_row, c + (ada_done + 2))
                        pool.dma_start(mod_rows[bass.ds(c + (ada0 - N_ADA1), 1), :], row_out[:, 0, :]).then_inc(s_row_out, 16)
                done += n
                if ada0 is not None:
                    ada_done += n
            for b in range(4):
                pool.wait_ge(s_stored[b], 16 * done)

            pool.dma_start(dtb_row[:, :], a["dn_dt_bias"].broadcast_to([P, HEADS])).then_inc(s_rows, 16)
            pool.dma_start(alog_row[:, :], a["dn_a_log"].broadcast_to([P, HEADS])).then_inc(s_rows, 16)
            pool.dma_start(og_row[:, :], a["dn_out_norm"].broadcast_to([P, HD])).then_inc(s_rows, 16)
            for par in range(2):
                ins = pool.memset(dn_xin[par][:, :, 0:PAD], 0.0)
            ins.then_inc(s_pool, 1)
            with pool.Fori(0, HEADS // 2) as i:
                for n in range(NL):
                    for par, d in enumerate(dn_heads):
                        if n == 0:
                            pool.wait_ge(s_vnat, count(i, 1, 0, par))
                            pool.wait_ge(s_gram, count(i, 2, 1, par))
                            pool.wait_ge(s_nt, count(i, 1, 0, par))
                        if n >= 2:
                            pool.wait_ge(s_xm, count(i, NL, n - 2, par))
                        pool.tensor_tensor(tiles(d.c_lev[n % 2]), tiles(d.n_t), plane(C_LEV + 1 + n), ALU.mult).then_inc(s_clev, 1)
                for par, d in enumerate(dn_heads):
                    pool.wait_ge(s_ot_out, count(i, 1, 0, par))
                    pool.dma_start(yb_t[bass.ds(i * 2 + par, 1)].rearrange("a p n -> (a p) n"), d.o_out).then_inc(s_yb, 16)
            pool.wait_ge(s_yb, 16 * HEADS)
            with pool.Fori(0, HEADS) as h:
                pool.wait_ge(s_av_out, h + 1)
                pool.dma_start(ya_t[bass.ds(h, 1)].rearrange("a p n -> (a p) n"), at_o).then_inc(s_ya, 16)
            tg = proj_t.rearrange("c b p n -> (c b) p n")
            with pool.Fori(0, 4) as c:
                for b in range(4):
                    pool.wait_ge(s_merged, c * 4 + (b + 3))
                    for k, first in enumerate((T_GA * 4, T_GB * 4)):
                        pool.dma_start(gate_in[:, (b % 2) * 2 + k, :],
                                       tg[bass.ds(c * 4 + (b + first), 1)].rearrange("a p n -> (a p) n")).then_inc(s_gate[b % 2], 16)
            pool.wait_ge(s_row_out, 16 * 16)
            flat = mod_rows.rearrange("c n -> (c n)")
            pool.dma_start(mr[:, :, :], flat.rearrange("(v t p) -> t v p", v=4, p=P)).then_inc(s_mr, 16)
            pool.dma_start(br[:, :, :], a["b_ada"][0, 2 * D:6 * D].rearrange("(v t p) -> t v p", v=4, p=P)).then_inc(s_mr, 16)
            for n, g in enumerate(("norm_mix_post", "norm_ffn_pre", "norm_ffn_post")):
                pool.dma_start(gr[:, n, :], a[g][0].rearrange("(t p) -> t p", p=P)).then_inc(s_mr, 16)
            pool.wait_ge(s_res, 1)
            pool.dma_start(rows4.rearrange("v (t p) -> t v p", p=P), mr[:, :, :]).then_inc(s_rows4, 16)
            for m in range(NT):
                pool.wait_ge(s_x1, m + 1)
                pool.dma_start(x1_s[m * P:(m + 1) * P, :], y_nat[:, m, :]).then_inc(s_x1_out, 16)
            for m in range(NT):
                pool.wait_ge(s_u2, m + 1)
                pool.dma_start(u2_s[m * P:(m + 1) * P, :], y_nat[:, m, :]).then_inc(s_u2_out, 16)
            pool.memset(fill[:, :], NO_ROW).then_inc(s_pool, 1)
            pool.wait_ge(s_pool, 2)
            pool.dma_start(table.rearrange("(p b) a -> p (b a)", p=P), fill[:, :]).then_inc(s_table, 16)
            pool.wait_ge(s_table, 16)
            pool.wait_ge(s_route_v, 8)
            for n in range(2 * NT):
                pool.indirect_dma_start(out=table, out_offset=bass.IndirectOffsetOnAxis(ap=place_i[:, n:n + 1], axis=0),
                                        in_=id_i[:, n:n + 1], in_offset=None,
                                        bounds_check=P * (NB + 1) - 1, oob_is_err=False).then_inc(s_table, 16)
            pool.wait_ge(s_table, 16 + 16 * 2 * NT)
            pool.dma_start(row_i[:, :], table.rearrange("(p b) a -> p (b a)", p=P)).then_inc(s_table, 16)
            pool.wait_ge(s_u2_out, 16 * NT)
            pool.wait_ge(s_u2t, ND)
            pool.memset(xg, 0.0).then_inc(s_pool, 1)
            pool.wait_ge(s_pool, 3)
            pool.wait_ge(s_route_v, 9)
            pool.wait_ge(s_route_v, 6)
            n_blocks = pool.value_load(plan[0:1, MAX_OVER:MAX_OVER + 1], min_val=EXPERTS, max_val=NB)

            def gather(j, n):
                pool.tensor_copy(g_idx[:, :], tok_i[:, bass.ds(j, 1)]).then_inc(s_gi, 1)
                pool.wait_ge(s_gi, n)
                pool.nop(nofuse=True)
                pool.indirect_dma_start(out=xg, out_offset=None, in_=u2_s,
                                        in_offset=bass.IndirectOffsetOnAxis(ap=g_idx[:, :], axis=0),
                                        bounds_check=SEQ - 1, oob_is_err=False).then_inc(s_xg, 16)

            gather(0, 1)
            with pool.Fori(0, n_blocks) as j:
                pool.wait_ge(s_xt, j * 4 + 4)
                pool.wait_ge(s_xg, j * 16 + 16)
                gather(j + 1, j + 2)
                pool.wait_ge(s_ysc, j * 16)
                pool.tensor_copy(y_idx[:, :], row_i[:, bass.ds(j, 1)]).then_inc(s_yi, 1)
                pool.wait_ge(s_yi, j + 1)
                pool.wait_ge(s_ye_a, j * 2 + 2)
                pool.wait_ge(s_ye_v, j * 2 + 2)
                pool.nop(nofuse=True)
                pool.indirect_dma_start(out=yb_s, out_offset=bass.IndirectOffsetOnAxis(ap=y_idx[:, :], axis=0),
                                        in_=y_e, in_offset=None,
                                        bounds_check=2 * SEQ - 1, oob_is_err=False).then_inc(s_ysc, 16)
            pool.wait_ge(s_xg, n_blocks * 16 + 16)
            pool.wait_ge(s_ysc, n_blocks * 16)
            pool.nop(nofuse=True)
            for m in range(NT):
                pool.wait_ge(s_f_out, m + 1)
                pool.dma_start(out[0, m * P:(m + 1) * P, :], f_x[m % 2]).then_inc(s_out[m % 2], 16)
            for par in range(2):
                pool.wait_ge(s_out[par], 16 * NT // 2)

        @block.tensor
        def _(pe):
            pe.sem_inc(s_used, 4)
            pe.wait_ge(s_const, 16 * 8)
            pe.transpose(ps[7][:, 0:48], vecs[0:48, 0, :], ident[0:48, 0:48])
            pe.transpose(ps[7][:, 64:160], vecs[0:96, 1, :], ident[0:96, 0:96])
            pe.transpose(ps[7][:, 192:288], vecs[0:96, 2, :], ident[0:96, 0:96]).then_inc(s_prep_pe, 1)

            def mod_columns(c, n, par):
                pe.wait_ge(s_acc, n)
                for j in range(4):
                    mm = pe.matmul(ps[6][:, bass.ds(c * 4 + j, 1)], acc[:, par, j * P:(j + 1) * P],
                                   ones[:, 0:1], start=True, stop=True)
                mm.then_inc(s_mod, 1)

            with pe.Fori(0, N_ADA1 // 2) as i:
                for par in range(2):
                    mod_columns(i * 2 + par, i * 2 + (par + 1), par)
            pe.wait_ge(s_xn, NT)
            for t in range(ND):
                if t >= 4:
                    pe.wait_ge(s_uhi, t - 3)
                for m in range(NT):
                    tr = pe.transpose(ps[t % 4][:, m * P:(m + 1) * P], x_all[:, m, t * P:(t + 1) * P], ident)
                tr.then_inc(s_ut, 1)
            pe.wait_ge(s_ulo, ND)
            pe.wait_ge(s_ba_split, 2)
            for m in range(NT):
                tok = slice(m * P, (m + 1) * P)
                for t in range(ND):
                    mm = split3(pe, ps[5][:, m * 16:(m + 1) * 16], u_hi[:, t, tok], u_lo[:, t, tok],
                                ba_hi[:, t, :], ba_lo[:, t, :], t == 0, t == ND - 1)
            mm.then_inc(s_prep_pe, 1)
            pe.wait_ge(s_uhi, ND)
            pe.wait_ge(s_prep_a, 5)

            done = ada_done = 0
            for col0, row0, n, natural, ada0 in PARTS:
                with pe.Fori(0, n) as c:
                    for s in range(4):
                        pe.wait_ge(s_lo, (c + done) * 4 + (s + 1))
                        for b in range(4):
                            if s == 0:
                                pe.wait_ge((s_ev_a, s_ev_v)[b // 2], (c + done) * 2 + (b % 2 + 1))
                            for t in range(4):
                                cols = slice(t * COLS, (t + 1) * COLS)
                                part = slice(t * COLS + b * P, t * COLS + (b + 1) * P)
                                w_lo = raw_r[s]
                                k = 4 * s + t
                                first, last = k == 0, k == ND - 1
                                if natural:
                                    tok = slice(b * P, (b + 1) * P)
                                    mm = split3(pe, ps[b][:, :], u_hi[:, k, tok], u_lo[:, k, tok],
                                                hi[s % 2][:, cols], w_lo[:, cols], first, last)
                                else:
                                    mm = split3(pe, ps[b][:, :], hi[s % 2][:, part], w_lo[:, part],
                                                u_hi[:, k, :], u_lo[:, k, :], first, last)
                            if s == 3 and b < 3:
                                mm.then_inc(s_bank, 1)
                        mm.then_inc(s_used, 1)
                    if ada0 is not None:
                        pe.wait_ge(s_acc, c + (N_ADA1 + ada_done + 1))
                        pe.wait_ge(s_row, c + (ada_done + 1))
                        pe.matmul(ps[7][0:1, :], ones[:, 0:1], acc[:, 0, :], start=True, stop=True).then_inc(s_mod, 1)
                done += n
                if ada0 is not None:
                    ada_done += n

            pe.wait_ge(s_prep_v, 4)
            for t in range(NT):
                pe.matmul(ps[5][:, t * HEADS:(t + 1) * HEADS], planes[:, C_CUM, :], g_nat[:, t, :], start=True, stop=True)
                mm = pe.matmul(ps[5][:, (NT + t) * HEADS:(NT + t + 1) * HEADS], planes[:, C_TAIL, :], g_nat[:, t, :], start=True, stop=True)
            mm.then_inc(s_prep_pe, 1)

            def per_tile(bank, lhs, rhs):
                for t in range(NT):
                    c = slice(t * P, (t + 1) * P)
                    mm = pe.matmul(bank[:, c], lhs[:, c], rhs if rhs.shape[1] == P else rhs[:, c], start=True, stop=True)
                return mm

            def per_tile_t(bank, x):
                for t in range(NT):
                    c = slice(t * P, (t + 1) * P)
                    mm = pe.transpose(bank[:, c], x[:, c], ident)
                return mm

            def dn_norms(i):
                for n, j in enumerate((1, 0)):
                    for par, d in enumerate(dn_heads):
                        pe.wait_ge(s_sq, count(i, 2, n, par))
                        if n == 0 and par == 0:
                            pe.wait_ge(s_state, i * 2 * NC)
                            pe.wait_ge(s_on, i * 2)
                            pe.wait_ge(s_ot_out, i * 2)
                        pe.matmul((d.sb, d.tb)[j][:, :], ones, d.sq[:, j, :], start=True, stop=True).then_inc(s_ss, 1)

            def dn_decay(i):
                for par, d in enumerate(dn_heads):
                    pe.wait_ge(s_gb, count(i, 1, 0, par))
                    per_tile(d.xb, d.inv, planes[:, C_CUM, :]).then_inc(s_gbc, 1)
                for par, d in enumerate(dn_heads):
                    pe.wait_ge(s_nroot, count(i, 2, 0, par))
                    per_tile(d.tb, d.inv_t, ident).then_inc(s_bbc, 1)

            def dn_gram(i):
                for par, d in enumerate(dn_heads):
                    pe.wait_ge(s_kb, count(i, 1, 0, par))
                    pe.wait_ge(s_nroot, count(i, 2, 1, par))
                    per_tile(d.sb, d.cv[:, 1, :], d.kb).then_inc(s_gram, 1)
                for par, d in enumerate(dn_heads):
                    pe.wait_ge(s_unit, count(i, 2, 1, par))
                    per_tile(d.tb, d.cv[:, 1, :], d.cv[:, 0, :]).then_inc(s_gram, 1)

            def dn_naturals(i):
                for par, d in enumerate(dn_heads):
                    pe.wait_ge(s_darg, count(i, 1, 0, par))
                    per_tile_t(d.xb, d.cv[:, 1, :]).then_inc(s_knat, 1)
                for par, d in enumerate(dn_heads):
                    pe.wait_ge(s_silu, count(i, 3, 2, par))
                    pe.wait_ge(s_qkt, count(i, 1, 0, par))
                    per_tile_t(d.tb, d.cv[:, 2, :]).then_inc(s_vnat, 1)
                for par, d in enumerate(dn_heads):
                    pe.wait_ge(s_first, count(i, 1, 0, par))
                    per_tile_t(d.sb, d.inv_t).then_inc(s_inv1, 1)

            def dn_level(i, n):
                for par, d in enumerate(dn_heads):
                    if n == 0:
                        pe.wait_ge(s_inv1_out, count(i, 1, 0, par))
                        pe.wait_ge(s_kfac, count(i, 1, 0, par))
                    else:
                        pe.wait_ge(s_inv, count(i, NL, n - 1, par))
                    pe.wait_ge(s_clev, count(i, NL, n, par))
                    per_tile(d.xb, d.c_lev[n % 2], d.inv).then_inc(s_xm, 1)
                for par, d in enumerate(dn_heads):
                    pe.wait_ge(s_xc, count(i, NL, n, par))
                    if n == 0:
                        pe.wait_ge(s_vb, count(i, 1, 0, par))
                    mm = per_tile(d.tb, d.x_sb, d.inv_t)
                    if n < NL - 1:
                        mm = per_tile(d.sb, d.inv_t, d.x_sb)
                    mm.then_inc(s_corr, 1)

            def dn_solve(i):
                for par, d in enumerate(dn_heads):
                    pe.wait_ge(s_inv, count(i, NL, NL - 1, par))
                    per_tile(d.tb, d.inv_t, d.v_b.rearrange("p t c -> p (t c)"))
                    per_tile(d.sb, d.k_bg.rearrange("p t c -> p (t c)"), d.inv_t).then_inc(s_uw, 1)

            def rows_of(c):
                return slice((c % 2) * CHUNK, (c % 2 + 1) * CHUNK), c // 2

            def dn_scan_w(i, c):
                r, t = rows_of(c)
                for par, d in enumerate(dn_heads):
                    if c == 1:
                        pe.wait_ge(s_w, count(i, 1, 0, par))
                    pe.wait_ge(s_state, count(i, NC, c - 1, par))
                    pe.nop(nofuse=True)
                    pe.matmul(d.xb[r, 0:HD], d.w_t[:, c * CHUNK:(c + 1) * CHUNK], d.state, start=True, stop=True).then_inc(s_ws, 1)

            def dn_scan_o(i, c):
                r, t = rows_of(c)
                for par, d in enumerate(dn_heads):
                    vn = d.u_sol[r, t * HD:(t + 1) * HD] if c == 0 else d.v_new[r, :]
                    if c == 0:
                        pe.wait_ge(s_u, count(i, 1, 0, par))
                        pe.wait_ge(s_w, count(i, 1, 0, par))
                    else:
                        pe.matmul(d.tb[r, t * HD:(t + 1) * HD], d.q_dec[:, c * CHUNK:(c + 1) * CHUNK], d.state, start=True, stop=False)
                        pe.wait_ge(s_vn, count(i, NC - 1, c - 1, par))
                    pe.nop(nofuse=True)
                    pe.matmul(d.tb[r, t * HD:(t + 1) * HD], d.qk_t[r, c * CHUNK:(c + 1) * CHUNK], vn, start=c == 0, stop=True)
                    pe.matmul(d.sb[:, 0:HD], d.k_tail[r, t, :], vn, start=True, stop=True).then_inc(s_sd, 1)

            def dn_out(i):
                for par, d in enumerate(dn_heads):
                    pe.wait_ge(s_on, count(i, 1, 0, par))
                    per_tile_t(d.xb, d.o_out).then_inc(s_ot, 1)

            pe.wait_ge(s_ev_a, 2 * N_IN + 2)
            pe.wait_ge(s_ev_v, 2 * N_IN + 2)
            with pe.Fori(0, HEADS // 2) as i:
                dn_norms(i)
                dn_decay(i)
                dn_gram(i)
                dn_naturals(i)
                for n in range(NL):
                    dn_level(i, n)
                dn_solve(i)
                for c in range(NC):
                    if c:
                        dn_scan_w(i, c)
                    dn_scan_o(i, c)
                dn_out(i)
            pe.sem_inc(s_av, 2)
            with pe.Fori(0, HEADS // 2) as i:
                for par in range(2):
                    h = i * 2 + par
                    pe.wait_ge(s_at_in[par], i * 48 + 48)
                    pe.wait_ge(s_pt_out, h * NT)
                    pe.nop(nofuse=True)
                    pe.matmul(ps[4][0:ROPE, :], planes[0:ROPE, C_ROT, 0:ROPE], at_q[par][0:ROPE, :], start=True, stop=True).then_inc(s_rot, 1)
                    pe.matmul(ps[5][0:ROPE, :], planes[0:ROPE, C_ROT, 0:ROPE], at_k[par][0:ROPE, :], start=True, stop=True).then_inc(s_rot, 1)
                    pe.wait_ge(s_roped, h * 2 + 2)
                    pe.wait_ge(s_av_out, h)
                    for m in range(NT):
                        pe.matmul(ps[m][:, 0:(m + 1) * P], at_q[par][:, m * P:(m + 1) * P], at_k[par][:, 0:(m + 1) * P],
                                  start=True, stop=True).then_inc(s_sc, 1)
                    for m in range(NT):
                        pe.wait_ge(s_prob, h * NT + (m + 1))
                        for k in range(m + 1):
                            tr = pe.transpose(ps[4 + k][:, m * P:(m + 1) * P], prob[:, m, k * P:(k + 1) * P], ident)
                    tr.then_inc(s_pt, 1)
                    for k in range(NT):
                        pe.wait_ge(s_pt_out, h * NT + (k + 1))
                        mm = pe.matmul(ps[0][:, k * P:SEQ], at_v[par][:, k, :], prob_t[:, k, k * P:SEQ],
                                       start=k == 0, stop=k == NT - 1)
                    mm.then_inc(s_av, 1)

            pe.wait_ge(s_ysplit, 4)
            pe.wait_ge(s_av_out, HEADS)
            with pe.Fori(0, 4) as c:
                for s in range(4):
                    pe.wait_ge(s_lo, (c + N_IN) * 4 + (s + 1))
                    for b in range(4):
                        if s == 0:
                            pe.wait_ge(s_merged, c * 4 + (b + 1))
                        for t in range(4):
                            part = slice(t * COLS + b * P, t * COLS + (b + 1) * P)
                            k = (s % 2) * 4 + t
                            y = (s // 2) * HEADS + k
                            mm = split3(pe, ps[b + 4 * (s // 2)][:, :], hi[s % 2][:, part], raw_r[s][:, part],
                                        yh[:, y, :], yl[:, y, :], k == 0, k == HEADS - 1)
                        if s == 3 and b < 3:
                            mm.then_inc(s_bank, 1)
                    mm.then_inc(s_used, 1)

            pe.wait_ge(s_ysplit, 8)
            pe.wait_ge(s_merged, 4 + 16)

            with pe.Fori(0, 4) as c:
                for s in range(4):
                    pe.wait_ge(s_lo, (c + (N_IN + 4)) * 4 + (s + 1))
                    for b in range(4):
                        if s == 0:
                            pe.wait_ge((s_ev_a, s_ev_v)[b // 2], (c + N_IN) * 2 + (b % 2 + 1))
                        tok = slice(b * P, (b + 1) * P)
                        for t in range(4):
                            cols = slice(t * COLS, (t + 1) * COLS)
                            k = 4 * s + t
                            mm = split3(pe, ps[b][:, :], yh[:, k, tok], yl[:, k, tok],
                                        hi[s % 2][:, cols], raw_r[s][:, cols], k == 0, k == ND - 1)
                        if s == 3 and b < 3:
                            mm.then_inc(s_bank, 1)
                    mm.then_inc(s_used, 1)

            pe.sem_inc(s_mused, 12)
            pe.wait_ge(s_u2, NT)
            pe.wait_ge(s_ev_a, 2 + 2 * (N_IN + 4))
            pe.wait_ge(s_ev_v, 2 + 2 * (N_IN + 4))
            for t in range(ND):
                if t >= 4:
                    pe.wait_ge(s_u2t_out, t - 3)
                for m in range(NT):
                    tr = pe.transpose(ps[t % 4][:, m * P:(m + 1) * P], y_nat[:, m, t * P:(t + 1) * P], ident)
                tr.then_inc(s_u2t, 1)
            pe.wait_ge(s_u2t_out, ND)
            pe.wait_ge(s_rowb, 16 * 7)
            for m in range(NT):
                for t in range(ND):
                    mm = pe.matmul(ps[4][:, m * NR:(m + 1) * NR], u2_t[:, t, m * P:(m + 1) * P], w_r[:, t, :],
                                   start=t == 0, stop=t == ND - 1)
            mm.then_inc(s_logit, 1)
            pe.wait_ge(s_route_v, 3)
            for m in range(NT):
                for k in range(m):
                    pe.matmul(ps[5][:, m * EXPERTS:(m + 1) * EXPERTS], ones, both[:, k, :], start=k == 0, stop=False)
                pe.matmul(ps[5][:, m * EXPERTS:(m + 1) * EXPERTS], planes[:, C_RANK, :], both[:, m, :], start=m == 0, stop=True)
            for m in range(NT):
                mm = pe.matmul(ps[6][:, 0:EXPERTS], ones, both[:, m, :], start=m == 0, stop=m == NT - 1)
            mm.then_inc(s_route_pe, 1)
            pe.wait_ge(s_route_v, 4)
            pe.transpose(ps[7][0:EXPERTS, 0:P], cnt[:, 1, :], ident).then_inc(s_route_pe, 1)
            pe.wait_ge(s_route_v, 5)
            pe.matmul(ps[5][:, 256:256 + EXPERTS], over_t[0:EXPERTS, :], planes[0:EXPERTS, C_RANK, 0:EXPERTS],
                      start=True, stop=True).then_inc(s_route_pe, 1)

            def block_transposes(n):
                for q in range(4):
                    if q >= 2:
                        pe.wait_ge(s_xelo, n + (q - 1))
                    for t in range(4):
                        tr = pe.transpose(ps[2 + q % 2][:, t * P:(t + 1) * P], xg[:, (4 * q + t) * P:(4 * q + t + 1) * P], ident)
                    tr.then_inc(s_xt, 1)

            pe.wait_ge(s_route_v, 6)
            n_blocks = pe.value_load(plan[0:1, MAX_OVER:MAX_OVER + 1], min_val=EXPERTS, max_val=NB)
            pe.wait_ge(s_xg, 16)
            block_transposes(0)
            with pe.Fori(0, n_blocks) as j:
                for s in range(8):
                    if s % 4 == 0:
                        pe.wait_ge(s_xelo, j * 4 + 4)
                        pe.wait_ge((s_htlo, s_h)[s // 4], j)
                    pe.wait_ge(s_mlo, j * 12 + (s + 1))
                    for t in range(4):
                        cols = slice(t * COLS, (t + 1) * COLS)
                        k = 4 * (s % 4) + t
                        mm = split3(pe, ps[s // 4][:, :], xe_hi[:, k, :], xe_lo[:, k, :],
                                    m_hi[s % 4][:, cols], m_raw_r[s][:, cols], k == 0, k == ND - 1)
                    mm.then_inc(s_mused, 1)
                pe.wait_ge(s_xg, j * 16 + 32)
                block_transposes(j * 4 + 4)
                pe.wait_ge(s_h, j + 1)
                for t in range(NF):
                    tr = pe.transpose(ps[0][:, t * P:(t + 1) * P], h_e[:, t * P:(t + 1) * P], ident)
                tr.then_inc(s_ht, 1)
                pe.wait_ge(s_htlo, j + 1)
                for s in range(8, 12):
                    pe.wait_ge(s_mlo, j * 12 + (s + 1))
                    for b in range(4):
                        if s == 8:
                            pe.wait_ge((s_ye_a, s_ye_v)[b // 2], j * 2)
                        cols = slice(b * COLS, (b + 1) * COLS)
                        mm = split3(pe, ps[4 + b][:, :], ht_hi[:, s - 8, :], ht_lo[:, s - 8, :],
                                    m_hi[s % 4][:, cols], m_raw_r[s][:, cols], s == 8, s == 11)
                        if s == 11 and b < 3:
                            mm.then_inc(s_ybank, 1)
                    mm.then_inc(s_mused, 1)

        @block.scalar
        def _(act):
            ch = Chain(act, s_act)
            act.sem_inc(s_ev_a, 2)
            act.wait_ge(s_prep_pe, 1)
            ch.do(act.copy(cond_raw[:, :], ps[7][:, 0:ND]))
            ch.do(act.activation(cond_sig[:, :], ps[7][:, 0:ND], ACT.Sigmoid))
            ch.do(act.copy(g_pre[:, :, :].rearrange("p a t -> p (a t)"), ps[7][:, ND:3 * ND]))
            ch.do(act.copy(b_col[:, :], ps[7][:, 64:160]))
            ch.link(act.copy(conv_col[:, :], ps[7][:, 192:288]))
            act.sem_inc(s_row, 1)
            act.sem_inc(s_prep_a, 1)
            act.wait_ge(s_prep_v, 1)
            act.activation(sin_t[:, :], ang[:, 2, :], ACT.Sin).then_inc(s_prep_a, 1)
            act.activation(cos_t[:, :], ang[:, 3, :], ACT.Sin, scale=-1.0, bias=half_pi[0:ROPE, :]).then_inc(s_prep_a, 1)
            for m in range(NT):
                act.wait_ge(s_x, 16 * (NT + 1))
                ch.do(act.activation(area_1[:, m * 4:(m + 1) * 4, :].rearrange("p a b -> p (a b)"),
                                     x_all[:, m, :], ACT.Square, accum_out=ssq[:, m:m + 1]))
            ch.sync()
            act.activation(rstd[:, :], ssq[:, :], ACT.Sqrt, scale=1.0 / D, bias=eps[:, :]).then_inc(s_prep_a, 1)
            act.wait_ge(s_mod, N_ADA1)
            act.copy(mod_col[:, 0:2 * ND], ps[6][:, 0:2 * ND]).then_inc(s_prep_a, 1)
            act.wait_ge(s_prep_v, 2)
            for t in range(ND):
                act.wait_ge(s_ut, t + 1)
                if t >= 2:
                    act.wait_ge(s_ulo, t - 1)
                ch.do(act.activation(u_tmp[:, t % 2, :], ps[t % 4][:, :], ACT.Identity, scale=a_col[:, 0, t:t + 1],
                               bias=mod_col[:, t:t + 1]))
                act.activation(u_hi[:, t, :], ps[t % 4][:, :], ACT.Identity, scale=a_col[:, 0, t:t + 1],
                               bias=mod_col[:, t:t + 1]).then_inc(s_uhi, 1)
            act.wait_ge(s_x, 16 * (NT + 1))
            act.copy(ba_hi[:, :, :], w_ba[:, :, :]).then_inc(s_ba_split, 1)
            act.wait_ge(s_prep_pe, 2)
            act.copy(ba[:, :, :].rearrange("p a b -> p (a b)"), ps[5][:, 0:NT * 16]).then_inc(s_prep_a, 1)

            def act_split(s, loaded, free):
                act.wait_ge(s_slot[s], loaded)
                act.wait_ge(s_used, free)
                act.copy(hi[s % 2][:, :], raw[s][:, :]).then_inc(s_hi, 1)

            act_split(0, N_ADA1 * 16 + 16, 3)
            done = ada_done = 0
            for col0, row0, n, natural, ada0 in PARTS:
                with act.Fori(0, n) as c:
                    for s in range(1, 5):
                        act_split(s % 4, (c + (N_ADA1 + done + s // 4)) * 16 + 16, (c + done) * 4 + (s + 3))
                    for b in range(2):
                        act.wait_ge(s_bank, (c + done) * 3 + (b + 1))
                        act.wait_ge(s_stored[b], (c + done) * 16)
                        act.copy(stage[:, b, :], ps[b][:, :]).then_inc(s_ev_a, 1)
                    if ada0 is not None:
                        act.wait_ge(s_mod, c + (N_ADA1 + ada_done + 1))
                        act.wait_ge(s_row_out, (c + ada_done) * 16)
                        act.copy(row_out[:, 0, :], ps[7][0:1, :]).then_inc(s_row, 1)
                done += n
                if ada0 is not None:
                    ada_done += n

            act.wait_ge(s_prep_v, 3)
            ch.link(act.activation(dec_in[:, 1, :, :], dec_in[:, 2, :, :], ACT.Exp))
            ch.link(act.activation(alog_row[:, :], alog_row[:, :], ACT.Exp))
            act.activation(dec_in[:, 2, :, :], dec_in[:, 1, :, :], ACT.Ln, bias=planes[:, C_ONES, 0:1]).then_inc(s_prep_a, 1)
            act.activation(beta[:, :, :], ba[:, :, 0:HEADS], ACT.Sigmoid).then_inc(s_prep_a, 1)
            act.wait_ge(s_prep_pe, 3)
            sums = ps[5][:, 0:2 * NT * HEADS].rearrange("p (a t h) -> p a t h", a=2, t=NT)
            ch.do(act.copy(gcum[:, :, :], sums[:, 0]))
            ch.do(act.activation(beta_g[:, :, :], sums[:, 0], ACT.Exp))
            act.activation(tail[:, :, :], sums[:, 1], ACT.Exp).then_inc(s_prep_a, 1)

            with act.Fori(0, HEADS // 2) as i:
                for n, j in enumerate((1, 0, 2)):
                    for par, d in enumerate(dn_heads):
                        act.wait_ge(s_conv, count(i, 3, n, par))
                        act.activation(d.xin[:, j, PAD:PAD + SEQ], d.cv[:, j, :], ACT.Sigmoid).then_inc(s_sig, 1)
                act.wait_ge(s_yb, i * 32)
                for n, j in enumerate((1, 0)):
                    for par, d in enumerate(dn_heads):
                        act.wait_ge(s_silu, count(i, 3, n, par))
                        act.activation(d.sq[:, j, :], d.cv[:, j, :], ACT.Square).then_inc(s_sq, 1)
                for n, j in enumerate((1, 0)):
                    for par, d in enumerate(dn_heads):
                        act.wait_ge(s_ss, count(i, 2, n, par))
                        act.activation(d.sq[:, j, :], (d.sb, d.tb)[j][:, :], ACT.Sqrt, bias=eps[:, :]).then_inc(s_nroot, 1)
                for par, d in enumerate(dn_heads):
                    act.wait_ge(s_gbc, count(i, 1, 0, par))
                    act.activation(d.e_g, d.xb[:, :], ACT.Exp).then_inc(s_eg, 1)
                for par, d in enumerate(dn_heads):
                    act.wait_ge(s_darg, count(i, 1, 0, par))
                    act.activation(d.dec, d.dec, ACT.Exp).then_inc(s_dec, 1)
                for par, d in enumerate(dn_heads):
                    act.wait_ge(s_inv1, count(i, 1, 0, par))
                    act.copy(d.inv, d.sb[:, :]).then_inc(s_inv1_out, 1)
                for n in range(NL):
                    for par, d in enumerate(dn_heads):
                        act.wait_ge(s_xm, count(i, NL, n, par))
                        if n == 0:
                            act.wait_ge(s_qkt, count(i, 1, 0, par))
                        act.copy(d.x_sb, d.xb[:, :]).then_inc(s_xc, 1)
                for par, d in enumerate(dn_heads):
                    act.wait_ge(s_uw, count(i, 1, 0, par))
                    act.copy(d.u_sol, d.tb[:, :]).then_inc(s_u, 1)
                act.wait_ge(s_dn_z, i * 32 + 32)
                for par, d in enumerate(dn_heads):
                    act.activation(d.z_sig, d.z_in, ACT.Sigmoid).then_inc(s_zsig, 1)
                for par, d in enumerate(dn_heads):
                    act.wait_ge(s_sd, count(i, NC, NC - 1, par))
                    act.activation(d.n_t, d.tb[:, :], ACT.Square).then_inc(s_osq, 1)
                for par, d in enumerate(dn_heads):
                    act.wait_ge(s_oms, count(i, 1, 0, par))
                    act.activation(d.o_ms, d.o_ms, ACT.Sqrt, scale=1.0 / HD, bias=eps[:, :]).then_inc(s_oroot, 1)
                for par, d in enumerate(dn_heads):
                    act.wait_ge(s_ot, count(i, 1, 0, par))
                    act.copy(d.o_out, d.xb[:, :]).then_inc(s_ot_out, 1)
            with act.Fori(0, HEADS) as h:
                for m in range(NT):
                    act.wait_ge(s_nmax, h * NT + (m + 1))
                    act.wait_ge(s_pt, h)
                    act.activation(prob[:, m, 0:(m + 1) * P], ps[m][:, 0:(m + 1) * P], ACT.Exp, scale=SCALE,
                                   bias=at_max[:, m:m + 1], accum_out=at_sum[:, m:m + 1]).then_inc(s_exp, 1)
                act.wait_ge(s_pt, h + 1)
                for k in range(NT):
                    act.copy(prob_t[:, k, k * P:SEQ], ps[4 + k][:, k * P:SEQ]).then_inc(s_pt_out, 1)
                act.wait_ge(s_av, h + 3)
                act.wait_ge(s_ya, h * 16)
                act.copy(at_o, ps[0][:, :]).then_inc(s_av_out, 1)

            def sigmoid_row(c, b):
                act.wait_ge(s_gate[b % 2], (c * 2 + b // 2) * 32 + 32)
                g = gate_in[:, (b % 2) * 2:(b % 2) * 2 + 2, :]
                act.activation(g, g, ACT.Sigmoid).then_inc(s_gsig, 1)

            act.wait_ge(s_yl, 32)
            for q in range(4):
                act.copy(yh[:, 4 * q:4 * q + 4, :], area_2[:, 4 * q:4 * q + 4, :]).then_inc(s_yh, 1)
            with act.Fori(0, 4) as c:
                for s in range(1, 5):
                    act_split(s % 4, (c + (N_ADA1 + N_IN + s // 4)) * 16 + 16, (c + N_IN) * 4 + (s + 3))
                    if s <= 2:
                        sigmoid_row(c, s - 1)
                for b in (2, 3):
                    sigmoid_row(c, b)
            act.wait_ge(s_used, 4 + 4 * (N_IN + 4))
            act.wait_ge(s_merged, 4 + 16)
            for q in range(4):
                act.copy(yh[:, 4 * q:4 * q + 4, :], merged[:, 4 * q:4 * q + 4, :]).then_inc(s_yh, 1)

            def project_out(c, last):
                for s in range(1, 4 if last else 5):
                    act_split(s % 4, (c + (N_ADA1 + N_IN + 4 + s // 4)) * 16 + 16, (c + (N_IN + 4)) * 4 + (s + 3))
                for b in range(2):
                    act.wait_ge(s_bank, (c + (N_IN + 4)) * 3 + (b + 1))
                    act.copy(y_nat[:, b, bass.ds(c * COLS, COLS)], ps[b][:, :]).then_inc(s_ev_a, 1)

            with act.Fori(0, 3) as c:
                project_out(c, False)
            project_out(3, True)
            act.wait_ge(s_ev_a, 2 + 2 * (N_IN + 4))
            act.wait_ge(s_ev_v, 2 + 2 * (N_IN + 4))
            junk = stage[:, :, :].rearrange("p a b -> p (a b)")
            for m in range(NT):
                ch.link(act.activation(junk, y_nat[:, m, :], ACT.Square, accum_out=ss2[:, 0, m:m + 1]))
            act.activation(ss2[:, 0, :], ss2[:, 0, :], ACT.Sqrt, scale=1.0 / D, bias=eps[:, :]).then_inc(s_rooty, 1)
            for m in range(NT):
                act.wait_ge(s_x1, m + 1)
                ch.link(act.activation(junk, y_nat[:, m, :], ACT.Square, accum_out=ss2[:, 1, m:m + 1]))
            act.activation(ss2[:, 1, :], ss2[:, 1, :], ACT.Sqrt, scale=1.0 / D, bias=eps[:, :]).then_inc(s_root1, 1)
            for t in range(ND):
                act.wait_ge(s_u2t, t + 1)
                act.copy(u2_t[:, t, :], ps[t % 4][:, :]).then_inc(s_u2t_out, 1)
            act.wait_ge(s_route_v, 1)
            act.activation(tmp4, tmp4, ACT.Exp).then_inc(s_route_a, 1)
            act.wait_ge(s_route_v, 2)
            act.activation(r1[:, 4, :], r1[:, 4, :], ACT.Exp).then_inc(s_route_a, 1)

            def expert_hi(j, x):
                act.wait_ge(s_mslot[x % 12], j * 16 + (mslot_base[x % 12] + 16 * (x // 12) + 16))
                act.wait_ge(s_mused, j * 12 + (x + 9))
                act.copy(m_hi[x % 4], m_raw[x % 12]).then_inc(s_mhi, 1)

            def rows_hi(n):
                for q in range(4):
                    act.wait_ge(s_xt, n + (q + 1))
                    act.copy(xe_hi[:, 4 * q:4 * q + 4, :].rearrange("p a b -> p (a b)"), ps[2 + q % 2][:, :]).then_inc(s_xehi, 1)

            act.wait_ge(s_ysplit, 8)
            for x in range(3):
                expert_hi(0, x)
            act.wait_ge(s_route_v, 6)
            n_blocks = act.value_load(plan[0:1, MAX_OVER:MAX_OVER + 1], min_val=EXPERTS, max_val=NB)
            rows_hi(0)
            with act.Fori(0, n_blocks) as j:
                for x in range(3, 8):
                    expert_hi(j, x)
                act.wait_ge(s_mused, j * 12 + 16)
                act.activation(h_sig, ps[0][:, :], ACT.Sigmoid).then_inc(s_hsig, 1)
                for x in range(8, 11):
                    expert_hi(j, x)
                rows_hi(j * 4 + 4)
                act.wait_ge(s_ht, j + 1)
                act.copy(ht_hi.rearrange("p a b -> p (a b)"), ps[0][:, :]).then_inc(s_hthi, 1)
                for x in range(11, 15):
                    expert_hi(j, x)
                act.wait_ge(s_ysc, j * 16)
                for b in range(2):
                    act.wait_ge(s_ybank, j * 3 + (b + 1))
                    act.copy(y_e[:, b * COLS:(b + 1) * COLS], ps[4 + b][:, :]).then_inc(s_ye_a, 1)
            for m in range(NT):
                act.wait_ge(s_f_y, m + 1)
                ch.link(act.activation(f_sq, f_y[m % 2][0], ACT.Square, accum_out=ss_f[:, m:m + 1]))
                act.activation(ss_f[:, m:m + 1], ss_f[:, m:m + 1], ACT.Sqrt, scale=1.0 / D, bias=eps[:, :]).then_inc(s_f_ss, 1)

        @block.vector
        def _(dve):
            ch = Chain(dve, s_dve)
            dve.sem_inc(s_ev_v, 2)
            dve.sem_inc(s_ada1_used, 4)
            dve.sem_inc(s_ada_used, 4)
            ch.do(dve.memset(half_pi[:, :], float(np.pi / 2)))
            ch.do(dve.memset(eps[:, :], EPS))
            dve.wait_ge(s_const, 16 * 8)
            ch.link(dve.tensor_copy(ang[:, 0, :], pos_i[:, :]))
            ch.link(dve.tensor_scalar(ang[:, 0, :], ang[:, 0, :], small[0:ROPE, 33:34], None, ALU.mult))
            ch.link(dve.tensor_scalar(ang[:, 1, :], ang[:, 0, :], float(1 / (2 * np.pi)), None, ALU.mult))
            ch.link(dve.tensor_scalar(ang[:, 1, :], ang[:, 1, :], ROUND, None, ALU.add))
            ch.link(dve.tensor_scalar(ang[:, 1, :], ang[:, 1, :], -ROUND, None, ALU.add))
            for part in (TWO_PI_1, TWO_PI_2, TWO_PI_3):
                ch.link(dve.scalar_tensor_tensor(ang[:, 0, :], ang[:, 1, :], -part, ang[:, 0, :], ALU.mult, ALU.add))
            ch.link(dve.tensor_scalar(ang[:, 2, :], ang[:, 0, :], -PI_BELOW, PI_BELOW, ALU.max, ALU.min))
            ch.link(dve.tensor_scalar(ang[:, 1, :], ang[:, 2, :], -1.0, None, ALU.mult))
            dve.tensor_tensor(ang[:, 3, :], ang[:, 1, :], ang[:, 2, :], ALU.max).then_inc(s_prep_v, 1)
            dve.wait_ge(s_prep_a, 1)
            ch.link(dve.tensor_tensor(cond[:, :], cond_raw[:, :], cond_sig[:, :], ALU.mult))

            def accumulate(ring, s, par, slot_done, used):
                for t in range(4):
                    w = ring[s][:, t * COLS:(t + 1) * COLS]
                    k = 4 * s + t
                    if k == 0:
                        ins = dve.tensor_scalar(acc[:, par, :], w, cond[:, 0:1], None, ALU.mult)
                    else:
                        ins = dve.scalar_tensor_tensor(acc[:, par, :], w, cond[:, k:k + 1], acc[:, par, :], ALU.mult, ALU.add)
                    if t < 3:
                        ch.link(ins)
                    else:
                        ins.then_inc(used, 1)
                        dve.wait_ge(used, slot_done)

            with ch.loop(N_ADA1 // 2, 24) as i:
                for par in range(2):
                    for s in range(4):
                        dve.wait_ge(s_slot[s], (i * 2 + par) * 16 + 16)
                        accumulate([r[:, :] for r in raw], s, par, (i * 2 + par) * 4 + (s + 5), s_ada1_used)
                    dve.sem_inc(s_acc, 1)
                    dve.wait_ge(s_mod, i * 2 + par)
            dve.wait_ge(s_prep_a, 5)
            ch.link(dve.tensor_tensor(mod_col[:, 0:2 * ND], mod_col[:, 0:2 * ND], b_col[:, 0:2 * ND], ALU.add))
            dve.scalar_tensor_tensor(a_col[:, 0, :], mod_col[:, ND:2 * ND], 1.0, g_pre[:, 0, :], ALU.add, ALU.mult).then_inc(s_prep_v, 1)
            dve.wait_ge(s_prep_a, 4)
            ch.link(dve.reciprocal(rstd[:, :], rstd[:, :]))
            for m in range(NT):
                dve.tensor_scalar(x_all[:, m, :], x_all[:, m, :], rstd[:, m:m + 1], None, ALU.mult).then_inc(s_xn, 1)
            for t in range(ND):
                dve.wait_ge(s_uhi, t + 1)
                dve.tensor_tensor(u_lo[:, t, :], u_tmp[:, t % 2, :], u_hi[:, t, :].bitcast(F32), ALU.subtract).then_inc(s_ulo, 1)
            dve.wait_ge(s_ba_split, 1)
            dve.tensor_tensor(ba_lo[:, :, :], w_ba[:, :, :], ba_hi[:, :, :].bitcast(F32), ALU.subtract).then_inc(s_ba_split, 1)
            dve.wait_ge(s_ulo, ND)

            def dve_split(s, ready):
                dve.wait_ge(s_hi, ready)
                dve.tensor_tensor(raw_r[s][:, :], raw[s][:, :], hi[s % 2][:, :].bitcast(F32),
                                  ALU.subtract).then_inc(s_lo, 1)

            dve_split(0, 1)
            done = ada_done = 0
            for col0, row0, n, natural, ada0 in PARTS:
                with ch.loop(n, 12 if ada0 is not None else 0) as c:
                    for s in range(4):
                        dve_split((s + 1) % 4, (c + done) * 4 + (s + 2))
                        if ada0 is not None:
                            if s == 0:
                                dve.wait_ge(s_mod, c + (N_ADA1 + ada_done))
                            dve.wait_ge(s_ada_slot[s], (c + ada_done) * 16 + 16)
                            accumulate(ada_ring, s, 0, (c + ada_done) * 4 + (s + 5), s_ada_used)
                    if ada0 is not None:
                        dve.sem_inc(s_acc, 1)
                    for b in range(2, 4):
                        if b == 2:
                            dve.wait_ge(s_bank, (c + done) * 3 + 3)
                        else:
                            dve.wait_ge(s_used, (c + done) * 4 + 8)
                        dve.wait_ge(s_stored[b], (c + done) * 16)
                        dve.tensor_copy(stage[:, b, :], ps[b][:, :]).then_inc(s_ev_v, 1)
                done += n
                if ada0 is not None:
                    ada_done += n

            dve.wait_ge(s_rows, 16 * 3)
            dve.wait_ge(s_prep_a, 6)
            ch.link(dve.tensor_tensor(dec_in[:, 0, :, :], ba[:, :, HEADS:2 * HEADS],
                                      dtb_row[:, :].rearrange("p (a h) -> p a h", a=1).broadcast_to([P, NT, HEADS]), ALU.add))
            ch.link(dve.tensor_scalar(dec_in[:, 1, :, :], dec_in[:, 0, :, :], -1.0, None, ALU.mult))
            dve.tensor_tensor(dec_in[:, 2, :, :], dec_in[:, 0, :, :], dec_in[:, 1, :, :], ALU.min).then_inc(s_prep_v, 1)
            dve.wait_ge(s_prep_a, 8)
            ch.link(dve.scalar_tensor_tensor(dec_in[:, 3, :, :], dec_in[:, 0, :, :], 0.0, dec_in[:, 2, :, :], ALU.max, ALU.add))
            ch.link(dve.tensor_scalar(dec_in[:, 3, :, :], dec_in[:, 3, :, :], -1.0, None, ALU.mult))
            dve.tensor_tensor(g_nat[:, :, :], dec_in[:, 3, :, :],
                              alog_row[:, :].rearrange("p (a h) -> p a h", a=1).broadcast_to([P, NT, HEADS]), ALU.mult).then_inc(s_prep_v, 1)
            dve.wait_ge(s_prep_a, 9)
            ch.link(dve.tensor_tensor(beta_g[:, :, :], beta_g[:, :, :], beta[:, :, :], ALU.mult))

            with ch.loop(HEADS // 2, 54) as i:
                dve.wait_ge(s_dn_in, i * 32 + 32)
                for j in (1, 0, 2):
                    for k in range(CONV):
                        for par, d in enumerate(dn_heads):
                            w = conv_col[:, bass.ds(i * 2 + (k * 3 * HEADS + j * HEADS + par), 1)]
                            src = d.xin[:, j, k:k + SEQ]
                            if k == 0:
                                ch.do(dve.tensor_scalar(d.cv[:, j, :], src, w, None, ALU.mult))
                            else:
                                ch.sync(but=0 if par and k == CONV - 1 else 1)
                                ins = dve.scalar_tensor_tensor(d.cv[:, j, :], src, w, d.cv[:, j, :], ALU.mult, ALU.add)
                                if k < CONV - 1:
                                    ch.do(ins)
                                else:
                                    ins.then_inc(s_conv, 1)
                for n, j in enumerate((1, 0, 2)):
                    for par, d in enumerate(dn_heads):
                        dve.wait_ge(s_sig, count(i, 3, n, par))
                        dve.tensor_tensor(d.cv[:, j, :], d.cv[:, j, :], d.xin[:, j, PAD:PAD + SEQ], ALU.mult).then_inc(s_silu, 1)
                for par, d in enumerate(dn_heads):
                    ch.do(dve.tensor_copy(tiles(d.inv), column(g_nat, i * 2 + par)))
                    dve.tensor_copy(tiles(d.inv_t), column(beta, i * 2 + par)).then_inc(s_gb, 1)
                for n, j in enumerate((1, 0)):
                    for par, d in enumerate(dn_heads):
                        dve.wait_ge(s_nroot, count(i, 2, n, par))
                        ch.do(dve.reciprocal(d.sq[:, j, :], d.sq[:, j, :]))
                    for par, d in enumerate(dn_heads):
                        ch.sync(but=1 - par)
                        dve.scalar_tensor_tensor(d.cv[:, j, :], d.cv[:, j, :], 1.0 if j else HD ** -0.5, d.sq[:, j, :],
                                                 ALU.mult, ALU.mult).then_inc(s_unit, 1)
                for par, d in enumerate(dn_heads):
                    dve.wait_ge(s_bbc, count(i, 1, 0, par))
                    dve.wait_ge(s_unit, count(i, 2, 0, par))
                    dve.tensor_tensor(d.kb, d.cv[:, 1, :], d.tb[:, :], ALU.mult).then_inc(s_kb, 1)
                for par, d in enumerate(dn_heads):
                    dve.wait_ge(s_eg, count(i, 1, 0, par))
                    for t in range(NT):
                        c = slice(t * P, (t + 1) * P)
                        ins = dve.scalar_tensor_tensor(d.dec[:, c], d.xb[:, c], gcum[:, t, bass.ds(i * 2 + par, 1)], planes[:, C_DEC, :],
                                                       ALU.subtract, ALU.add)
                        ins.then_inc(s_darg, 1) if t == NT - 1 else ch.do(ins)
                for par, d in enumerate(dn_heads):
                    dve.wait_ge(s_unit, count(i, 2, 1, par))
                    ch.do(dve.tensor_tensor(d.q_dec, d.cv[:, 0, :], d.e_g, ALU.mult))
                    ch.do(dve.tensor_copy(d.g_last, d.e_g[:, CHUNK - 1::CHUNK]))
                for par, d in enumerate(dn_heads):
                    dve.wait_ge(s_dec, count(i, 1, 0, par))
                    dve.wait_ge(s_gram, count(i, 2, 0, par))
                    dve.tensor_tensor(d.n_t, d.sb[:, :], d.dec, ALU.mult).then_inc(s_nt, 1)
                for par, d in enumerate(dn_heads):
                    dve.wait_ge(s_gram, count(i, 2, 1, par))
                    dve.tensor_tensor(d.qk_t, d.tb[:, :], d.dec, ALU.mult).then_inc(s_qkt, 1)
                for par, d in enumerate(dn_heads):
                    dve.wait_ge(s_nt, count(i, 1, 0, par))
                    dve.wait_ge(s_gbc, count(i, 1, 0, par))
                    dve.wait_ge(s_bbc, count(i, 1, 0, par))
                    ch.do(dve.tensor_tensor(tiles(d.inv_t), tiles(d.n_t), plane(C_LEV), ALU.mult))
                for par, d in enumerate(dn_heads):
                    ch.sync(but=1 - par)
                    dve.tensor_tensor(tiles(d.inv_t), plane(C_ID), tiles(d.inv_t), ALU.subtract).then_inc(s_first, 1)
                for par, d in enumerate(dn_heads):
                    dve.wait_ge(s_knat, count(i, 1, 0, par))
                    ch.do(dve.tensor_tensor(d.k_bg, tiles(d.xb[:, :]), column(beta_g, i * 2 + par), ALU.mult))
                    dve.tensor_tensor(d.k_tail, tiles(d.xb[:, :]), column(tail, i * 2 + par), ALU.mult).then_inc(s_kfac, 1)
                for par, d in enumerate(dn_heads):
                    dve.wait_ge(s_vnat, count(i, 1, 0, par))
                    dve.tensor_tensor(d.v_b, tiles(d.tb[:, :]), column(beta, i * 2 + par), ALU.mult).then_inc(s_vb, 1)
                for n in range(NL):
                    for par, d in enumerate(dn_heads):
                        dve.wait_ge(s_corr, count(i, NL, n, par))
                        dve.wait_ge(s_inv if n else s_first, count(i, NL if n else 1, n - 1 if n else 0, par))
                        ins = dve.tensor_tensor(d.inv_t, d.inv_t, d.tb[:, :], ALU.subtract)
                        if n < NL - 1:
                            ch.do(ins)
                            ins = dve.tensor_tensor(d.inv, d.inv, d.sb[:, :], ALU.subtract)
                        ins.then_inc(s_inv, 1)
                for par, d in enumerate(dn_heads):
                    dve.wait_ge(s_uw, count(i, 1, 0, par))
                    dve.tensor_copy(d.w_t, d.sb[:, :]).then_inc(s_w, 1)
                for c in range(NC):
                    r, t = slice((c % 2) * CHUNK, (c % 2 + 1) * CHUNK), c // 2
                    if c:
                        for par, d in enumerate(dn_heads):
                            dve.wait_ge(s_ws, count(i, NC - 1, c - 1, par))
                            if c == 1:
                                dve.wait_ge(s_u, count(i, 1, 0, par))
                            dve.tensor_tensor(d.v_new[r, :], d.u_sol[r, t * HD:(t + 1) * HD], d.xb[r, 0:HD], ALU.subtract).then_inc(s_vn, 1)
                    for par, d in enumerate(dn_heads):
                        dve.wait_ge(s_sd, count(i, NC, c, par))
                        if c == 0:
                            dve.tensor_copy(d.state, d.sb[:, 0:HD]).then_inc(s_state, 1)
                        else:
                            dve.wait_ge(s_state, count(i, NC, c - 1, par))
                            dve.scalar_tensor_tensor(d.state, d.state, d.g_last[:, c:c + 1], d.sb[:, 0:HD],
                                                     ALU.mult, ALU.add).then_inc(s_state, 1)
                for par, d in enumerate(dn_heads):
                    dve.wait_ge(s_zsig, count(i, 1, 0, par))
                    ch.do(dve.tensor_tensor(d.z_sig, d.z_sig, d.z_in, ALU.mult))
                for par, d in enumerate(dn_heads):
                    ch.sync(but=1)
                    ch.do(dve.tensor_tensor(d.z_sig, d.z_sig,
                                            og_row[:, :].rearrange("p (a c) -> p a c", a=1).broadcast_to([P, NT, HD]), ALU.mult))
                for par, d in enumerate(dn_heads):
                    dve.wait_ge(s_osq, count(i, 1, 0, par))
                    dve.tensor_reduce(d.o_ms, tiles(d.n_t), AX, ALU.add).then_inc(s_oms, 1)
                for par, d in enumerate(dn_heads):
                    dve.wait_ge(s_oroot, count(i, 1, 0, par))
                    ch.do(dve.reciprocal(d.o_ms, d.o_ms))
                for par, d in enumerate(dn_heads):
                    ch.sync(but=1)
                    ch.do(dve.tensor_tensor(tiles(d.o_out), tiles(d.tb[:, :]), d.o_ms.rearrange("p (t a) -> p t a", a=1).broadcast_to([P, NT, HD]), ALU.mult))
                for par, d in enumerate(dn_heads):
                    ch.sync(but=1 - par)
                    dve.tensor_tensor(tiles(d.o_out), tiles(d.o_out), d.z_sig, ALU.mult).then_inc(s_on, 1)

            with ch.loop(HEADS // 2, 2 * 16) as i:
                for par in range(2):
                    h = i * 2 + par
                    for n, x in enumerate((at_q[par], at_k[par])):
                        dve.wait_ge(s_rot, h * 2 + (n + 1))
                        ch.link(dve.tensor_tensor(rot[0:ROPE, :], ps[4 + n][0:ROPE, :], sin_t[:, :], ALU.mult))
                        if n == 0:
                            dve.wait_ge(s_rot, h * 2 + 2)
                        ch.link(dve.tensor_tensor(x[0:ROPE, :], x[0:ROPE, :], cos_t[:, :], ALU.mult))
                        dve.tensor_tensor(x[0:ROPE, :], x[0:ROPE, :], rot[0:ROPE, :], ALU.add).then_inc(s_roped, 1)
                        dve.wait_ge(s_roped, h * 2 + (n + 1))
                    for m in range(NT):
                        dve.wait_ge(s_sc, h * NT + (m + 1))
                        diag = ps[m][:, m * P:(m + 1) * P]
                        ch.link(dve.tensor_tensor(diag, diag, planes[:, C_CAUSAL, :], ALU.add))
                        ch.link(dve.reduce_max(at_raw[:, m:m + 1], ps[m][:, 0:(m + 1) * P], AX))
                        dve.tensor_scalar(at_max[:, m:m + 1], at_raw[:, m:m + 1], -SCALE, None, ALU.mult).then_inc(s_nmax, 1)
                    for m in range(NT):
                        dve.wait_ge(s_exp, h * NT + (m + 1))
                        ch.link(dve.reciprocal(at_sum[:, m:m + 1], at_sum[:, m:m + 1]))
                        dve.tensor_scalar(prob[:, m, 0:(m + 1) * P], prob[:, m, 0:(m + 1) * P], at_sum[:, m:m + 1], None,
                                          ALU.mult).then_inc(s_prob, 1)

            for q in range(4):
                dve.wait_ge(s_yh, q + 1)
                dve.tensor_tensor(yl[:, 4 * q:4 * q + 4, :], area_2[:, 4 * q:4 * q + 4, :],
                                  yh[:, 4 * q:4 * q + 4, :].bitcast(F32), ALU.subtract).then_inc(s_ysplit, 1)
            dve.sem_inc(s_merged, 4)
            with ch.loop(4, 8) as c:
                for s in range(4):
                    dve_split((s + 1) % 4, (c + N_IN) * 4 + (s + 2))
                for b in range(4):
                    g = gate_in[:, (b % 2) * 2, :], gate_in[:, (b % 2) * 2 + 1, :]
                    dve.wait_ge(s_gsig, c * 4 + (b + 1))
                    if b < 3:
                        dve.wait_ge(s_bank, (c + N_IN) * 3 + (b + 1))
                    else:
                        dve.wait_ge(s_used, (c + N_IN) * 4 + 8)
                    ch.do(dve.tensor_tensor(g[0], g[0], ps[b][:, :], ALU.mult))
                    ch.link(dve.tensor_tensor(g[1], g[1], ps[4 + b][:, :], ALU.mult))
                    dve.tensor_tensor(merged[:, bass.ds(c * 4 + b, 1), :].rearrange("p a n -> p (a n)"), g[0], g[1],
                                      ALU.add).then_inc(s_merged, 1)
            for q in range(4):
                dve.wait_ge(s_yh, q + 5)
                dve.tensor_tensor(yl[:, 4 * q:4 * q + 4, :], merged[:, 4 * q:4 * q + 4, :],
                                  yh[:, 4 * q:4 * q + 4, :].bitcast(F32), ALU.subtract).then_inc(s_ysplit, 1)

            def project_out(c, last):
                for s in range(3 if last else 4):
                    dve_split((s + 1) % 4, (c + (N_IN + 4)) * 4 + (s + 2))
                for b in range(2, 4):
                    if b == 2:
                        dve.wait_ge(s_bank, (c + (N_IN + 4)) * 3 + 3)
                    else:
                        dve.wait_ge(s_used, (c + (N_IN + 4)) * 4 + 8)
                    dve.tensor_copy(y_nat[:, b, bass.ds(c * COLS, COLS)], ps[b][:, :]).then_inc(s_ev_v, 1)

            with dve.Fori(0, 3) as c:
                project_out(c, False)
            project_out(3, True)

            dve.wait_ge(s_mr, 16 * 5)
            ch.link(dve.tensor_tensor(mr[:, :, :], mr[:, :, :], br[:, :, :], ALU.add))
            ch.do(dve.tensor_tensor(mr[:, 0, :], mr[:, 0, :], gr[:, 0, :], ALU.mult))
            ch.do(dve.scalar_tensor_tensor(mr[:, 2, :], mr[:, 2, :], 1.0, gr[:, 1, :], ALU.add, ALU.mult))
            dve.tensor_tensor(mr[:, 3, :], mr[:, 3, :], gr[:, 2, :], ALU.mult).then_inc(s_res, 1)

            dve.wait_ge(s_rooty, 1)
            ch.link(dve.reciprocal(ss2[:, 0, :], ss2[:, 0, :]))
            dve.wait_ge(s_rowb, 16 * 7)
            for m in range(NT):
                ch.link(dve.scalar_tensor_tensor(y_nat[:, m, :], y_nat[:, m, :], ss2[:, 0, m:m + 1], row_g1, ALU.mult, ALU.mult))
                dve.wait_ge(s_xin2, (m + 1) * 16)
                dve.tensor_tensor(y_nat[:, m, :], y_nat[:, m, :], x_in, ALU.add).then_inc(s_x1, 1)
            dve.wait_ge(s_root1, 1)
            ch.link(dve.reciprocal(ss2[:, 1, :], ss2[:, 1, :]))
            for m in range(NT):
                dve.wait_ge(s_x1_out, 16 * NT)
                ch.link(dve.scalar_tensor_tensor(y_nat[:, m, :], y_nat[:, m, :], ss2[:, 1, m:m + 1], row_a2, ALU.mult, ALU.mult))
                dve.tensor_tensor(y_nat[:, m, :], y_nat[:, m, :], row_s2, ALU.add).then_inc(s_u2, 1)

            def over_tiles(x, n):
                return x.rearrange("p (t a) -> p t a", a=1).broadcast_to([P, NT, n])

            def numbers(n):
                return small[:, 0:n].rearrange("p (a e) -> p a e", a=1).broadcast_to([P, NT, n])

            def first_of_max(x, best, one_hot, scratch, index, n):
                ch.link(dve.tensor_reduce(best, x, AX, ALU.max))
                ch.link(dve.tensor_tensor(scratch, x, over_tiles(best, n), ALU.is_equal))
                ch.link(dve.tensor_scalar(scratch, scratch, -1000.0, 1000.0, ALU.mult, ALU.add))
                ch.link(dve.tensor_tensor(scratch, scratch, numbers(n), ALU.add))
                ch.link(dve.tensor_reduce(index, scratch, AX, ALU.min))
                ch.link(dve.tensor_tensor(one_hot, numbers(n), over_tiles(index, n), ALU.is_equal))

            def look_up(dst, values, one_hot, n):
                ch.link(dve.tensor_tensor(tmp32, values, one_hot, ALU.mult))
                ch.link(dve.tensor_reduce(dst, tmp32, AX, ALU.add))

            dve.wait_ge(s_logit, 1)
            ch.link(dve.tensor_tensor(logit, ps[4][:, 0:NT * NR].rearrange("p (t n) -> p t n", t=NT),
                                      b_r[:, :].rearrange("p (a n) -> p a n", a=1).broadcast_to([P, NT, NR]), ALU.add))
            g_log = logit[:, :, 0:GROUPS]
            first_of_max(g_log, r1[:, 0, :], oh_g, tmp4, r1[:, 1, :], GROUPS)
            dve.tensor_tensor(tmp4, g_log, over_tiles(r1[:, 0, :], GROUPS), ALU.subtract).then_inc(s_route_v, 1)
            ch.link(dve.tensor_scalar(oh_g, oh_g, -NEG, NEG, ALU.mult, ALU.add))
            for g in range(GROUPS):
                ch.do(dve.tensor_tensor(e_log[:, :, g * PER_GROUP:(g + 1) * PER_GROUP],
                                        logit[:, :, GROUPS + g * PER_GROUP:GROUPS + (g + 1) * PER_GROUP],
                                        oh_g[:, :, g:g + 1].broadcast_to([P, NT, PER_GROUP]), ALU.add))
            ch.sync()
            first_of_max(e_log, r1[:, 2, :], oh1, tmp32, r1[:, 5, :], EXPERTS)
            ch.link(dve.tensor_scalar(tmp32, oh1, 2 * NEG, None, ALU.mult))
            ch.link(dve.tensor_tensor(e_log, e_log, tmp32, ALU.add))
            first_of_max(e_log, r1[:, 3, :], oh2, tmp32, r1[:, 6, :], EXPERTS)
            dve.tensor_tensor(r1[:, 4, :], r1[:, 3, :], r1[:, 2, :], ALU.subtract).then_inc(s_route_v, 1)
            dve.tensor_tensor(both, oh1, oh2, ALU.add).then_inc(s_route_v, 1)
            dve.wait_ge(s_route_a, 1)
            ch.link(dve.tensor_reduce(r1[:, 7, :], tmp4, AX, ALU.add))
            dve.wait_ge(s_route_a, 2)
            ch.link(dve.tensor_scalar(r1[:, 8, :], r1[:, 4, :], 1.0, None, ALU.add))
            ch.link(dve.tensor_tensor(r1[:, 8, :], r1[:, 8, :], r1[:, 7, :], ALU.mult))
            ch.link(dve.reciprocal(wts[:, 0, :], r1[:, 8, :]))
            ch.link(dve.tensor_tensor(wts[:, 1, :], wts[:, 0, :], r1[:, 4, :], ALU.mult))
            dve.wait_ge(s_route_pe, 1)
            ch.do(dve.tensor_copy(rank, ps[5][:, 0:NT * EXPERTS].rearrange("p (t e) -> p t e", t=NT)))
            ch.link(dve.tensor_copy(cnt[:, 0, :], ps[6][:, 0:EXPERTS]))
            ch.link(dve.tensor_scalar(cnt[:, 1, :], cnt[:, 0, :], float(ROWS), None, ALU.is_gt))
            for q in (2, 3):
                ch.link(dve.tensor_scalar(cnt[:, 2, :], cnt[:, 0, :], float(q * ROWS), None, ALU.is_gt))
                ins = dve.tensor_tensor(cnt[:, 1, :], cnt[:, 1, :], cnt[:, 2, :], ALU.add)
                ch.link(ins) if q == 2 else ins.then_inc(s_route_v, 1)
            dve.wait_ge(s_route_pe, 2)
            dve.tensor_copy(over_t[0:EXPERTS, :], ps[7][0:EXPERTS, 0:P]).then_inc(s_route_v, 1)
            dve.wait_ge(s_route_pe, 3)
            ch.link(dve.tensor_scalar(cnt[:, 2, :], ps[5][:, 256:256 + EXPERTS], float(EXPERTS), None, ALU.add))
            ch.link(dve.tensor_tensor(cnt[:, 3, :], cnt[:, 2, :], cnt[:, 1, :], ALU.add))
            ch.link(dve.tensor_tensor(tmp7, cnt[:, 3:4, :].broadcast_to([P, MAX_OVER, EXPERTS]),
                                      small[:, 40:40 + MAX_OVER].rearrange("p (n a) -> p n a", a=1).broadcast_to([P, MAX_OVER, EXPERTS]),
                                      ALU.is_le))
            ch.link(dve.tensor_reduce(plan_f[:, 0:MAX_OVER], tmp7, AX, ALU.add))
            ch.link(dve.tensor_scalar(plan_f[:, 0:MAX_OVER], plan_f[:, 0:MAX_OVER], float(EXPERTS - 1), None, ALU.min))
            ch.link(dve.tensor_copy(plan_f[:, MAX_OVER:MAX_OVER + 1], cnt[:, 3, EXPERTS - 1:EXPERTS]))
            ch.do(dve.tensor_copy(plan[:, :], plan_f[:, :]))
            ch.sync()
            dve.sem_inc(s_route_v, 1)
            base = cnt[:, 2:3, :].broadcast_to([P, NT, EXPERTS])
            for k, one_hot in enumerate((oh1, oh2)):
                look_up(r1[:, 9, :], rank, one_hot, EXPERTS)
                look_up(r1[:, 10, :], base, one_hot, EXPERTS)
                ch.link(dve.tensor_scalar(r1[:, 11, :], r1[:, 9, :], float(ROWS), None, ALU.is_ge))
                ch.link(dve.tensor_copy(r1[:, 12, :], r1[:, 11, :]))
                for q in (2, 3):
                    ch.link(dve.tensor_scalar(r1[:, 13, :], r1[:, 9, :], float(q * ROWS), None, ALU.is_ge))
                    ch.link(dve.tensor_tensor(r1[:, 12, :], r1[:, 12, :], r1[:, 13, :], ALU.add))
                ch.link(dve.tensor_tensor(r1[:, 10, :], r1[:, 10, :], r1[:, 12, :], ALU.add))
                ch.link(dve.scalar_tensor_tensor(r1[:, 10, :], r1[:, 10, :], -1.0, r1[:, 5 + k, :], ALU.add, ALU.subtract))
                ch.link(dve.tensor_tensor(r1[:, 10, :], r1[:, 10, :], r1[:, 11, :], ALU.mult))
                ch.link(dve.tensor_tensor(r1[:, 10, :], r1[:, 10, :], r1[:, 5 + k, :], ALU.add))
                ch.link(dve.scalar_tensor_tensor(r1[:, 9, :], r1[:, 12, :], -float(ROWS), r1[:, 9, :], ALU.mult, ALU.add))
                ch.link(dve.scalar_tensor_tensor(place[:, k, :], r1[:, 9, :], float(NB + 1), r1[:, 10, :], ALU.mult, ALU.add))
                for m in range(NT):
                    ch.do(dve.tensor_scalar(r1[:, 14 + k, m:m + 1], small[:, 32:33], float(m * P + k * SEQ), None, ALU.add))
                ch.sync()
            dve.tensor_copy(place_i[:, :], place.rearrange("p k t -> p (k t)")).then_inc(s_route_v, 1)
            dve.tensor_copy(id_i[:, :], r1[:, 14:16, :].rearrange("p k t -> p (k t)")).then_inc(s_route_v, 1)
            dve.wait_ge(s_table, 32 + 16 * 2 * NT)
            ch.link(dve.tensor_copy(row_f[:, :], row_i[:, :]))
            ch.link(dve.tensor_scalar(tok_f[:, :], row_f[:, :], float(SEQ), -float(SEQ), ALU.is_ge, ALU.mult))
            ch.link(dve.tensor_tensor(tok_f[:, :], tok_f[:, :], row_f[:, :], ALU.add))
            dve.tensor_copy(tok_i[:, :], tok_f[:, :]).then_inc(s_route_v, 1)

            def expert_lo(j, x):
                dve.wait_ge(s_mhi, j * 12 + (x + 1))
                dve.tensor_tensor(m_raw_r[x % 12], m_raw[x % 12], m_hi[x % 4].bitcast(F32),
                                  ALU.subtract).then_inc(s_mlo, 1)

            def rows_lo(n):
                for q in range(4):
                    dve.wait_ge(s_xehi, n + (q + 1))
                    dve.tensor_tensor(xe_lo[:, 4 * q:4 * q + 4, :].rearrange("p a b -> p (a b)"), ps[2 + q % 2][:, :],
                                      xe_hi[:, 4 * q:4 * q + 4, :].bitcast(F32).rearrange("p a b -> p (a b)"),
                                      ALU.subtract).then_inc(s_xelo, 1)

            for x in range(3):
                expert_lo(0, x)
            n_blocks = dve.value_load(plan[0:1, MAX_OVER:MAX_OVER + 1], min_val=EXPERTS, max_val=NB)
            rows_lo(0)
            with ch.loop(n_blocks, 1) as j:
                for x in range(3, 11):
                    expert_lo(j, x)
                dve.wait_ge(s_hsig, j + 1)
                ch.link(dve.tensor_tensor(h_e, h_sig, ps[0][:, :], ALU.mult))
                dve.wait_ge(s_mused, j * 12 + 20)
                dve.tensor_tensor(h_e, h_e, ps[1][:, :], ALU.mult).then_inc(s_h, 1)
                rows_lo(j * 4 + 4)
                dve.wait_ge(s_hthi, j + 1)
                dve.tensor_tensor(ht_lo.rearrange("p a b -> p (a b)"), ps[0][:, :],
                                  ht_hi.bitcast(F32).rearrange("p a b -> p (a b)"), ALU.subtract).then_inc(s_htlo, 1)
                for x in range(11, 15):
                    expert_lo(j, x)
                dve.wait_ge(s_ysc, j * 16)
                for b in range(2, 4):
                    if b == 2:
                        dve.wait_ge(s_ybank, j * 3 + 3)
                    else:
                        dve.wait_ge(s_mused, j * 12 + 24)
                    dve.tensor_copy(y_e[:, b * COLS:(b + 1) * COLS], ps[4 + b][:, :]).then_inc(s_ye_v, 1)

            dve.wait_ge(s_g2, 16)
            for m in range(NT):
                dve.wait_ge(s_at_in[m % 2], HEADS // 2 * 48 + (m // 2 + 1) * 48)
                y0, y1, x1 = f_y[m % 2][0], f_y[m % 2][1], f_x[m % 2]
                ch.link(dve.tensor_scalar(y0, y0, wts[:, 0, m:m + 1], None, ALU.mult))
                dve.scalar_tensor_tensor(y0, y1, wts[:, 1, m:m + 1], y0, ALU.mult, ALU.add).then_inc(s_f_y, 1)
                dve.wait_ge(s_f_ss, m + 1)
                ch.link(dve.reciprocal(ss_f[:, m:m + 1], ss_f[:, m:m + 1]))
                ch.link(dve.scalar_tensor_tensor(y0, y0, ss_f[:, m:m + 1], row_g2, ALU.mult, ALU.mult))
                dve.tensor_tensor(x1, x1, y0, ALU.add).then_inc(s_f_out, 1)


def kernel(**inputs):
    import numpy as _np
    import concourse.bacc as _bacc
    from concourse import mybir as _mybir
    from concourse.bass_utils import run_bass_kernel_spmd as _run

    nc = _bacc.Bacc("TRN2", target_bir_lowering=False, num_devices=1)
    planes, small = shape_constants()
    arrays, aps = {}, {}
    for name, x in {**inputs, "planes": planes, "small": small}.items():
        x = _np.ascontiguousarray(x)
        arrays[f"in_{name}_dram"] = x
        aps[name] = nc.dram_tensor(f"in_{name}_dram", x.shape, _mybir.dt.from_np(x.dtype), kind="ExternalInput").ap()
    out = nc.dram_tensor("out_dram", (1, SEQ, D), F32, kind="ExternalOutput").ap()

    def dram(name, shape, dt=F32):
        return nc.dram_tensor(f"{name}_dram", shape, dt).ap()

    build(nc, aps, out, dram)
    r = _run(nc, [arrays], core_ids=[0])
    return r.results[0]["out_dram"]
```

```python
from contextlib import ExitStack, contextmanager

import numpy as np

import concourse.bass as bass
from concourse import mybir

F32 = mybir.dt.float32
F32R = mybir.dt.float32r
I32 = mybir.dt.int32
ALU = mybir.AluOpType
ACT = mybir.ActivationFunctionType
AX = mybir.AxisListType.X

P = 128
SEQ = 512
D = 2048
ND = D // P
NT = SEQ // P
HD = 128
HEADS = 8
WIDTH = HEADS * HD
ROPE = HD // 4
HALF = ROPE // 2
ROPE_THETA = 500000.0
CHUNK = 64
CONV = 4
GROUPS, PER_GROUP = 4, 8
EXPERTS = GROUPS * PER_GROUP
FF = 512
NF = FF // P
ROWS = 128
MAX_OVER = (SEQ * 2) // (ROWS + 1)
COLS = 512
SLOT = 4 * COLS
EPS = 1e-6
NEG = -1.0e30
IN_QA, IN_KA, IN_VA, IN_DN, IN_Z = 0, WIDTH, 2 * WIDTH, 3 * WIDTH, 6 * WIDTH
IN_BETA = 7 * WIDTH
IN_GA = IN_BETA + 2 * HEADS
IN_GB = IN_GA + D
LEVELS = (1, 2, 4, 8, 16, 32)

TWO_PI_1 = 6.28125
TWO_PI_2 = float(np.float32(np.round((2 * np.pi - 6.28125) * 2.0 ** 20) / 2.0 ** 20))
TWO_PI_3 = float(np.float32(2 * np.pi - 6.28125 - TWO_PI_2))
ROUND = 1.5 * 2.0 ** 23
PI_BELOW = 3.1415925

(C_ID, C_ONES, C_CUM, C_TAIL, C_DEC, C_CAUSAL, C_RANK, C_ROT, C_LEV) = (0, 1, 2, 3, 4, 5, 6, 7, 8)
N_CONST = C_LEV + len(LEVELS)


def shape_constants():
    c = np.zeros((N_CONST, P, P), np.float32)
    k, i = np.meshgrid(np.arange(P), np.arange(P), indexing="ij")
    same = (k // CHUNK) == (i // CHUNK)
    c[C_ID] = np.eye(P)
    c[C_ONES] = 1.0
    c[C_CUM] = same & (k <= i)
    c[C_TAIL] = same & (k > i)
    c[C_DEC] = np.where(same & (i >= k), 0.0, NEG)
    c[C_CAUSAL] = np.where(i <= k, 0.0, NEG)
    c[C_RANK] = k < i
    for a in range(HALF):
        c[C_ROT, a + HALF, a] = -1.0
        c[C_ROT, a, a + HALF] = 1.0
    for n, s in enumerate(LEVELS):
        c[C_LEV + n] = (k // (2 * s) == i // (2 * s)) & (k % (2 * s) < s) & (i % (2 * s) >= s)
    planes = np.ascontiguousarray(c.transpose(1, 0, 2))
    small = np.zeros((P, 64), np.float32)
    small[:, 0:32] = np.arange(32)
    small[:, 32] = np.arange(P)
    f = np.power(np.float64(ROPE_THETA), -np.arange(HALF) * (2.0 / ROPE)).astype(np.float32)
    small[0:ROPE, 33] = np.concatenate([f, f])
    small[:, 40:40 + MAX_OVER] = EXPERTS + np.arange(MAX_OVER)
    return planes, small


class Chain:

    def __init__(self, eng, sem):
        self.eng, self.sem, self.base, self.off = eng, sem, 0, 0

    def do(self, ins):
        ins.then_inc(self.sem, 1)
        self.off += 1
        return ins

    def sync(self, but=0):
        self.eng.wait_ge(self.sem, self.base + (self.off - but))

    def link(self, ins):
        self.do(ins)
        self.sync()

    @contextmanager
    def loop(self, n, per):
        base, off = self.base, self.off
        with self.eng.Fori(0, n) as i:
            self.base, self.off = i * per + (base + off), 0
            yield i
            assert self.off == per, f"this loop signals {self.off} times a turn"
        self.base, self.off = base, off + n * per


class Carve:

    def __init__(self, *areas):
        self.areas = [[x, 0] for x in areas]

    def take(self, shape):
        n = int(np.prod(shape[1:]))
        for area in self.areas:
            x, at = area
            if at + n <= x.shape[1]:
                area[1] += n
                part = x[:, at:at + n]
                if len(shape) == 3:
                    part = part.rearrange("p (a b) -> p a b", a=shape[1])
                return part
        raise ValueError("the areas are full")


def count(i, k, n, par):
    return i * (2 * k) + (2 * n + par + 1)


class DeltaHead:

    def __init__(self, mem, banks, xin, z_in):
        self.tb, self.sb, self.xb = banks
        self.xin = xin
        self.z_in = z_in
        self.cv = mem.take([P, 3, SEQ])
        self.kb = mem.take([P, SEQ])
        self.e_g = mem.take([P, SEQ])
        self.q_dec = mem.take([P, SEQ])
        self.dec = mem.take([P, SEQ])
        self.n_t = mem.take([P, SEQ])
        self.qk_t = mem.take([P, SEQ])
        self.k_bg = mem.take([P, NT, HD])
        self.k_tail = mem.take([P, NT, HD])
        self.v_b = mem.take([P, NT, HD])
        self.inv = mem.take([P, SEQ])
        self.inv_t = mem.take([P, SEQ])
        self.state = mem.take([P, HD])
        self.v_new = mem.take([P, HD])
        self.g_last = mem.take([P, SEQ // CHUNK])
        self.o_ms = mem.take([P, NT])
        self.sq = mem.take([P, 2, SEQ])
        self.w_t, self.u_sol, self.x_sb = self.e_g, self.kb, self.dec
        self.z_sig = self.k_bg
        self.c_lev = [self.cv[:, 1, :], self.cv[:, 2, :]]
        self.o_out = self.n_t


def build(nc, a, out, dram):
    ctx = ExitStack()
    with ctx:
        starts = {}

        def sb(name, shape, dt=F32):
            starts[name] = -(-nc.sbuf_base // 32) * 32
            return ctx.enter_context(nc.sbuf_tensor(name, shape, dt))

        def rounded(name, shape):
            return nc.alloc_sbuf_tensor_at(name + "_r", shape, F32R, offset=starts[name])

        def sem(name):
            return ctx.enter_context(nc.semaphore(name))

        proj_t = dram("proj_t", [18, NT, P, SEQ])
        proj_n = dram("proj_n", [NT, P, 4 * COLS])
        mod_rows = dram("mod_rows", [16, COLS])
        T_QA, T_KA, T_DN, T_GA, T_GB = 0, 2, 4, 10, 14

        planes = sb("planes", [P, N_CONST, P])
        small = sb("small", [P, 64])
        half_pi = sb("half_pi", [P, 1])
        eps = sb("eps", [P, 1])
        cond = sb("cond", [P, ND])
        g_pre = sb("g_pre", [P, 2, ND])
        b_col = sb("b_col", [P, 6 * ND])
        conv_col = sb("conv_col", [P, CONV * 3 * HEADS])
        mod_col = sb("mod_col", [P, 6 * ND])
        a_col = sb("a_col", [P, 2, ND])
        row_out = sb("row_out", [1, 2, COLS])
        cos_t = sb("cos_t", [ROPE, SEQ])
        sin_t = sb("sin_t", [ROPE, SEQ])
        ba = sb("ba", [P, NT, 2 * HEADS])
        raw = [sb(f"raw{i}", [P, SLOT]) for i in range(4)]
        raw_r = [rounded(f"raw{i}", [P, SLOT]) for i in range(4)]
        hi = [sb(f"hi{i}", [P, SLOT], F32R) for i in range(2)]
        area = sb("area", [P, 2 * ND, SEQ])
        area_r = rounded("area", [P, 2 * ND, SEQ])
        u_hi, u_lo = area_r[:, 0:ND, :], area_r[:, ND:2 * ND, :]
        area_1, area_2 = area[:, 0:ND, :], area[:, ND:2 * ND, :]
        stage = sb("stage", [P, 4, COLS])
        acc = sb("acc", [P, 2, COLS])
        x_all = sb("x_all", [P, NT, D])
        x_all_r = rounded("x_all", [P, NT, D])
        stage_r = rounded("stage", [P, 4, COLS])
        ada_ring = [x_all[:, s, :] for s in range(NT)]
        vecs = stage[:, 0, 0:3 * P].rearrange("p (v c) -> p v c", v=3)
        u_tmp = acc
        ssq = sb("ssq", [P, NT])
        rstd = sb("rstd", [P, NT])
        w_ba = sb("w_ba", [P, ND, 2 * HEADS])
        cond_raw = sb("cond_raw", [P, ND])
        cond_sig = sb("cond_sig", [P, ND])
        ba_hi = sb("ba_hi", [P, ND, 2 * HEADS], F32R)
        ba_lo = sb("ba_lo", [P, ND, 2 * HEADS], F32R)
        ang_mem = sb("ang_mem", [P, SLOT])
        ang_r = rounded("ang_mem", [P, SLOT])
        ang = ang_mem[0:ROPE, :].rearrange("p (a n) -> p a n", a=4)
        pos_i = sb("pos_i", [ROPE, SEQ], I32)

        ps = [ctx.enter_context(nc.psum_tensor(f"ps{i}", [P, 512], F32)) for i in range(8)]
        ident = planes[:, C_ID, :]
        ones = planes[:, C_ONES, :]

        s_const = sem("s_const")
        s_x = sem("s_x")
        s_slot = [sem(f"s_slot{i}") for i in range(4)]
        s_ada_slot = [sem(f"s_ada_slot{i}") for i in range(4)]
        s_hi = sem("s_hi")
        s_lo = sem("s_lo")
        s_used = sem("s_used")
        s_ada1_used = sem("s_ada1_used")
        s_ada_used = sem("s_ada_used")
        s_acc = sem("s_acc")
        s_mod = sem("s_mod")
        s_rstd = sem("s_rstd")
        s_xn = sem("s_xn")
        s_ut = sem("s_ut")
        s_xcol = sem("s_xcol")
        s_utmp = sem("s_utmp")
        s_uhi = sem("s_uhi")
        s_ulo = sem("s_ulo")
        s_ba_split = sem("s_ba_split")
        s_bank = sem("s_bank")
        s_ev_a = sem("s_ev_a")
        s_ev_v = sem("s_ev_v")
        s_stored = [sem(f"s_stored{i}") for i in range(4)]
        s_row = sem("s_row")
        s_row_out = sem("s_row_out")
        s_prep_pe = sem("s_prep_pe")
        s_prep_a = sem("s_prep_a")
        s_prep_v = sem("s_prep_v")
        s_act = sem("s_act")
        s_dve = sem("s_dve")
        s_pool = sem("s_pool")

        w_in, w_ada = a["w_in"][0], a["w_ada"][0]
        w_in_v = w_in.rearrange("(t p) n -> p t n", p=P)
        w_ada_v = w_ada.rearrange("(t p) n -> p t n", p=P)
        x_v = a["x"][0].rearrange("(t p) d -> p t d", p=P)


        yb_t = dram("yb_t", [HEADS, P, SEQ])
        dtb_row = sb("dtb_row", [P, HEADS])
        alog_row = sb("alog_row", [P, HEADS])
        og_row = sb("og_row", [P, HD])
        dec_in = sb("dec_in", [P, 4, NT, HEADS])
        g_nat = sb("g_nat", [P, NT, HEADS])
        beta = sb("beta", [P, NT, HEADS])
        gcum = sb("gcum", [P, NT, HEADS])
        tail = sb("tail", [P, NT, HEADS])
        beta_g = sb("beta_g", [P, NT, HEADS])
        PAD = CONV - 1
        dn = Carve(area_1.rearrange("p a b -> p (a b)"), area_2.rearrange("p a b -> p (a b)"),
                   x_all[:, :, :].rearrange("p a b -> p (a b)"))
        dn_xin = [dn.take([P, 3, PAD + SEQ]) for _ in range(2)]
        dn_z = [dn.take([P, NT, HD]) for _ in range(2)]
        dn_heads = [DeltaHead(dn, banks, dn_xin[par], dn_z[par])
                    for par, banks in enumerate(((ps[4], ps[5], ps[6]), (ps[0], ps[1], ps[7])))]

        s_rows = sem("s_rows")
        s_dn_in = sem("s_dn_in")
        s_dn_z = sem("s_dn_z")
        s_conv = sem("s_conv")
        s_sig = sem("s_sig")
        s_silu = sem("s_silu")
        s_sq = sem("s_sq")
        s_ss = sem("s_ss")
        s_nroot = sem("s_nroot")
        s_unit = sem("s_unit")
        s_gb = sem("s_gb")
        s_gbc = sem("s_gbc")
        s_bbc = sem("s_bbc")
        s_eg = sem("s_eg")
        s_darg = sem("s_darg")
        s_dec = sem("s_dec")
        s_kb = sem("s_kb")
        s_gram = sem("s_gram")
        s_knat = sem("s_knat")
        s_vnat = sem("s_vnat")
        s_nt = sem("s_nt")
        s_qkt = sem("s_qkt")
        s_first = sem("s_first")
        s_kfac = sem("s_kfac")
        s_vb = sem("s_vb")
        s_inv1 = sem("s_inv1")
        s_inv1_out = sem("s_inv1_out")
        s_clev = sem("s_clev")
        s_xm = sem("s_xm")
        s_xc = sem("s_xc")
        s_corr = sem("s_corr")
        s_inv = sem("s_inv")
        s_uw = sem("s_uw")
        s_u = sem("s_u")
        s_w = sem("s_w")
        s_ws = sem("s_ws")
        s_vn = sem("s_vn")
        s_sd = sem("s_sd")
        s_state = sem("s_state")
        s_osq = sem("s_osq")
        s_oms = sem("s_oms")
        s_oroot = sem("s_oroot")
        s_zsig = sem("s_zsig")
        s_zmul = sem("s_zmul")
        s_zgain = sem("s_zgain")
        s_on = sem("s_on")
        s_ot = sem("s_ot")
        s_ot_out = sem("s_ot_out")
        s_yb = sem("s_yb")
        NL = len(LEVELS) - 1
        NC = SEQ // CHUNK

        def tiles(x):
            return x.rearrange("p (t c) -> p t c", t=NT)

        def column(x, h):
            return x[:, :, bass.ds(h, 1)].broadcast_to([P, NT, HD])

        def plane(c):
            return planes[:, c:c + 1, :].broadcast_to([P, NT, P])

        PARTS = [
            (IN_DN, T_DN, 4, False, 12), (IN_DN + 4 * COLS, T_DN + 4, 2, False, None),
            (IN_Z, 2, 2, True, None), (IN_VA, 0, 2, True, None),
            (IN_QA, T_QA, 4, False, 16), (IN_GA, T_GA, 4, False, 8), (IN_GB, T_GB, 4, False, 20),
        ]
        N_ADA1 = 8

        gate_in = sb("gate_in", [P, 4, SEQ])

        SCALE = HD ** -0.5
        at = Carve(stage[:, :, :].rearrange("p a b -> p (a b)"), gate_in[:, :, :].rearrange("p a b -> p (a b)"),
                   x_all[:, :, :].rearrange("p a b -> p (a b)"))
        at_q = [at.take([P, SEQ]) for _ in range(2)]
        at_k = [at.take([P, SEQ]) for _ in range(2)]
        at_v = [at.take([P, NT, HD]) for _ in range(2)]
        rot = at.take([P, SEQ])
        prob = at.take([P, NT, SEQ])
        prob_t = at.take([P, NT, SEQ])
        at_scores = [ps[1][:, 2 * P:3 * P], ps[1][:, 0:2 * P], ps[2][:, 0:3 * P], ps[3][:, 0:4 * P]]
        at_turned = [ps[4][:, 0:4 * P], ps[5][:, P:4 * P], ps[6][:, 0:2 * P], ps[5][:, 0:P]]
        at_raw = sb("at_raw", [P, NT])
        at_max = sb("at_max", [P, NT])
        at_sum = sb("at_sum", [P, NT])
        s_at_in = [sem(f"s_at_in{i}") for i in range(2)]
        s_rot = sem("s_rot")
        s_roped = sem("s_roped")
        s_sc = sem("s_sc")
        s_nmax = sem("s_nmax")
        s_exp = sem("s_exp")
        s_prob = sem("s_prob")
        s_pt = sem("s_pt")
        s_pt_out = sem("s_pt_out")
        s_av = sem("s_av")
        s_av_out = sem("s_av_out")
        s_av_lo = sem("s_av_lo")

        N_IN = sum(p[2] for p in PARTS)
        yh = u_hi[:, :, :]
        yl = u_lo[:, :, :]
        merged = x_all[:, :, :].rearrange("p m (k n) -> p (m k) n", n=SEQ)
        y_nat = x_all
        s_yl = sem("s_yl")
        s_yh = sem("s_yh")
        s_ysplit = sem("s_ysplit")
        s_gate = [sem(f"s_gate{i}") for i in range(2)]
        s_gsig = sem("s_gsig")
        s_merged = sem("s_merged")

        rows4 = dram("rows4", [4, D])
        x1_s = dram("x1_s", [SEQ, D])
        u2_s = dram("u2_s", [SEQ, D])
        yb_s = dram("yb_s", [2 * SEQ, D])
        NB = EXPERTS + MAX_OVER
        table = dram("table", [P * (NB + 1), 1], I32)
        mr = sb("mr", [ND, 4, P])
        br = sb("br", [ND, 4, P])
        gr = sb("gr", [ND, 3, P])
        row_g1 = gate_in[:, :, :].rearrange("p a b -> p (a b)")
        row_a2 = ang_mem[:, :]
        row_s2 = stage[:, :, :].rearrange("p a b -> p (a b)")
        u2_nat = area_2.rearrange("p (m k) n -> p m (k n)", m=NT)
        u2_t = area_1
        w_r = sb("w_r", [P, ND, GROUPS + EXPERTS])
        NR = GROUPS + EXPERTS
        b_r = sb("b_r", [P, NR])
        ss2 = sb("ss2", [P, 2, NT])
        ss_y = sb("ss_y", [P, NT, 4])
        s_ysq = sem("s_ysq")
        s_ysum = sem("s_ysum")
        s_mr = sem("s_mr")
        s_rows4 = sem("s_rows4")
        s_rowb = sem("s_rowb")
        s_xin2 = sem("s_xin2")
        s_res = sem("s_res")
        s_rooty = sem("s_rooty")
        s_x1 = sem("s_x1")
        s_root1 = sem("s_root1")
        s_u2 = sem("s_u2")
        s_x1_out = sem("s_x1_out")
        s_u2_out = sem("s_u2_out")
        s_u2t = sem("s_u2t")
        s_u2t_out = sem("s_u2t_out")
        s_route_v = sem("s_route_v")
        s_route_a = sem("s_route_a")
        s_route_pe = sem("s_route_pe")
        s_table = sem("s_table")
        s_logit = sem("s_logit")

        rt = Carve(stage[:, :, :].rearrange("p a b -> p (a b)"))
        logit = rt.take([P, NT, NR])
        e_log = rt.take([P, NT, EXPERTS])
        tmp32 = rt.take([P, NT, EXPERTS])
        oh1 = rt.take([P, NT, EXPERTS])
        oh2 = rt.take([P, NT, EXPERTS])
        both = rt.take([P, NT, EXPERTS])
        rank = rt.take([P, NT, EXPERTS])
        oh_g = rt.take([P, NT, GROUPS])
        tmp4 = rt.take([P, NT, GROUPS])
        r1 = rt.take([P, 16, NT])
        cnt = rt.take([P, 4, EXPERTS])
        tmp7 = rt.take([P, MAX_OVER, EXPERTS])
        over_t = rt.take([P, P])
        place = rt.take([P, 2, NT])
        wts = sb("wts", [P, 2, NT])
        place_i = sb("place_i", [P, 2 * NT], I32)
        id_i = sb("id_i", [P, 2 * NT], I32)
        plan_f = sb("plan_f", [P, MAX_OVER + 2])
        plan = sb("plan", [P, MAX_OVER + 2], I32)
        fill = sb("fill", [P, NB + 1], I32)
        row_i = sb("row_i", [P, NB + 1], I32)
        row_f = sb("row_f", [P, NB + 1])
        tok_f = sb("tok_f", [P, NB + 1])
        tok_i = sb("tok_i", [P, NB + 1], I32)
        NO_ROW = 1 << 20

        mo = Carve(area_2.rearrange("p a b -> p (a b)"), area_1.rearrange("p a b -> p (a b)"))
        mo_r = Carve(u_lo.rearrange("p a b -> p (a b)"), u_hi.rearrange("p a b -> p (a b)"))
        m_raw = [raw[i][:, :] for i in range(4)] + [mo.take([P, SLOT]) for _ in range(8)]
        m_raw_r = [raw_r[i][:, :] for i in range(4)] + [mo_r.take([P, SLOT]) for _ in range(8)]
        m_hi = [hi[i][:, :] for i in range(2)] + [
            ang_r[:, :], stage_r[:, :, :].rearrange("p a b -> p (a b)")]
        mx = Carve(x_all[:, :, :].rearrange("p a b -> p (a b)"))
        xg = mx.take([P, D])
        y_e = mx.take([P, D])
        mx_r = Carve(x_all_r[:, 2:4, :].rearrange("p a b -> p (a b)"))
        xe_hi = mx_r.take([P, ND, P])
        xe_lo = mx_r.take([P, ND, P])
        me = Carve(gate_in[:, :, :].rearrange("p a b -> p (a b)"))
        h_sig, h_e = me.take([P, FF]), me.take([P, FF])
        gate_in_r = rounded("gate_in", [P, 4, SEQ])
        ht_hi = gate_in_r[:, 2, :].rearrange("p (a b) -> p a b", a=NF)
        ht_lo = gate_in_r[:, 3, :].rearrange("p (a b) -> p a b", a=NF)
        g_idx = sb("g_idx", [P, 1], I32)
        y_idx = sb("y_idx", [P, 1], I32)
        s_mslot = s_slot + s_ada_slot + [sem(f"s_mslot{i}") for i in range(4)]
        mslot_base = [16 * (N_ADA1 + N_IN + 8)] * 4 + [16 * 16] * 4 + [0] * 4
        s_mhi = sem("s_mhi")
        s_mlo = sem("s_mlo")
        s_mused = sem("s_mused")
        s_gi = sem("s_gi")
        s_yi = sem("s_yi")
        s_xg = sem("s_xg")
        s_xt = sem("s_xt")
        s_xehi = sem("s_xehi")
        s_xelo = sem("s_xelo")
        s_hsig = sem("s_hsig")
        s_h = sem("s_h")
        s_ht = sem("s_ht")
        s_hthi = sem("s_hthi")
        s_htlo = sem("s_htlo")
        s_ybank = sem("s_ybank")
        s_ye_a = sem("s_ye_a")
        s_ye_v = sem("s_ye_v")
        s_ysc = sem("s_ysc")

        f_x, row_g2 = m_raw[3:7], m_raw[7]
        f_y = [[m_raw[0], m_raw[1]], [m_raw[2], m_raw[8]], [m_raw[9], m_raw[10]], [m_raw[11], xg]]
        f_sq = x_all[:, 2, :]
        s_f_in = s_at_in + [s_xin2, s_yl]
        f_in_base = [HEADS // 2 * 48] * 2 + [16 * NT, 16]
        ss_f = sb("ss_f", [P, NT])
        s_g2 = sem("s_g2")
        s_f_y = sem("s_f_y")
        s_f_ss = sem("s_f_ss")
        s_f_out = sem("s_f_out")
        s_out = sem("s_out")

        def split3(eng, bank, l_hi, l_lo, r_hi, r_lo, first, last):
            eng.matmul(bank, l_hi, r_hi, start=first, stop=False)
            eng.matmul(bank, l_hi, r_lo, start=False, stop=False)
            return eng.matmul(bank, l_lo, r_hi, start=False, stop=last)

        block = ctx.enter_context(nc.Block())

        @block.sync
        def _(sp):
            sp.dma_start(planes[:, :, :], a["planes"]).then_inc(s_const, 16)
            sp.dma_start(small[:, :], a["small"]).then_inc(s_const, 16)
            sp.dma_start(vecs[0:ND, 0, :], a["c"][0].rearrange("(t p) -> t p", p=P)).then_inc(s_const, 16)
            sp.dma_start(vecs[ND:2 * ND, 0, :], a["norm_mix_pre"][0].rearrange("(t p) -> t p", p=P)).then_inc(s_const, 16)
            sp.dma_start(vecs[2 * ND:3 * ND, 0, :], a["norm_ffn_pre"][0].rearrange("(t p) -> t p", p=P)).then_inc(s_const, 16)
            sp.dma_start(vecs[0:96, 1, :], a["b_ada"][0].rearrange("(t p) -> t p", p=P)).then_inc(s_const, 16)
            sp.dma_start(vecs[0:96, 2, :], a["conv_w"][0].rearrange("k (t p) -> (k t) p", p=P)).then_inc(s_const, 16)
            sp.dma_start(pos_i[:, :], a["positions"].broadcast_to([ROPE, SEQ])).then_inc(s_const, 16)
            def ada1_slots(c):
                for s in range(4):
                    sp.wait_ge(s_ada1_used, c * 4 + (s + 1))
                    sp.dma_start(raw[s][:, :].rearrange("p (t n) -> p t n", t=4),
                                 w_ada_v[:, 4 * s:4 * s + 4, bass.ds(c * COLS, COLS)]).then_inc(s_slot[s], 16)

            ada1_slots(0)
            for t in range(NT):
                sp.dma_start(x_all[:, t, :], x_v[:, t, :]).then_inc(s_x, 16)
            sp.dma_start(w_ba[:, :, :], w_in_v[:, :, IN_BETA:IN_BETA + 2 * HEADS]).then_inc(s_x, 16)
            with sp.Fori(1, N_ADA1) as c:
                ada1_slots(c)
            sp.wait_ge(s_ada1_used, 4 + 4 * N_ADA1)
            done = ada_done = 0
            for col0, row0, n, natural, ada0 in PARTS:
                with sp.Fori(0, n) as c:
                    for s in range(4):
                        sp.wait_ge(s_used, (c + done) * 4 + (s + 1))
                        sp.dma_start(raw[s][:, :].rearrange("p (t n) -> p t n", t=4),
                                     w_in_v[:, 4 * s:4 * s + 4, bass.ds(c * COLS + col0, COLS)]).then_inc(s_slot[s], 16)
                    if ada0 is not None:
                        for s in range(4):
                            if s == 0 and ada_done == 0:
                                sp.wait_ge(s_ut, ND)
                            sp.wait_ge(s_ada_used, (c + ada_done) * 4 + (s + 1))
                            sp.dma_start(ada_ring[s].rearrange("p (t n) -> p t n", t=4),
                                         w_ada_v[:, 4 * s:4 * s + 4, bass.ds((c + ada0) * COLS, COLS)]).then_inc(s_ada_slot[s], 16)
                done += n
                if ada0 is not None:
                    ada_done += n
            w_moba = a["w_branch_moba"][0].rearrange("(t p) n -> p t n", p=P)
            w_delta = a["w_branch_delta"][0].rearrange("(t p) n -> p t n", p=P)
            w_out = a["w_out"][0].rearrange("(t p) n -> p t n", p=P)

            def merge_slot(c, s):
                sp.wait_ge(s_used, (c + N_IN) * 4 + (s + 1))
                sp.dma_start(raw[s][:, :].rearrange("p (t n) -> p t n", t=4),
                             (w_moba, w_delta)[s // 2][:, 4 * (s % 2):4 * (s % 2) + 4, bass.ds(c * COLS, COLS)]).then_inc(s_slot[s], 16)

            for s in range(4):
                merge_slot(0, s)
            for b in range(4):
                sp.wait_ge(s_stored[b], 16 * N_IN)
            sp.wait_ge(s_pool, 1)
            blocks = proj_t.rearrange("c b p n -> (c b) p n")[T_DN * 4:(T_DN + 6) * 4].rearrange("(j h) p n -> h p j n", j=3)
            with sp.Fori(0, HEADS // 2) as i:
                sp.wait_ge(s_silu, i * 6)
                for par in range(2):
                    sp.dma_start(dn_xin[par][:, :, PAD:PAD + SEQ],
                                 blocks[bass.ds(i * 2 + par, 1)].rearrange("a p j n -> (a p) j n")).then_inc(s_dn_in, 16)
                sp.wait_ge(s_on, i * 2)
                for par in range(2):
                    sp.dma_start(dn_z[par], proj_n[:, :, bass.ds((i * 2 + par) * HD + WIDTH, HD)].rearrange("b p n -> p b n")).then_inc(s_dn_z, 16)
            tq = proj_t.rearrange("c b p n -> (c b) p n")
            with sp.Fori(0, HEADS // 2) as i:
                for par in range(2):
                    sp.wait_ge(s_av, i * 2 + (par + 1))
                    for dst, first in ((at_q[par], T_QA * 4), (at_k[par], T_KA * 4)):
                        sp.dma_start(dst, tq[bass.ds(i * 2 + (par + first), 1)].rearrange("a p n -> (a p) n")).then_inc(s_at_in[par], 16)
                    sp.dma_start(at_v[par], proj_n[:, :, bass.ds((i * 2 + par) * HD, HD)].rearrange("b p n -> p b n")).then_inc(s_at_in[par], 16)
            sp.wait_ge(s_ot_out, HEADS)
            sp.wait_ge(s_yb, 16 * HEADS)
            sp.dma_start(area_2[:, HEADS:2 * HEADS, :], yb_t.rearrange("h p n -> p h n")).then_inc(s_yl, 16)
            with sp.Fori(1, 4) as c:
                for s in range(4):
                    merge_slot(c, s)
            with sp.Fori(0, 4) as c:
                for s in range(4):
                    sp.wait_ge(s_used, (c + (N_IN + 4)) * 4 + (s + 1))
                    sp.dma_start(raw[s][:, :].rearrange("p (t n) -> p t n", t=4),
                                 w_out[:, 4 * s:4 * s + 4, bass.ds(c * COLS, COLS)]).then_inc(s_slot[s], 16)
            sp.dma_start(w_r[:, :, 0:GROUPS], a["router_group_w"][0].rearrange("(t p) n -> p t n", p=P)).then_inc(s_rowb, 16)
            sp.dma_start(w_r[:, :, GROUPS:NR], a["router_expert_w"][0].rearrange("(t p) n -> p t n", p=P)).then_inc(s_rowb, 16)
            sp.dma_start(b_r[:, 0:GROUPS], a["router_group_b"].broadcast_to([P, GROUPS])).then_inc(s_rowb, 16)
            sp.dma_start(b_r[:, GROUPS:NR], a["router_expert_b"].broadcast_to([P, EXPERTS])).then_inc(s_rowb, 16)
            sp.wait_ge(s_rows4, 16)
            sp.wait_ge(s_merged, 4 + 16)
            for n, dst in enumerate((row_g1, row_s2, row_a2)):
                sp.dma_start(dst, rows4[n:n + 1, :].broadcast_to([P, D])).then_inc(s_rowb, 16)
            for m in range(NT):
                sp.wait_ge(s_used, 4 * (N_IN + 7) + (m + 5))
                sp.dma_start(raw[m][:, :], x_v[:, m, :]).then_inc(s_xin2, 16)

            def expert_slot(e, j, s):
                sp.wait_ge(s_mused, j * 12 + (s + 1))
                if s < 8:
                    src = a[("expert_w_gate", "expert_w_up")[s // 4]][0, bass.ds(e, 1), (s % 4) * 4 * P:(s % 4 + 1) * 4 * P, :]
                    sp.dma_start(m_raw[s].rearrange("p (t n) -> p t n", t=4),
                                 src.rearrange("a (t p) n -> p (a t) n", p=P)).then_inc(s_mslot[s], 16)
                else:
                    src = a["expert_w_down"][0, bass.ds(e, 1), (s - 8) * P:(s - 7) * P, :]
                    sp.dma_start(m_raw[s], src.rearrange("a p n -> (a p) n")).then_inc(s_mslot[s], 16)

            for s in range(4):
                sp.wait_ge(s_x1, s + 1)
                expert_slot(0, 0, s)
            sp.wait_ge(s_u2_out, 16 * NT)
            sp.wait_ge(s_logit, 1)
            for s in range(4, 12):
                expert_slot(0, 0, s)
            with sp.Fori(1, EXPERTS) as j:
                for s in range(12):
                    expert_slot(j, j, s)
            sp.wait_ge(s_route_v, 6)
            n_blocks = sp.value_load(plan[0:1, MAX_OVER:MAX_OVER + 1], min_val=EXPERTS, max_val=NB)
            with sp.If(n_blocks > EXPERTS):
                with sp.Fori(EXPERTS, n_blocks) as j:
                    e = sp.value_load(plan[0:1, bass.ds(j - EXPERTS, 1)], min_val=0, max_val=EXPERTS - 1)
                    for s in range(12):
                        expert_slot(e, j, s)
            for n in range(5):
                sp.wait_ge(s_mused, n_blocks * 12 + (n + 4))
                src = x1_s[n * P:(n + 1) * P, :] if n < NT else rows4[3:4, :].broadcast_to([P, D])
                sp.dma_start(m_raw[3 + n], src).then_inc(s_g2, 16)
            sp.wait_ge(s_mused, n_blocks * 12 + 12)
            sp.nop(nofuse=True)
            sp.wait_ge(s_mlo, n_blocks * 12)
            sp.nop(nofuse=True)
            sp.wait_ge(s_ysc, n_blocks * 16)
            sp.nop(nofuse=True)
            sp.wait_ge(s_xg, n_blocks * 16 + 16)
            for m in range(NT):
                for k in range(2):
                    sp.dma_start(f_y[m][k], yb_s[k * SEQ + m * P:k * SEQ + (m + 1) * P, :]).then_inc(s_f_in[m], 16)

        @block.gpsimd
        def _(pool):
            done = ada_done = 0
            for col0, row0, n, natural, ada0 in PARTS:
                with pool.Fori(0, n) as c:
                    for b in range(4):
                        pool.wait_ge((s_ev_a, s_ev_v)[b // 2], (c + done) * 2 + (b % 2 + 3))
                        dst = (proj_n[b, :, bass.ds((c + row0) * COLS, COLS)] if natural else
                               proj_t[bass.ds(c + row0, 1), b].rearrange("a p n -> (a p) n"))
                        pool.dma_start(dst,
                                     stage[:, b, :]).then_inc(s_stored[b], 16)
                    if ada0 is not None:
                        pool.wait_ge(s_row, c + (ada_done + 2))
                        pool.dma_start(mod_rows[bass.ds(c + (ada0 - N_ADA1), 1), :], row_out[:, 0, :]).then_inc(s_row_out, 16)
                done += n
                if ada0 is not None:
                    ada_done += n
            for b in range(4):
                pool.wait_ge(s_stored[b], 16 * done)

            pool.dma_start(dtb_row[:, :], a["dn_dt_bias"].broadcast_to([P, HEADS])).then_inc(s_rows, 16)
            pool.dma_start(alog_row[:, :], a["dn_a_log"].broadcast_to([P, HEADS])).then_inc(s_rows, 16)
            pool.dma_start(og_row[:, :], a["dn_out_norm"].broadcast_to([P, HD])).then_inc(s_rows, 16)
            for par in range(2):
                ins = pool.memset(dn_xin[par][:, :, 0:PAD], 0.0)
            ins.then_inc(s_pool, 1)
            with pool.Fori(0, HEADS // 2) as i:
                for n in range(NL):
                    for par, d in enumerate(dn_heads):
                        if n == 0:
                            pool.wait_ge(s_vnat, count(i, 1, 0, par))
                            pool.wait_ge(s_gram, count(i, 2, 1, par))
                            pool.wait_ge(s_nt, count(i, 1, 0, par))
                        if n >= 2:
                            pool.wait_ge(s_xm, count(i, NL, n - 2, par))
                        pool.tensor_tensor(tiles(d.c_lev[n % 2]), tiles(d.n_t), plane(C_LEV + 1 + n), ALU.mult).then_inc(s_clev, 1)
                for par, d in enumerate(dn_heads):
                    pool.wait_ge(s_zsig, count(i, 1, 0, par))
                    pool.tensor_tensor(d.z_sig, d.z_sig, d.z_in, ALU.mult).then_inc(s_zmul, 1)
                for par, d in enumerate(dn_heads):
                    pool.wait_ge(s_zmul, count(i, 1, 0, par))
                    pool.tensor_tensor(d.z_sig, d.z_sig, og_row[:, :].rearrange("p (a c) -> p a c", a=1).broadcast_to([P, NT, HD]),
                                       ALU.mult).then_inc(s_zgain, 1)
                for par, d in enumerate(dn_heads):
                    pool.wait_ge(s_ot_out, count(i, 1, 0, par))
                    pool.dma_start(yb_t[bass.ds(i * 2 + par, 1)].rearrange("a p n -> (a p) n"), d.o_out).then_inc(s_yb, 16)
            pool.wait_ge(s_yb, 16 * HEADS)
            pool.wait_ge(s_row_out, 16 * 16)
            flat = mod_rows.rearrange("c n -> (c n)")
            pool.dma_start(mr[:, :, :], flat.rearrange("(v t p) -> t v p", v=4, p=P)).then_inc(s_mr, 16)
            pool.dma_start(br[:, :, :], a["b_ada"][0, 2 * D:6 * D].rearrange("(v t p) -> t v p", v=4, p=P)).then_inc(s_mr, 16)
            for n, g in enumerate(("norm_mix_post", "norm_ffn_pre", "norm_ffn_post")):
                pool.dma_start(gr[:, n, :], a[g][0].rearrange("(t p) -> t p", p=P)).then_inc(s_mr, 16)
            pool.wait_ge(s_res, 1)
            pool.dma_start(rows4.rearrange("v (t p) -> t v p", p=P), mr[:, :, :]).then_inc(s_rows4, 16)
            tg = proj_t.rearrange("c b p n -> (c b) p n")
            with pool.Fori(0, 4) as c:
                for b in range(4):
                    pool.wait_ge(s_merged, c * 4 + (b + 3))
                    for k, first in enumerate((T_GA * 4, T_GB * 4)):
                        pool.dma_start(gate_in[:, (b % 2) * 2 + k, :],
                                       tg[bass.ds(c * 4 + (b + first), 1)].rearrange("a p n -> (a p) n")).then_inc(s_gate[b % 2], 16)
            pool.memset(fill[:, :], NO_ROW).then_inc(s_pool, 1)
            pool.wait_ge(s_pool, 2)
            pool.dma_start(table.rearrange("(p b) a -> p (b a)", p=P), fill[:, :]).then_inc(s_table, 16)
            for m in range(NT):
                pool.wait_ge(s_x1, m + 1)
                pool.dma_start(x1_s[m * P:(m + 1) * P, :], y_nat[:, m, :]).then_inc(s_x1_out, 16)
            for m in range(NT):
                pool.wait_ge(s_u2, m + 1)
                pool.dma_start(u2_s[m * P:(m + 1) * P, :], u2_nat[:, m, :]).then_inc(s_u2_out, 16)
            pool.wait_ge(s_table, 16)
            pool.wait_ge(s_route_v, 8)
            for n in range(2 * NT):
                pool.indirect_dma_start(out=table, out_offset=bass.IndirectOffsetOnAxis(ap=place_i[:, n:n + 1], axis=0),
                                        in_=id_i[:, n:n + 1], in_offset=None,
                                        bounds_check=P * (NB + 1) - 1, oob_is_err=False).then_inc(s_table, 16)
            pool.wait_ge(s_table, 16 + 16 * 2 * NT)
            pool.dma_start(row_i[:, :], table.rearrange("(p b) a -> p (b a)", p=P)).then_inc(s_table, 16)
            pool.wait_ge(s_u2_out, 16 * NT)
            pool.wait_ge(s_x1_out, 16 * NT)
            pool.memset(xg, 0.0).then_inc(s_pool, 1)
            pool.wait_ge(s_pool, 3)
            pool.wait_ge(s_route_v, 9)
            pool.wait_ge(s_route_v, 6)
            n_blocks = pool.value_load(plan[0:1, MAX_OVER:MAX_OVER + 1], min_val=EXPERTS, max_val=NB)

            def gather(j, n):
                pool.tensor_copy(g_idx[:, :], tok_i[:, bass.ds(j, 1)]).then_inc(s_gi, 1)
                pool.wait_ge(s_gi, n)
                pool.nop(nofuse=True)
                pool.indirect_dma_start(out=xg, out_offset=None, in_=u2_s,
                                        in_offset=bass.IndirectOffsetOnAxis(ap=g_idx[:, :], axis=0),
                                        bounds_check=SEQ - 1, oob_is_err=False).then_inc(s_xg, 16)

            gather(0, 1)
            with pool.Fori(0, n_blocks) as j:
                pool.wait_ge(s_xt, j * 4 + 4)
                pool.wait_ge(s_xg, j * 16 + 16)
                gather(j + 1, j + 2)
                pool.wait_ge(s_ysc, j * 16)
                pool.tensor_copy(y_idx[:, :], row_i[:, bass.ds(j, 1)]).then_inc(s_yi, 1)
                pool.wait_ge(s_yi, j + 1)
                pool.wait_ge(s_ye_a, j * 2 + 2)
                pool.wait_ge(s_ye_v, j * 2 + 2)
                pool.nop(nofuse=True)
                pool.indirect_dma_start(out=yb_s, out_offset=bass.IndirectOffsetOnAxis(ap=y_idx[:, :], axis=0),
                                        in_=y_e, in_offset=None,
                                        bounds_check=2 * SEQ - 1, oob_is_err=False).then_inc(s_ysc, 16)
            pool.wait_ge(s_xg, n_blocks * 16 + 16)
            pool.wait_ge(s_ysc, n_blocks * 16)
            pool.nop(nofuse=True)
            for m in range(NT):
                pool.wait_ge(s_f_out, m + 1)
                pool.dma_start(out[0, m * P:(m + 1) * P, :], f_x[m]).then_inc(s_out, 16)
            pool.wait_ge(s_out, 16 * NT)

        @block.tensor
        def _(pe):
            pe.sem_inc(s_used, 4)
            pe.wait_ge(s_const, 16 * 8)
            pe.transpose(ps[7][:, 0:48], vecs[0:48, 0, :], ident[0:48, 0:48])
            pe.transpose(ps[7][:, 64:160], vecs[0:96, 1, :], ident[0:96, 0:96])
            pe.transpose(ps[7][:, 192:288], vecs[0:96, 2, :], ident[0:96, 0:96]).then_inc(s_prep_pe, 1)

            def mod_columns(c, n, par):
                pe.wait_ge(s_acc, n)
                for j in range(4):
                    mm = pe.matmul(ps[6][:, bass.ds(c * 4 + j, 1)], acc[:, par, j * P:(j + 1) * P],
                                   ones[:, 0:1], start=True, stop=True)
                mm.then_inc(s_mod, 1)

            with pe.Fori(0, N_ADA1 // 4) as i:
                for par in range(2):
                    mod_columns(i * 2 + par, i * 2 + (par + 1), par)
            pe.wait_ge(s_xn, NT)
            for t in range(ND):
                if t >= 4:
                    pe.wait_ge(s_xcol, t - 3)
                for m in range(NT):
                    tr = pe.transpose(ps[t % 4][:, m * P:(m + 1) * P], x_all[:, m, t * P:(t + 1) * P], ident)
                tr.then_inc(s_ut, 1)
            with pe.Fori(N_ADA1 // 4, N_ADA1 // 2) as i:
                for par in range(2):
                    mod_columns(i * 2 + par, i * 2 + (par + 1), par)
            pe.wait_ge(s_xcol, ND)
            pe.wait_ge(s_prep_a, 5)

            done = ada_done = 0
            for col0, row0, n, natural, ada0 in PARTS:
                with pe.Fori(0, n) as c:
                    for s in range(4):
                        pe.wait_ge(s_lo, (c + done) * 4 + (s + 1))
                        if done == 0:
                            pe.wait_ge(s_ulo, 4 * s + 4)
                        for b in range(4):
                            if s == 0:
                                pe.wait_ge((s_ev_a, s_ev_v)[b // 2], (c + done) * 2 + (b % 2 + 1))
                            for t in range(4):
                                cols = slice(t * COLS, (t + 1) * COLS)
                                part = slice(t * COLS + b * P, t * COLS + (b + 1) * P)
                                w_lo = raw_r[s]
                                k = 4 * s + t
                                first, last = k == 0, k == ND - 1
                                if natural:
                                    tok = slice(b * P, (b + 1) * P)
                                    mm = split3(pe, ps[b][:, :], u_hi[:, k, tok], u_lo[:, k, tok],
                                                hi[s % 2][:, cols], w_lo[:, cols], first, last)
                                else:
                                    mm = split3(pe, ps[b][:, :], hi[s % 2][:, part], w_lo[:, part],
                                                u_hi[:, k, :], u_lo[:, k, :], first, last)
                            if s == 3 and b < 3:
                                mm.then_inc(s_bank, 1)
                        mm.then_inc(s_used, 1)
                    if ada0 is not None:
                        pe.wait_ge(s_acc, c + (N_ADA1 + ada_done + 1))
                        pe.wait_ge(s_row, c + (ada_done + 1))
                        pe.matmul(ps[7][0:1, :], ones[:, 0:1], acc[:, 0, :], start=True, stop=True).then_inc(s_mod, 1)
                if done == 0:
                    pe.wait_ge(s_ba_split, 2)
                    for m in range(NT):
                        tok = slice(m * P, (m + 1) * P)
                        for t in range(ND):
                            mm = split3(pe, ps[5][:, m * 16:(m + 1) * 16], u_hi[:, t, tok], u_lo[:, t, tok],
                                        ba_hi[:, t, :], ba_lo[:, t, :], t == 0, t == ND - 1)
                    mm.then_inc(s_prep_pe, 1)
                done += n
                if ada0 is not None:
                    ada_done += n

            pe.wait_ge(s_prep_v, 4)
            for t in range(NT):
                pe.matmul(ps[5][:, t * HEADS:(t + 1) * HEADS], planes[:, C_CUM, :], g_nat[:, t, :], start=True, stop=True)
                mm = pe.matmul(ps[5][:, (NT + t) * HEADS:(NT + t + 1) * HEADS], planes[:, C_TAIL, :], g_nat[:, t, :], start=True, stop=True)
            mm.then_inc(s_prep_pe, 1)

            def per_tile(bank, lhs, rhs):
                for t in range(NT):
                    c = slice(t * P, (t + 1) * P)
                    mm = pe.matmul(bank[:, c], lhs[:, c], rhs if rhs.shape[1] == P else rhs[:, c], start=True, stop=True)
                return mm

            def per_tile_t(bank, x):
                for t in range(NT):
                    c = slice(t * P, (t + 1) * P)
                    mm = pe.transpose(bank[:, c], x[:, c], ident)
                return mm

            def dn_norms(i):
                for n, j in enumerate((1, 0)):
                    for par, d in enumerate(dn_heads):
                        pe.wait_ge(s_sq, count(i, 2, n, par))
                        if n == 0 and par == 0:
                            pe.wait_ge(s_state, i * 2 * NC)
                            pe.wait_ge(s_on, i * 2)
                        pe.matmul((d.sb, d.tb)[j][:, :], ones, d.sq[:, j, :], start=True, stop=True).then_inc(s_ss, 1)

            def dn_decay(i):
                pe.wait_ge(s_ot_out, i * 2)
                for par, d in enumerate(dn_heads):
                    pe.wait_ge(s_gb, count(i, 1, 0, par))
                    per_tile(d.xb, d.inv, planes[:, C_CUM, :]).then_inc(s_gbc, 1)
                for par, d in enumerate(dn_heads):
                    pe.wait_ge(s_nroot, count(i, 2, 0, par))
                    per_tile(d.tb, d.inv_t, ident).then_inc(s_bbc, 1)

            def dn_gram(i):
                for par, d in enumerate(dn_heads):
                    pe.wait_ge(s_kb, count(i, 1, 0, par))
                    pe.wait_ge(s_nroot, count(i, 2, 1, par))
                    per_tile(d.sb, d.cv[:, 1, :], d.kb).then_inc(s_gram, 1)
                for par, d in enumerate(dn_heads):
                    pe.wait_ge(s_unit, count(i, 2, 1, par))
                    per_tile(d.tb, d.cv[:, 1, :], d.cv[:, 0, :]).then_inc(s_gram, 1)

            def dn_naturals(i):
                for par, d in enumerate(dn_heads):
                    pe.wait_ge(s_darg, count(i, 1, 0, par))
                    per_tile_t(d.xb, d.cv[:, 1, :]).then_inc(s_knat, 1)
                for par, d in enumerate(dn_heads):
                    pe.wait_ge(s_silu, count(i, 3, 2, par))
                    pe.wait_ge(s_qkt, count(i, 1, 0, par))
                    per_tile_t(d.tb, d.cv[:, 2, :]).then_inc(s_vnat, 1)
                for par, d in enumerate(dn_heads):
                    pe.wait_ge(s_first, count(i, 1, 0, par))
                    per_tile_t(d.sb, d.inv_t).then_inc(s_inv1, 1)

            def dn_level(i, n):
                for par, d in enumerate(dn_heads):
                    if n == 0:
                        pe.wait_ge(s_inv1_out, count(i, 1, 0, par))
                        pe.wait_ge(s_kfac, count(i, 1, 0, par))
                    else:
                        pe.wait_ge(s_inv, count(i, NL, n - 1, par))
                    pe.wait_ge(s_clev, count(i, NL, n, par))
                    per_tile(d.xb, d.c_lev[n % 2], d.inv).then_inc(s_xm, 1)
                for par, d in enumerate(dn_heads):
                    pe.wait_ge(s_xc, count(i, NL, n, par))
                    if n == 0:
                        pe.wait_ge(s_vb, count(i, 1, 0, par))
                    mm = per_tile(d.tb, d.x_sb, d.inv_t)
                    if n < NL - 1:
                        mm = per_tile(d.sb, d.inv_t, d.x_sb)
                    mm.then_inc(s_corr, 1)

            def dn_solve(i):
                for par, d in enumerate(dn_heads):
                    pe.wait_ge(s_inv, count(i, NL, NL - 1, par))
                    per_tile(d.tb, d.inv_t, d.v_b.rearrange("p t c -> p (t c)"))
                    per_tile(d.sb, d.k_bg.rearrange("p t c -> p (t c)"), d.inv_t).then_inc(s_uw, 1)

            def rows_of(c):
                return slice((c % 2) * CHUNK, (c % 2 + 1) * CHUNK), c // 2

            def dn_scan_w(i, c):
                r, t = rows_of(c)
                for par, d in enumerate(dn_heads):
                    if c == 1:
                        pe.wait_ge(s_w, count(i, 1, 0, par))
                    pe.wait_ge(s_state, count(i, NC, c - 1, par))
                    pe.nop(nofuse=True)
                    pe.matmul(d.xb[r, 0:HD], d.w_t[:, c * CHUNK:(c + 1) * CHUNK], d.state, start=True, stop=True).then_inc(s_ws, 1)

            def dn_scan_o(i, c):
                r, t = rows_of(c)
                for par, d in enumerate(dn_heads):
                    vn = d.u_sol[r, t * HD:(t + 1) * HD] if c == 0 else d.v_new[r, :]
                    if c == 0:
                        pe.wait_ge(s_u, count(i, 1, 0, par))
                        pe.wait_ge(s_w, count(i, 1, 0, par))
                    else:
                        pe.matmul(d.tb[r, t * HD:(t + 1) * HD], d.q_dec[:, c * CHUNK:(c + 1) * CHUNK], d.state, start=True, stop=False)
                        pe.wait_ge(s_vn, count(i, NC - 1, c - 1, par))
                    pe.nop(nofuse=True)
                    pe.matmul(d.tb[r, t * HD:(t + 1) * HD], d.qk_t[r, c * CHUNK:(c + 1) * CHUNK], vn, start=c == 0, stop=True)
                    pe.matmul(d.sb[:, 0:HD], d.k_tail[r, t, :], vn, start=True, stop=True).then_inc(s_sd, 1)

            def dn_out(i):
                for par, d in enumerate(dn_heads):
                    pe.wait_ge(s_on, count(i, 1, 0, par))
                    per_tile_t(d.xb, d.o_out).then_inc(s_ot, 1)

            pe.sem_inc(s_av, 2)
            pe.wait_ge(s_ev_a, 2 * N_IN + 2)
            pe.wait_ge(s_ev_v, 2 * N_IN + 2)
            with pe.Fori(0, HEADS // 2) as i:
                dn_norms(i)
                dn_decay(i)
                dn_gram(i)
                dn_naturals(i)
                for n in range(NL):
                    dn_level(i, n)
                dn_solve(i)
                for c in range(NC):
                    if c:
                        dn_scan_w(i, c)
                    dn_scan_o(i, c)
                dn_out(i)

            def at_rotate(par, loaded):
                pe.wait_ge(s_at_in[par], loaded)
                pe.nop(nofuse=True)
                for bank, x in ((ps[0], at_q[par]), (ps[7], at_k[par])):
                    pe.matmul(bank[0:ROPE, :], planes[0:ROPE, C_ROT, 0:ROPE], x[0:ROPE, :], start=True, stop=True).then_inc(s_rot, 1)

            def at_head(i, par, last):
                h = i * 2 + par
                pe.wait_ge(s_roped, h * 2 + 2)
                for m in range(NT):
                    pe.matmul(at_scores[m], at_q[par][:, m * P:(m + 1) * P], at_k[par][:, 0:(m + 1) * P],
                              start=True, stop=True).then_inc(s_sc, 1)
                if not last:
                    at_rotate(1 - par, (i + par) * 48 + 48)
                pe.wait_ge(s_av_out, h)
                pe.wait_ge(s_av_lo, h)
                for m in range(NT):
                    pe.wait_ge(s_prob, h * NT + (m + 1))
                    for k in range(m + 1):
                        tr = pe.transpose(at_turned[k][:, (m - k) * P:(m - k + 1) * P], prob[:, m, k * P:(k + 1) * P], ident)
                tr.then_inc(s_pt, 1)
                for k in range(NT):
                    pe.wait_ge(s_pt_out, h * NT + (k + 1))
                    mm = pe.matmul(ps[4][:, k * P:SEQ], at_v[par][:, k, :], prob_t[:, k, k * P:SEQ],
                                   start=k == 0, stop=k == NT - 1)
                mm.then_inc(s_av, 1)

            pe.wait_ge(s_ot_out, HEADS)
            at_rotate(0, 48)
            with pe.Fori(0, HEADS // 2 - 1) as i:
                for par in range(2):
                    at_head(i, par, False)
            for par in range(2):
                at_head(HEADS // 2 - 1, par, par == 1)

            pe.wait_ge(s_av_out, HEADS)
            pe.wait_ge(s_av_lo, HEADS)
            with pe.Fori(0, 4) as c:
                for s in range(4):
                    pe.wait_ge(s_lo, (c + N_IN) * 4 + (s + 1))
                    if s == 2:
                        pe.wait_ge(s_ysplit, 2)
                    for b in range(4):
                        if s == 0:
                            pe.wait_ge(s_merged, c * 4 + (b + 1))
                        for t in range(4):
                            part = slice(t * COLS + b * P, t * COLS + (b + 1) * P)
                            k = (s % 2) * 4 + t
                            y = (s // 2) * HEADS + k
                            mm = split3(pe, ps[b + 4 * (s // 2)][:, :], hi[s % 2][:, part], raw_r[s][:, part],
                                        yh[:, y, :], yl[:, y, :], k == 0, k == HEADS - 1)
                        if s == 3 and b < 3:
                            mm.then_inc(s_bank, 1)
                    mm.then_inc(s_used, 1)

            pe.wait_ge(s_ysplit, 6)
            pe.wait_ge(s_merged, 4 + 16)

            with pe.Fori(0, 4) as c:
                for s in range(4):
                    pe.wait_ge(s_lo, (c + (N_IN + 4)) * 4 + (s + 1))
                    for b in range(4):
                        if s == 0:
                            pe.wait_ge((s_ev_a, s_ev_v)[b // 2], (c + N_IN) * 2 + (b % 2 + 1))
                        tok = slice(b * P, (b + 1) * P)
                        for t in range(4):
                            cols = slice(t * COLS, (t + 1) * COLS)
                            k = 4 * s + t
                            mm = split3(pe, ps[b][:, :], yh[:, k, tok], yl[:, k, tok],
                                        hi[s % 2][:, cols], raw_r[s][:, cols], k == 0, k == ND - 1)
                        if s == 3 and b < 3:
                            mm.then_inc(s_bank, 1)
                    mm.then_inc(s_used, 1)

            pe.sem_inc(s_mused, 12)
            pe.wait_ge(s_ev_a, 2 + 2 * (N_IN + 4))
            pe.wait_ge(s_ev_v, 2 + 2 * (N_IN + 4))
            pe.wait_ge(s_rowb, 16 * 7)
            for m in range(NT):
                pe.wait_ge(s_u2, m + 1)
                for q in range(4):
                    if m:
                        pe.wait_ge(s_u2t_out, 4 * m + q - 3)
                    for t in range(4):
                        tr = pe.transpose(ps[q][:, t * P:(t + 1) * P], u2_nat[:, m, (4 * q + t) * P:(4 * q + t + 1) * P], ident)
                    tr.then_inc(s_u2t, 1)
                pe.wait_ge(s_u2t_out, 4 * m + 4)
                for t in range(ND):
                    mm = pe.matmul(ps[4][:, m * NR:(m + 1) * NR], u2_t[:, t, m * P:(m + 1) * P], w_r[:, t, :],
                                   start=t == 0, stop=t == ND - 1)
            mm.then_inc(s_logit, 1)
            pe.wait_ge(s_route_v, 3)
            for m in range(NT):
                for k in range(m):
                    pe.matmul(ps[5][:, m * EXPERTS:(m + 1) * EXPERTS], ones, both[:, k, :], start=k == 0, stop=False)
                pe.matmul(ps[5][:, m * EXPERTS:(m + 1) * EXPERTS], planes[:, C_RANK, :], both[:, m, :], start=m == 0, stop=True)
            for m in range(NT):
                mm = pe.matmul(ps[6][:, 0:EXPERTS], ones, both[:, m, :], start=m == 0, stop=m == NT - 1)
            mm.then_inc(s_route_pe, 1)
            pe.wait_ge(s_route_v, 4)
            pe.transpose(ps[7][0:EXPERTS, 0:P], cnt[:, 1, :], ident).then_inc(s_route_pe, 1)
            pe.wait_ge(s_route_v, 5)
            pe.matmul(ps[5][:, 256:256 + EXPERTS], over_t[0:EXPERTS, :], planes[0:EXPERTS, C_RANK, 0:EXPERTS],
                      start=True, stop=True).then_inc(s_route_pe, 1)

            def block_transposes(n):
                for q in range(4):
                    if q >= 2:
                        pe.wait_ge(s_xelo, n + (q - 1))
                    for t in range(4):
                        tr = pe.transpose(ps[2 + q % 2][:, t * P:(t + 1) * P], xg[:, (4 * q + t) * P:(4 * q + t + 1) * P], ident)
                    tr.then_inc(s_xt, 1)

            pe.wait_ge(s_route_v, 6)
            n_blocks = pe.value_load(plan[0:1, MAX_OVER:MAX_OVER + 1], min_val=EXPERTS, max_val=NB)
            pe.wait_ge(s_xg, 16)
            block_transposes(0)
            with pe.Fori(0, n_blocks) as j:
                for s in range(8):
                    if s % 4 == 0:
                        pe.wait_ge(s_xelo, j * 4 + 4)
                        pe.wait_ge((s_htlo, s_h)[s // 4], j)
                    pe.wait_ge(s_mlo, j * 12 + (s + 1))
                    for t in range(4):
                        cols = slice(t * COLS, (t + 1) * COLS)
                        k = 4 * (s % 4) + t
                        mm = split3(pe, ps[s // 4][:, :], xe_hi[:, k, :], xe_lo[:, k, :],
                                    m_hi[s % 4][:, cols], m_raw_r[s][:, cols], k == 0, k == ND - 1)
                    mm.then_inc(s_mused, 1)
                pe.wait_ge(s_xg, j * 16 + 32)
                block_transposes(j * 4 + 4)
                pe.wait_ge(s_h, j + 1)
                for t in range(NF):
                    tr = pe.transpose(ps[0][:, t * P:(t + 1) * P], h_e[:, t * P:(t + 1) * P], ident)
                tr.then_inc(s_ht, 1)
                pe.wait_ge(s_htlo, j + 1)
                for s in range(8, 12):
                    pe.wait_ge(s_mlo, j * 12 + (s + 1))
                    for b in range(4):
                        if s == 8:
                            pe.wait_ge((s_ye_a, s_ye_v)[b // 2], j * 2)
                        cols = slice(b * COLS, (b + 1) * COLS)
                        mm = split3(pe, ps[4 + b][:, :], ht_hi[:, s - 8, :], ht_lo[:, s - 8, :],
                                    m_hi[s % 4][:, cols], m_raw_r[s][:, cols], s == 8, s == 11)
                        if s == 11 and b < 3:
                            mm.then_inc(s_ybank, 1)
                    mm.then_inc(s_mused, 1)

        @block.scalar
        def _(act):
            ch = Chain(act, s_act)
            act.sem_inc(s_ev_a, 2)
            act.wait_ge(s_prep_pe, 1)
            ch.do(act.copy(cond_raw[:, :], ps[7][:, 0:ND]))
            ch.do(act.activation(cond_sig[:, :], ps[7][:, 0:ND], ACT.Sigmoid))
            ch.do(act.copy(g_pre[:, :, :].rearrange("p a t -> p (a t)"), ps[7][:, ND:3 * ND]))
            ch.do(act.copy(b_col[:, :], ps[7][:, 64:160]))
            ch.link(act.copy(conv_col[:, :], ps[7][:, 192:288]))
            act.sem_inc(s_row, 1)
            act.sem_inc(s_prep_a, 1)
            act.wait_ge(s_prep_v, 1)
            act.activation(sin_t[:, :], ang[:, 2, :], ACT.Sin).then_inc(s_prep_a, 1)
            act.activation(cos_t[:, :], ang[:, 3, :], ACT.Sin, scale=-1.0, bias=half_pi[0:ROPE, :]).then_inc(s_prep_a, 1)
            for m in range(NT):
                act.wait_ge(s_x, 16 * (NT + 1))
                ch.do(act.activation(area_1[:, m * 4:(m + 1) * 4, :].rearrange("p a b -> p (a b)"),
                                     x_all[:, m, :], ACT.Square, accum_out=ssq[:, m:m + 1]))
            ch.sync()
            act.activation(rstd[:, :], ssq[:, :], ACT.Sqrt, scale=1.0 / D, bias=eps[:, :]).then_inc(s_prep_a, 1)
            act.wait_ge(s_rstd, 1)
            for m in range(NT):
                act.activation(x_all[:, m, :], x_all[:, m, :], ACT.Identity, scale=rstd[:, m:m + 1]).then_inc(s_xn, 1)
            for t in range(ND):
                act.wait_ge(s_ut, t + 1)
                act.copy(area_1[:, t, :], ps[t % 4][:, :]).then_inc(s_xcol, 1)
            act.copy(ba_hi[:, :, :], w_ba[:, :, :]).then_inc(s_ba_split, 1)
            act.wait_ge(s_mod, N_ADA1)
            act.copy(mod_col[:, 0:2 * ND], ps[6][:, 0:2 * ND]).then_inc(s_prep_a, 1)

            def act_split(s, loaded, free):
                act.wait_ge(s_slot[s], loaded)
                act.wait_ge(s_used, free)
                act.copy(hi[s % 2][:, :], raw[s][:, :]).then_inc(s_hi, 1)

            for t in range(ND):
                act.wait_ge(s_utmp, t + 1)
                act.copy(u_hi[:, t, :], u_tmp[:, t % 2, :]).then_inc(s_uhi, 1)
                if t == 3:
                    act_split(0, N_ADA1 * 16 + 16, 3)
            done = ada_done = 0
            for col0, row0, n, natural, ada0 in PARTS:
                with act.Fori(0, n) as c:
                    for s in range(1, 5):
                        act_split(s % 4, (c + (N_ADA1 + done + s // 4)) * 16 + 16, (c + done) * 4 + (s + 3))
                    for b in range(2):
                        act.wait_ge(s_bank, (c + done) * 3 + (b + 1))
                        act.wait_ge(s_stored[b], (c + done) * 16)
                        act.copy(stage[:, b, :], ps[b][:, :]).then_inc(s_ev_a, 1)
                    if ada0 is not None:
                        act.wait_ge(s_mod, c + (N_ADA1 + ada_done + 1))
                        act.wait_ge(s_row_out, (c + ada_done) * 16)
                        act.copy(row_out[:, 0, :], ps[7][0:1, :]).then_inc(s_row, 1)
                if done == 0:
                    act.wait_ge(s_prep_pe, 2)
                    act.copy(ba[:, :, :].rearrange("p a b -> p (a b)"), ps[5][:, 0:NT * 16]).then_inc(s_prep_a, 1)
                done += n
                if ada0 is not None:
                    ada_done += n

            act.wait_ge(s_prep_v, 3)
            ch.link(act.activation(dec_in[:, 1, :, :], dec_in[:, 2, :, :], ACT.Exp))
            ch.link(act.activation(alog_row[:, :], alog_row[:, :], ACT.Exp))
            act.activation(dec_in[:, 2, :, :], dec_in[:, 1, :, :], ACT.Ln, bias=planes[:, C_ONES, 0:1]).then_inc(s_prep_a, 1)
            act.activation(beta[:, :, :], ba[:, :, 0:HEADS], ACT.Sigmoid).then_inc(s_prep_a, 1)
            act.wait_ge(s_prep_pe, 3)
            sums = ps[5][:, 0:2 * NT * HEADS].rearrange("p (a t h) -> p a t h", a=2, t=NT)
            ch.do(act.copy(gcum[:, :, :], sums[:, 0]))
            ch.do(act.activation(beta_g[:, :, :], sums[:, 0], ACT.Exp))
            act.activation(tail[:, :, :], sums[:, 1], ACT.Exp).then_inc(s_prep_a, 1)

            def dn_sigmoids(i):
                for n, j in enumerate((1, 0, 2)):
                    for par, d in enumerate(dn_heads):
                        act.wait_ge(s_conv, count(i, 3, n, par))
                        act.activation(d.xin[:, j, PAD:PAD + SEQ], d.cv[:, j, :], ACT.Sigmoid).then_inc(s_sig, 1)

            def dn_columns(i):
                for par, d in enumerate(dn_heads):
                    ch.do(act.copy(tiles(d.inv), column(g_nat, i * 2 + par)))
                    act.copy(tiles(d.inv_t), column(beta, i * 2 + par)).then_inc(s_gb, 1)

            def dn_turn(i, last):
                for n, j in enumerate((1, 0)):
                    for par, d in enumerate(dn_heads):
                        act.wait_ge(s_silu, count(i, 3, n, par))
                        act.activation(d.sq[:, j, :], d.cv[:, j, :], ACT.Square).then_inc(s_sq, 1)
                for n, j in enumerate((1, 0)):
                    for par, d in enumerate(dn_heads):
                        act.wait_ge(s_ss, count(i, 2, n, par))
                        act.activation(d.sq[:, j, :], (d.sb, d.tb)[j][:, :], ACT.Sqrt, bias=eps[:, :]).then_inc(s_nroot, 1)
                for par, d in enumerate(dn_heads):
                    act.wait_ge(s_gbc, count(i, 1, 0, par))
                    act.activation(d.e_g, d.xb[:, :], ACT.Exp).then_inc(s_eg, 1)
                for par, d in enumerate(dn_heads):
                    act.wait_ge(s_darg, count(i, 1, 0, par))
                    act.activation(d.dec, d.dec, ACT.Exp).then_inc(s_dec, 1)
                for par, d in enumerate(dn_heads):
                    act.wait_ge(s_inv1, count(i, 1, 0, par))
                    act.copy(d.inv, d.sb[:, :]).then_inc(s_inv1_out, 1)
                for n in range(NL):
                    for par, d in enumerate(dn_heads):
                        act.wait_ge(s_xm, count(i, NL, n, par))
                        if n == 0:
                            act.wait_ge(s_qkt, count(i, 1, 0, par))
                        act.copy(d.x_sb, d.xb[:, :]).then_inc(s_xc, 1)
                for par, d in enumerate(dn_heads):
                    act.wait_ge(s_uw, count(i, 1, 0, par))
                    act.copy(d.u_sol, d.tb[:, :]).then_inc(s_u, 1)
                act.wait_ge(s_dn_z, i * 32 + 32)
                for par, d in enumerate(dn_heads):
                    act.activation(d.z_sig, d.z_in, ACT.Sigmoid).then_inc(s_zsig, 1)
                if not last:
                    dn_sigmoids(i + 1)
                    dn_columns(i + 1)
                for par, d in enumerate(dn_heads):
                    act.wait_ge(s_sd, count(i, NC, NC - 1, par))
                    act.activation(d.n_t, d.tb[:, :], ACT.Square).then_inc(s_osq, 1)
                for par, d in enumerate(dn_heads):
                    act.wait_ge(s_oms, count(i, 1, 0, par))
                    act.activation(d.o_ms, d.o_ms, ACT.Sqrt, scale=1.0 / HD, bias=eps[:, :]).then_inc(s_oroot, 1)
                for par, d in enumerate(dn_heads):
                    act.wait_ge(s_ot, count(i, 1, 0, par))
                    act.copy(d.o_out, d.xb[:, :]).then_inc(s_ot_out, 1)

            dn_sigmoids(0)
            act.wait_ge(s_prep_v, 4)
            dn_columns(0)
            with ch.loop(HEADS // 2 - 1, 2) as i:
                dn_turn(i, False)
            dn_turn(HEADS // 2 - 1, True)
            act.wait_ge(s_yb, 16 * HEADS)
            with act.Fori(0, HEADS) as h:
                for m in range(NT):
                    act.wait_ge(s_nmax, h * NT + (max(m, 1) + 1))
                    act.wait_ge(s_pt, h)
                    act.activation(prob[:, m, 0:(m + 1) * P], at_scores[m], ACT.Exp, scale=SCALE,
                                   bias=at_max[:, m:m + 1], accum_out=at_sum[:, m:m + 1]).then_inc(s_exp, 1)
                act.wait_ge(s_pt, h + 1)
                act.wait_ge(s_av, h + 2)
                for k in range(NT):
                    act.copy(prob_t[:, k, k * P:SEQ], at_turned[k]).then_inc(s_pt_out, 1)
                act.wait_ge(s_av, h + 3)
                act.copy(yh[:, bass.ds(h, 1), :].rearrange("p a n -> p (a n)"), ps[4][:, :]).then_inc(s_av_out, 1)

            def sigmoid_row(c, b):
                act.wait_ge(s_gate[b % 2], (c * 2 + b // 2) * 32 + 32)
                g = gate_in[:, (b % 2) * 2:(b % 2) * 2 + 2, :]
                act.activation(g, g, ACT.Sigmoid).then_inc(s_gsig, 1)

            act.wait_ge(s_yl, 16)
            for q in range(2, 4):
                act.copy(yh[:, 4 * q:4 * q + 4, :], area_2[:, 4 * q:4 * q + 4, :]).then_inc(s_yh, 1)
            with act.Fori(0, 4) as c:
                for s in range(1, 5):
                    act_split(s % 4, (c + (N_ADA1 + N_IN + s // 4)) * 16 + 16, (c + N_IN) * 4 + (s + 3))
                    if s <= 2:
                        sigmoid_row(c, s - 1)
                for b in (2, 3):
                    sigmoid_row(c, b)
            act.wait_ge(s_used, 4 + 4 * (N_IN + 4))
            act.wait_ge(s_merged, 4 + 16)
            for q in range(4):
                act.copy(yh[:, 4 * q:4 * q + 4, :], merged[:, 4 * q:4 * q + 4, :]).then_inc(s_yh, 1)

            def project_out(c, last):
                for s in range(1, 4 if last else 5):
                    act_split(s % 4, (c + (N_ADA1 + N_IN + 4 + s // 4)) * 16 + 16, (c + (N_IN + 4)) * 4 + (s + 3))
                for b in range(2):
                    act.wait_ge(s_bank, (c + (N_IN + 4)) * 3 + (b + 1))
                    act.copy(y_nat[:, b, bass.ds(c * COLS, COLS)], ps[b][:, :]).then_inc(s_ev_a, 1)

            def square_out(c):
                act.wait_ge(s_ev_a, c * 2 + (2 * N_IN + 4))
                act.wait_ge(s_ev_v, c * 2 + (2 * N_IN + 4))
                for b in range(NT):
                    ch.link(act.activation(acc[:, 0, :], y_nat[:, b, bass.ds(c * COLS, COLS)], ACT.Square,
                                           accum_out=ss_y[:, b, bass.ds(c, 1)]))

            with ch.loop(3, NT) as c:
                project_out(c, False)
                square_out(c)
            project_out(3, True)
            square_out(3)
            act.sem_inc(s_ysq, 1)
            act.wait_ge(s_ysum, 1)
            act.activation(ss2[:, 0, :], ss2[:, 0, :], ACT.Sqrt, scale=1.0 / D, bias=eps[:, :]).then_inc(s_rooty, 1)

            def root_x1(m):
                act.wait_ge(s_x1, m + 1)
                ch.link(act.activation(u2_nat[:, m, :], y_nat[:, m, :], ACT.Square, accum_out=ss2[:, 1, m:m + 1]))
                act.activation(ss2[:, 1, m:m + 1], ss2[:, 1, m:m + 1], ACT.Sqrt, scale=1.0 / D, bias=eps[:, :]).then_inc(s_root1, 1)

            root_x1(0)
            for m in range(NT):
                if m + 1 < NT:
                    root_x1(m + 1)
                for q in range(4):
                    act.wait_ge(s_u2t, 4 * m + q + 1)
                    act.copy(u2_t[:, 4 * q:4 * q + 4, m * P:(m + 1) * P], ps[q][:, :].rearrange("p (a n) -> p a n", a=4)).then_inc(s_u2t_out, 1)
            act.wait_ge(s_route_v, 1)
            act.activation(tmp4, tmp4, ACT.Exp).then_inc(s_route_a, 1)
            act.wait_ge(s_route_v, 2)
            act.activation(r1[:, 4, :], r1[:, 4, :], ACT.Exp).then_inc(s_route_a, 1)

            def expert_hi(j, x):
                act.wait_ge(s_mslot[x % 12], j * 16 + (mslot_base[x % 12] + 16 * (x // 12) + 16))
                act.wait_ge(s_mused, j * 12 + (x + 9))
                act.copy(m_hi[x % 4], m_raw[x % 12]).then_inc(s_mhi, 1)

            def rows_hi(n):
                for q in range(4):
                    act.wait_ge(s_xt, n + (q + 1))
                    act.copy(xe_hi[:, 4 * q:4 * q + 4, :].rearrange("p a b -> p (a b)"), ps[2 + q % 2][:, :]).then_inc(s_xehi, 1)

            act.wait_ge(s_ysplit, 6)
            for x in range(3):
                expert_hi(0, x)
            act.wait_ge(s_route_v, 6)
            last_block = act.value_load(plan[0:1, MAX_OVER + 1:MAX_OVER + 2], min_val=EXPERTS - 1, max_val=NB - 1)
            rows_hi(0)
            def block_turn(j, last):
                for x in range(3, 8):
                    expert_hi(j, x)
                act.wait_ge(s_mused, j * 12 + 16)
                act.activation(h_sig, ps[0][:, :], ACT.Sigmoid).then_inc(s_hsig, 1)
                for x in range(8, 11):
                    expert_hi(j, x)
                rows_hi(j * 4 + 4)
                act.wait_ge(s_ht, j + 1)
                act.copy(ht_hi.rearrange("p a b -> p (a b)"), ps[0][:, :]).then_inc(s_hthi, 1)
                for x in range(11, 12 if last else 15):
                    expert_hi(j, x)
                act.wait_ge(s_ysc, j * 16)
                for b in range(2):
                    act.wait_ge(s_ybank, j * 3 + (b + 1))
                    act.copy(y_e[:, b * COLS:(b + 1) * COLS], ps[4 + b][:, :]).then_inc(s_ye_a, 1)

            with act.Fori(0, last_block) as j:
                block_turn(j, False)
            block_turn(last_block, True)
            for m in range(NT):
                act.wait_ge(s_f_y, m + 1)
                ch.link(act.activation(f_sq, f_y[m][0], ACT.Square, accum_out=ss_f[:, m:m + 1]))
                act.activation(ss_f[:, m:m + 1], ss_f[:, m:m + 1], ACT.Sqrt, scale=1.0 / D, bias=eps[:, :]).then_inc(s_f_ss, 1)

        @block.vector
        def _(dve):
            ch = Chain(dve, s_dve)
            dve.sem_inc(s_ev_v, 2)
            dve.sem_inc(s_ada1_used, 4)
            dve.sem_inc(s_ada_used, 4)
            ch.do(dve.memset(half_pi[:, :], float(np.pi / 2)))
            ch.do(dve.memset(eps[:, :], EPS))
            dve.wait_ge(s_const, 16 * 8)
            ch.link(dve.tensor_copy(ang[:, 0, :], pos_i[:, :]))
            ch.link(dve.tensor_scalar(ang[:, 0, :], ang[:, 0, :], small[0:ROPE, 33:34], None, ALU.mult))
            ch.link(dve.tensor_scalar(ang[:, 1, :], ang[:, 0, :], float(1 / (2 * np.pi)), None, ALU.mult))
            ch.link(dve.tensor_scalar(ang[:, 1, :], ang[:, 1, :], ROUND, None, ALU.add))
            ch.link(dve.tensor_scalar(ang[:, 1, :], ang[:, 1, :], -ROUND, None, ALU.add))
            for part in (TWO_PI_1, TWO_PI_2, TWO_PI_3):
                ch.link(dve.scalar_tensor_tensor(ang[:, 0, :], ang[:, 1, :], -part, ang[:, 0, :], ALU.mult, ALU.add))
            ch.link(dve.tensor_scalar(ang[:, 2, :], ang[:, 0, :], -PI_BELOW, PI_BELOW, ALU.max, ALU.min))
            ch.link(dve.tensor_scalar(ang[:, 1, :], ang[:, 2, :], -1.0, None, ALU.mult))
            dve.tensor_tensor(ang[:, 3, :], ang[:, 1, :], ang[:, 2, :], ALU.max).then_inc(s_prep_v, 1)
            dve.wait_ge(s_prep_a, 1)
            ch.link(dve.tensor_tensor(cond[:, :], cond_raw[:, :], cond_sig[:, :], ALU.mult))

            def accumulate(ring, s, par, slot_done, used):
                for t in range(4):
                    w = ring[s][:, t * COLS:(t + 1) * COLS]
                    k = 4 * s + t
                    if k == 0:
                        ins = dve.tensor_scalar(acc[:, par, :], w, cond[:, 0:1], None, ALU.mult)
                    else:
                        ins = dve.scalar_tensor_tensor(acc[:, par, :], w, cond[:, k:k + 1], acc[:, par, :], ALU.mult, ALU.add)
                    if t < 3:
                        ch.link(ins)
                    else:
                        ins.then_inc(used, 1)
                        dve.wait_ge(used, slot_done)

            def ada1_pair(i):
                for par in range(2):
                    for s in range(4):
                        dve.wait_ge(s_slot[s], (i * 2 + par) * 16 + 16)
                        accumulate([r[:, :] for r in raw], s, par, (i * 2 + par) * 4 + (s + 5), s_ada1_used)
                    dve.sem_inc(s_acc, 1)
                    dve.wait_ge(s_mod, i * 2 + par)

            ada1_pair(0)
            dve.wait_ge(s_prep_a, 4)
            dve.reciprocal(rstd[:, :], rstd[:, :]).then_inc(s_rstd, 1)
            with ch.loop(N_ADA1 // 2 - 1, 24) as i:
                ada1_pair(i + 1)
            dve.wait_ge(s_ba_split, 1)
            dve.tensor_tensor(ba_lo[:, :, :], w_ba[:, :, :], ba_hi[:, :, :].bitcast(F32), ALU.subtract).then_inc(s_ba_split, 1)
            dve.wait_ge(s_prep_a, 5)
            ch.link(dve.tensor_tensor(mod_col[:, 0:2 * ND], mod_col[:, 0:2 * ND], b_col[:, 0:2 * ND], ALU.add))
            dve.scalar_tensor_tensor(a_col[:, 0, :], mod_col[:, ND:2 * ND], 1.0, g_pre[:, 0, :], ALU.add, ALU.mult).then_inc(s_prep_v, 1)
            dve.wait_ge(s_prep_v, 2)
            dve.wait_ge(s_xcol, ND)

            def dve_split(s, ready):
                dve.wait_ge(s_hi, ready)
                dve.tensor_tensor(raw_r[s][:, :], raw[s][:, :], hi[s % 2][:, :].bitcast(F32),
                                  ALU.subtract).then_inc(s_lo, 1)

            def u_block(t):
                if t >= 2:
                    dve.wait_ge(s_ulo, t - 1)
                dve.tensor_scalar(u_tmp[:, t % 2, :], area_1[:, t, :], a_col[:, 0, t:t + 1], mod_col[:, t:t + 1],
                                  ALU.mult, ALU.add).then_inc(s_utmp, 1)

            u_block(0)
            for t in range(ND):
                if t + 1 < ND:
                    u_block(t + 1)
                dve.wait_ge(s_uhi, t + 1)
                dve.tensor_tensor(u_lo[:, t, :], u_tmp[:, t % 2, :], u_hi[:, t, :].bitcast(F32), ALU.subtract).then_inc(s_ulo, 1)
                if t == 4:
                    dve_split(0, 1)
            dve.wait_ge(s_ulo, ND)

            done = ada_done = 0
            for col0, row0, n, natural, ada0 in PARTS:
                with ch.loop(n, 12 if ada0 is not None else 0) as c:
                    for s in range(4):
                        dve_split((s + 1) % 4, (c + done) * 4 + (s + 2))
                        if ada0 is not None:
                            if s == 0:
                                dve.wait_ge(s_mod, c + (N_ADA1 + ada_done))
                            dve.wait_ge(s_ada_slot[s], (c + ada_done) * 16 + 16)
                            accumulate(ada_ring, s, 0, (c + ada_done) * 4 + (s + 5), s_ada_used)
                    if ada0 is not None:
                        dve.sem_inc(s_acc, 1)
                    for b in range(2, 4):
                        if b == 2:
                            dve.wait_ge(s_bank, (c + done) * 3 + 3)
                        else:
                            dve.wait_ge(s_used, (c + done) * 4 + 8)
                        dve.wait_ge(s_stored[b], (c + done) * 16)
                        dve.tensor_copy(stage[:, b, :], ps[b][:, :]).then_inc(s_ev_v, 1)
                done += n
                if ada0 is not None:
                    ada_done += n

            dve.wait_ge(s_rows, 16 * 3)
            dve.wait_ge(s_prep_a, 6)
            ch.link(dve.tensor_tensor(dec_in[:, 0, :, :], ba[:, :, HEADS:2 * HEADS],
                                      dtb_row[:, :].rearrange("p (a h) -> p a h", a=1).broadcast_to([P, NT, HEADS]), ALU.add))
            ch.link(dve.tensor_scalar(dec_in[:, 1, :, :], dec_in[:, 0, :, :], -1.0, None, ALU.mult))
            dve.tensor_tensor(dec_in[:, 2, :, :], dec_in[:, 0, :, :], dec_in[:, 1, :, :], ALU.min).then_inc(s_prep_v, 1)
            dve.wait_ge(s_prep_a, 8)
            ch.link(dve.scalar_tensor_tensor(dec_in[:, 3, :, :], dec_in[:, 0, :, :], 0.0, dec_in[:, 2, :, :], ALU.max, ALU.add))
            ch.link(dve.tensor_scalar(dec_in[:, 3, :, :], dec_in[:, 3, :, :], -1.0, None, ALU.mult))
            dve.tensor_tensor(g_nat[:, :, :], dec_in[:, 3, :, :],
                              alog_row[:, :].rearrange("p (a h) -> p a h", a=1).broadcast_to([P, NT, HEADS]), ALU.mult).then_inc(s_prep_v, 1)
            dve.wait_ge(s_prep_a, 9)
            ch.link(dve.tensor_tensor(beta_g[:, :, :], beta_g[:, :, :], beta[:, :, :], ALU.mult))

            CONV_STEPS = 2 * 3 * (CONV + 1)

            def dn_conv(i, step):
                par = step % 2
                d = dn_heads[par]
                if step < 2 * 3 * CONV:
                    n, k = step // (2 * CONV), step // 2 % CONV
                    j = (1, 0, 2)[n]
                    if step == 0:
                        dve.wait_ge(s_dn_in, i * 32 + 32)
                    w = conv_col[:, bass.ds(i * 2 + (k * 3 * HEADS + j * HEADS + par), 1)]
                    src = d.xin[:, j, k:k + SEQ]
                    if k == 0:
                        ch.do(dve.tensor_scalar(d.cv[:, j, :], src, w, None, ALU.mult))
                        return
                    ch.sync(but=0 if par and k == CONV - 1 else 1)
                    ins = dve.scalar_tensor_tensor(d.cv[:, j, :], src, w, d.cv[:, j, :], ALU.mult, ALU.add)
                    if k < CONV - 1:
                        ch.do(ins)
                    else:
                        ins.then_inc(s_conv, 1)
                else:
                    n = step // 2 - 3 * CONV
                    j = (1, 0, 2)[n]
                    dve.wait_ge(s_sig, count(i, 3, n, par))
                    dve.tensor_tensor(d.cv[:, j, :], d.cv[:, j, :], d.xin[:, j, PAD:PAD + SEQ], ALU.mult).then_inc(s_silu, 1)

            def dn_turn(i, last):
                for n, j in enumerate((1, 0)):
                    for par, d in enumerate(dn_heads):
                        dve.wait_ge(s_nroot, count(i, 2, n, par))
                        ch.do(dve.reciprocal(d.sq[:, j, :], d.sq[:, j, :]))
                    for par, d in enumerate(dn_heads):
                        ch.sync(but=1 - par)
                        dve.scalar_tensor_tensor(d.cv[:, j, :], d.cv[:, j, :], 1.0 if j else HD ** -0.5, d.sq[:, j, :],
                                                 ALU.mult, ALU.mult).then_inc(s_unit, 1)
                for par, d in enumerate(dn_heads):
                    dve.wait_ge(s_bbc, count(i, 1, 0, par))
                    dve.wait_ge(s_unit, count(i, 2, 0, par))
                    dve.tensor_tensor(d.kb, d.cv[:, 1, :], d.tb[:, :], ALU.mult).then_inc(s_kb, 1)
                for par, d in enumerate(dn_heads):
                    dve.wait_ge(s_eg, count(i, 1, 0, par))
                    for t in range(NT):
                        c = slice(t * P, (t + 1) * P)
                        ins = dve.scalar_tensor_tensor(d.dec[:, c], d.xb[:, c], gcum[:, t, bass.ds(i * 2 + par, 1)], planes[:, C_DEC, :],
                                                       ALU.subtract, ALU.add)
                        ins.then_inc(s_darg, 1) if t == NT - 1 else ch.do(ins)
                for par, d in enumerate(dn_heads):
                    dve.wait_ge(s_unit, count(i, 2, 1, par))
                    ch.do(dve.tensor_tensor(d.q_dec, d.cv[:, 0, :], d.e_g, ALU.mult))
                    ch.do(dve.tensor_copy(d.g_last, d.e_g[:, CHUNK - 1::CHUNK]))
                dve.wait_ge(s_yb, i * 32)
                for par, d in enumerate(dn_heads):
                    dve.wait_ge(s_dec, count(i, 1, 0, par))
                    dve.wait_ge(s_gram, count(i, 2, 0, par))
                    dve.tensor_tensor(d.n_t, d.sb[:, :], d.dec, ALU.mult).then_inc(s_nt, 1)
                for par, d in enumerate(dn_heads):
                    dve.wait_ge(s_gram, count(i, 2, 1, par))
                    dve.tensor_tensor(d.qk_t, d.tb[:, :], d.dec, ALU.mult).then_inc(s_qkt, 1)
                for par, d in enumerate(dn_heads):
                    dve.wait_ge(s_nt, count(i, 1, 0, par))
                    dve.wait_ge(s_gbc, count(i, 1, 0, par))
                    dve.wait_ge(s_bbc, count(i, 1, 0, par))
                    ch.do(dve.tensor_tensor(tiles(d.inv_t), tiles(d.n_t), plane(C_LEV), ALU.mult))
                for par, d in enumerate(dn_heads):
                    ch.sync(but=1 - par)
                    dve.tensor_tensor(tiles(d.inv_t), plane(C_ID), tiles(d.inv_t), ALU.subtract).then_inc(s_first, 1)
                for par, d in enumerate(dn_heads):
                    dve.wait_ge(s_knat, count(i, 1, 0, par))
                    ch.do(dve.tensor_tensor(d.k_bg, tiles(d.xb[:, :]), column(beta_g, i * 2 + par), ALU.mult))
                    dve.tensor_tensor(d.k_tail, tiles(d.xb[:, :]), column(tail, i * 2 + par), ALU.mult).then_inc(s_kfac, 1)
                for par, d in enumerate(dn_heads):
                    dve.wait_ge(s_vnat, count(i, 1, 0, par))
                    dve.tensor_tensor(d.v_b, tiles(d.tb[:, :]), column(beta, i * 2 + par), ALU.mult).then_inc(s_vb, 1)
                for n in range(NL):
                    for par, d in enumerate(dn_heads):
                        dve.wait_ge(s_corr, count(i, NL, n, par))
                        dve.wait_ge(s_inv if n else s_first, count(i, NL if n else 1, n - 1 if n else 0, par))
                        ins = dve.tensor_tensor(d.inv_t, d.inv_t, d.tb[:, :], ALU.subtract)
                        if n < NL - 1:
                            ch.do(ins)
                            ins = dve.tensor_tensor(d.inv, d.inv, d.sb[:, :], ALU.subtract)
                        ins.then_inc(s_inv, 1)
                for par, d in enumerate(dn_heads):
                    dve.wait_ge(s_uw, count(i, 1, 0, par))
                    dve.tensor_copy(d.w_t, d.sb[:, :]).then_inc(s_w, 1)
                for c in range(NC):
                    r, t = slice((c % 2) * CHUNK, (c % 2 + 1) * CHUNK), c // 2
                    if c:
                        for par, d in enumerate(dn_heads):
                            dve.wait_ge(s_ws, count(i, NC - 1, c - 1, par))
                            if c == 1:
                                dve.wait_ge(s_u, count(i, 1, 0, par))
                            dve.tensor_tensor(d.v_new[r, :], d.u_sol[r, t * HD:(t + 1) * HD], d.xb[r, 0:HD], ALU.subtract).then_inc(s_vn, 1)
                    if not last:
                        for step in range(4 * c, min(4 * c + 2, CONV_STEPS)):
                            dn_conv(i + 1, step)
                    for par, d in enumerate(dn_heads):
                        dve.wait_ge(s_sd, count(i, NC, c, par))
                        if c == 0:
                            dve.tensor_copy(d.state, d.sb[:, 0:HD]).then_inc(s_state, 1)
                        else:
                            dve.wait_ge(s_state, count(i, NC, c - 1, par))
                            dve.scalar_tensor_tensor(d.state, d.state, d.g_last[:, c:c + 1], d.sb[:, 0:HD],
                                                     ALU.mult, ALU.add).then_inc(s_state, 1)
                    if not last:
                        for step in range(4 * c + 2, min(4 * c + 4, CONV_STEPS)):
                            dn_conv(i + 1, step)
                for par, d in enumerate(dn_heads):
                    dve.wait_ge(s_osq, count(i, 1, 0, par))
                    dve.tensor_reduce(d.o_ms, tiles(d.n_t), AX, ALU.add).then_inc(s_oms, 1)
                for par, d in enumerate(dn_heads):
                    dve.wait_ge(s_oroot, count(i, 1, 0, par))
                    ch.do(dve.reciprocal(d.o_ms, d.o_ms))
                for par, d in enumerate(dn_heads):
                    ch.sync(but=1)
                    ch.do(dve.tensor_tensor(tiles(d.o_out), tiles(d.tb[:, :]), d.o_ms.rearrange("p (t a) -> p t a", a=1).broadcast_to([P, NT, HD]), ALU.mult))
                for par, d in enumerate(dn_heads):
                    ch.sync(but=1 - par)
                    dve.wait_ge(s_zgain, count(i, 1, 0, par))
                    dve.tensor_tensor(tiles(d.o_out), tiles(d.o_out), d.z_sig, ALU.mult).then_inc(s_on, 1)

            for step in range(CONV_STEPS):
                dn_conv(0, step)
            with ch.loop(HEADS // 2 - 1, 48) as i:
                dn_turn(i, False)
            dn_turn(HEADS // 2 - 1, True)

            def at_rope(par, h):
                for n, (bank, x) in enumerate(((ps[0], at_q[par]), (ps[7], at_k[par]))):
                    dve.wait_ge(s_rot, h * 2 + (n + 1))
                    ch.link(dve.tensor_tensor(rot[0:ROPE, :], bank[0:ROPE, :], sin_t[:, :], ALU.mult))
                    if n == 0:
                        dve.wait_ge(s_rot, h * 2 + 2)
                    ch.link(dve.tensor_tensor(x[0:ROPE, :], x[0:ROPE, :], cos_t[:, :], ALU.mult))
                    dve.tensor_tensor(x[0:ROPE, :], x[0:ROPE, :], rot[0:ROPE, :], ALU.add).then_inc(s_roped, 1)
                    dve.wait_ge(s_roped, h * 2 + (n + 1))

            def at_softmax(h):
                for m in range(NT):
                    dve.wait_ge(s_sc, h * NT + (max(m, 1) + 1))
                    diag = at_scores[m][:, m * P:(m + 1) * P]
                    ch.link(dve.tensor_tensor(diag, diag, planes[:, C_CAUSAL, :], ALU.add))
                    ch.link(dve.reduce_max(at_raw[:, m:m + 1], at_scores[m], AX))
                    dve.tensor_scalar(at_max[:, m:m + 1], at_raw[:, m:m + 1], -SCALE, None, ALU.mult).then_inc(s_nmax, 1)
                for m in range(NT):
                    dve.wait_ge(s_exp, h * NT + (m + 1))
                    ch.link(dve.reciprocal(at_sum[:, m:m + 1], at_sum[:, m:m + 1]))
                    dve.tensor_scalar(prob[:, m, 0:(m + 1) * P], prob[:, m, 0:(m + 1) * P], at_sum[:, m:m + 1], None,
                                      ALU.mult).then_inc(s_prob, 1)

            def at_low(h):
                dve.wait_ge(s_av_out, h + 1)
                part = yl[:, bass.ds(h, 1), :].rearrange("p a n -> p (a n)")
                high = yh[:, bass.ds(h, 1), :].rearrange("p a n -> p (a n)").bitcast(F32)
                dve.tensor_tensor(part, ps[4][:, :], high, ALU.subtract).then_inc(s_av_lo, 1)

            at_rope(0, 0)
            with ch.loop(HEADS // 2 - 1, 2 * 16) as i:
                for par in range(2):
                    h = i * 2 + par
                    at_softmax(h)
                    at_rope(1 - par, h + 1)
                    at_low(h)
            for h in range(HEADS - 2, HEADS):
                at_softmax(h)
                if h == HEADS - 2:
                    at_rope(1, h + 1)
                at_low(h)

            dve.wait_ge(s_mr, 16 * 5)
            ch.link(dve.tensor_tensor(mr[:, :, :], mr[:, :, :], br[:, :, :], ALU.add))
            ch.do(dve.tensor_tensor(mr[:, 0, :], mr[:, 0, :], gr[:, 0, :], ALU.mult))
            ch.do(dve.scalar_tensor_tensor(mr[:, 2, :], mr[:, 2, :], 1.0, gr[:, 1, :], ALU.add, ALU.mult))
            dve.tensor_tensor(mr[:, 3, :], mr[:, 3, :], gr[:, 2, :], ALU.mult).then_inc(s_res, 1)

            for q in range(2, 4):
                dve.wait_ge(s_yh, q - 1)
                dve.tensor_tensor(yl[:, 4 * q:4 * q + 4, :], area_2[:, 4 * q:4 * q + 4, :],
                                  yh[:, 4 * q:4 * q + 4, :].bitcast(F32), ALU.subtract).then_inc(s_ysplit, 1)
            dve.sem_inc(s_merged, 4)
            with ch.loop(4, 8) as c:
                for s in range(4):
                    dve_split((s + 1) % 4, (c + N_IN) * 4 + (s + 2))
                for b in range(4):
                    g = gate_in[:, (b % 2) * 2, :], gate_in[:, (b % 2) * 2 + 1, :]
                    dve.wait_ge(s_gsig, c * 4 + (b + 1))
                    if b < 3:
                        dve.wait_ge(s_bank, (c + N_IN) * 3 + (b + 1))
                    else:
                        dve.wait_ge(s_used, (c + N_IN) * 4 + 8)
                    ch.do(dve.tensor_tensor(g[0], g[0], ps[b][:, :], ALU.mult))
                    ch.link(dve.tensor_tensor(g[1], g[1], ps[4 + b][:, :], ALU.mult))
                    dve.tensor_tensor(merged[:, bass.ds(c * 4 + b, 1), :].rearrange("p a n -> p (a n)"), g[0], g[1],
                                      ALU.add).then_inc(s_merged, 1)
            for q in range(4):
                dve.wait_ge(s_yh, q + 3)
                dve.tensor_tensor(yl[:, 4 * q:4 * q + 4, :], merged[:, 4 * q:4 * q + 4, :],
                                  yh[:, 4 * q:4 * q + 4, :].bitcast(F32), ALU.subtract).then_inc(s_ysplit, 1)

            def project_out(c, last):
                for s in range(3 if last else 4):
                    dve_split((s + 1) % 4, (c + (N_IN + 4)) * 4 + (s + 2))
                for b in range(2, 4):
                    if b == 2:
                        dve.wait_ge(s_bank, (c + (N_IN + 4)) * 3 + 3)
                    else:
                        dve.wait_ge(s_used, (c + (N_IN + 4)) * 4 + 8)
                    dve.tensor_copy(y_nat[:, b, bass.ds(c * COLS, COLS)], ps[b][:, :]).then_inc(s_ev_v, 1)

            with dve.Fori(0, 3) as c:
                project_out(c, False)
            project_out(3, True)

            dve.wait_ge(s_ysq, 1)
            dve.tensor_reduce(ss2[:, 0, :], ss_y[:, :, :], AX, ALU.add).then_inc(s_ysum, 1)
            dve.wait_ge(s_rooty, 1)
            ch.link(dve.reciprocal(ss2[:, 0, :], ss2[:, 0, :]))
            dve.wait_ge(s_rowb, 16 * 7)
            dve.wait_ge(s_xin2, 16 * NT)

            def first_residual(m):
                ch.link(dve.scalar_tensor_tensor(y_nat[:, m, :], y_nat[:, m, :], ss2[:, 0, m:m + 1], row_g1, ALU.mult, ALU.mult))
                dve.tensor_tensor(y_nat[:, m, :], y_nat[:, m, :], raw[m][:, :], ALU.add).then_inc(s_x1, 1)

            def second_input(m):
                dve.wait_ge(s_root1, m + 1)
                ch.link(dve.reciprocal(ss2[:, 1, m:m + 1], ss2[:, 1, m:m + 1]))
                ch.link(dve.scalar_tensor_tensor(u2_nat[:, m, :], y_nat[:, m, :], ss2[:, 1, m:m + 1], row_a2, ALU.mult, ALU.mult))
                dve.tensor_tensor(u2_nat[:, m, :], u2_nat[:, m, :], row_s2, ALU.add).then_inc(s_u2, 1)

            first_residual(0)
            for m in range(NT):
                if m + 1 < NT:
                    first_residual(m + 1)
                second_input(m)

            def over_tiles(x, n):
                return x.rearrange("p (t a) -> p t a", a=1).broadcast_to([P, NT, n])

            def numbers(n):
                return small[:, 0:n].rearrange("p (a e) -> p a e", a=1).broadcast_to([P, NT, n])

            def first_of_max(x, best, one_hot, scratch, index, n):
                ch.link(dve.tensor_reduce(best, x, AX, ALU.max))
                ch.link(dve.tensor_tensor(scratch, x, over_tiles(best, n), ALU.is_equal))
                ch.link(dve.tensor_scalar(scratch, scratch, -1000.0, 1000.0, ALU.mult, ALU.add))
                ch.link(dve.tensor_tensor(scratch, scratch, numbers(n), ALU.add))
                ch.link(dve.tensor_reduce(index, scratch, AX, ALU.min))
                ch.link(dve.tensor_tensor(one_hot, numbers(n), over_tiles(index, n), ALU.is_equal))

            def look_up(dst, values, one_hot, n):
                ch.link(dve.tensor_tensor(tmp32, values, one_hot, ALU.mult))
                ch.link(dve.tensor_reduce(dst, tmp32, AX, ALU.add))

            dve.wait_ge(s_logit, 1)
            ch.link(dve.tensor_tensor(logit, ps[4][:, 0:NT * NR].rearrange("p (t n) -> p t n", t=NT),
                                      b_r[:, :].rearrange("p (a n) -> p a n", a=1).broadcast_to([P, NT, NR]), ALU.add))
            g_log = logit[:, :, 0:GROUPS]
            first_of_max(g_log, r1[:, 0, :], oh_g, tmp4, r1[:, 1, :], GROUPS)
            dve.tensor_tensor(tmp4, g_log, over_tiles(r1[:, 0, :], GROUPS), ALU.subtract).then_inc(s_route_v, 1)
            ch.link(dve.tensor_scalar(oh_g, oh_g, -NEG, NEG, ALU.mult, ALU.add))
            for g in range(GROUPS):
                ch.do(dve.tensor_tensor(e_log[:, :, g * PER_GROUP:(g + 1) * PER_GROUP],
                                        logit[:, :, GROUPS + g * PER_GROUP:GROUPS + (g + 1) * PER_GROUP],
                                        oh_g[:, :, g:g + 1].broadcast_to([P, NT, PER_GROUP]), ALU.add))
            ch.sync()
            first_of_max(e_log, r1[:, 2, :], oh1, tmp32, r1[:, 5, :], EXPERTS)
            ch.link(dve.tensor_scalar(tmp32, oh1, 2 * NEG, None, ALU.mult))
            ch.link(dve.tensor_tensor(e_log, e_log, tmp32, ALU.add))
            first_of_max(e_log, r1[:, 3, :], oh2, tmp32, r1[:, 6, :], EXPERTS)
            dve.tensor_tensor(r1[:, 4, :], r1[:, 3, :], r1[:, 2, :], ALU.subtract).then_inc(s_route_v, 1)
            dve.tensor_tensor(both, oh1, oh2, ALU.add).then_inc(s_route_v, 1)
            dve.wait_ge(s_route_a, 1)
            ch.link(dve.tensor_reduce(r1[:, 7, :], tmp4, AX, ALU.add))
            dve.wait_ge(s_route_a, 2)
            ch.link(dve.tensor_scalar(r1[:, 8, :], r1[:, 4, :], 1.0, None, ALU.add))
            ch.link(dve.tensor_tensor(r1[:, 8, :], r1[:, 8, :], r1[:, 7, :], ALU.mult))
            ch.link(dve.reciprocal(wts[:, 0, :], r1[:, 8, :]))
            ch.link(dve.tensor_tensor(wts[:, 1, :], wts[:, 0, :], r1[:, 4, :], ALU.mult))
            dve.wait_ge(s_route_pe, 1)
            ch.do(dve.tensor_copy(rank, ps[5][:, 0:NT * EXPERTS].rearrange("p (t e) -> p t e", t=NT)))
            ch.link(dve.tensor_copy(cnt[:, 0, :], ps[6][:, 0:EXPERTS]))
            ch.link(dve.tensor_scalar(cnt[:, 1, :], cnt[:, 0, :], float(ROWS), None, ALU.is_gt))
            for q in (2, 3):
                ch.link(dve.tensor_scalar(cnt[:, 2, :], cnt[:, 0, :], float(q * ROWS), None, ALU.is_gt))
                ins = dve.tensor_tensor(cnt[:, 1, :], cnt[:, 1, :], cnt[:, 2, :], ALU.add)
                ch.link(ins) if q == 2 else ins.then_inc(s_route_v, 1)
            dve.wait_ge(s_route_pe, 2)
            dve.tensor_copy(over_t[0:EXPERTS, :], ps[7][0:EXPERTS, 0:P]).then_inc(s_route_v, 1)
            dve.wait_ge(s_route_pe, 3)
            ch.link(dve.tensor_scalar(cnt[:, 2, :], ps[5][:, 256:256 + EXPERTS], float(EXPERTS), None, ALU.add))
            ch.link(dve.tensor_tensor(cnt[:, 3, :], cnt[:, 2, :], cnt[:, 1, :], ALU.add))
            ch.link(dve.tensor_tensor(tmp7, cnt[:, 3:4, :].broadcast_to([P, MAX_OVER, EXPERTS]),
                                      small[:, 40:40 + MAX_OVER].rearrange("p (n a) -> p n a", a=1).broadcast_to([P, MAX_OVER, EXPERTS]),
                                      ALU.is_le))
            ch.link(dve.tensor_reduce(plan_f[:, 0:MAX_OVER], tmp7, AX, ALU.add))
            ch.link(dve.tensor_scalar(plan_f[:, 0:MAX_OVER], plan_f[:, 0:MAX_OVER], float(EXPERTS - 1), None, ALU.min))
            ch.link(dve.tensor_copy(plan_f[:, MAX_OVER:MAX_OVER + 1], cnt[:, 3, EXPERTS - 1:EXPERTS]))
            ch.link(dve.tensor_scalar(plan_f[:, MAX_OVER + 1:MAX_OVER + 2], plan_f[:, MAX_OVER:MAX_OVER + 1], -1.0, None, ALU.add))
            ch.do(dve.tensor_copy(plan[:, :], plan_f[:, :]))
            ch.sync()
            dve.sem_inc(s_route_v, 1)
            base = cnt[:, 2:3, :].broadcast_to([P, NT, EXPERTS])
            for k, one_hot in enumerate((oh1, oh2)):
                look_up(r1[:, 9, :], rank, one_hot, EXPERTS)
                look_up(r1[:, 10, :], base, one_hot, EXPERTS)
                ch.link(dve.tensor_scalar(r1[:, 11, :], r1[:, 9, :], float(ROWS), None, ALU.is_ge))
                ch.link(dve.tensor_copy(r1[:, 12, :], r1[:, 11, :]))
                for q in (2, 3):
                    ch.link(dve.tensor_scalar(r1[:, 13, :], r1[:, 9, :], float(q * ROWS), None, ALU.is_ge))
                    ch.link(dve.tensor_tensor(r1[:, 12, :], r1[:, 12, :], r1[:, 13, :], ALU.add))
                ch.link(dve.tensor_tensor(r1[:, 10, :], r1[:, 10, :], r1[:, 12, :], ALU.add))
                ch.link(dve.scalar_tensor_tensor(r1[:, 10, :], r1[:, 10, :], -1.0, r1[:, 5 + k, :], ALU.add, ALU.subtract))
                ch.link(dve.tensor_tensor(r1[:, 10, :], r1[:, 10, :], r1[:, 11, :], ALU.mult))
                ch.link(dve.tensor_tensor(r1[:, 10, :], r1[:, 10, :], r1[:, 5 + k, :], ALU.add))
                ch.link(dve.scalar_tensor_tensor(r1[:, 9, :], r1[:, 12, :], -float(ROWS), r1[:, 9, :], ALU.mult, ALU.add))
                ch.link(dve.scalar_tensor_tensor(place[:, k, :], r1[:, 9, :], float(NB + 1), r1[:, 10, :], ALU.mult, ALU.add))
                for m in range(NT):
                    ch.do(dve.tensor_scalar(r1[:, 14 + k, m:m + 1], small[:, 32:33], float(m * P + k * SEQ), None, ALU.add))
                ch.sync()
            dve.tensor_copy(place_i[:, :], place.rearrange("p k t -> p (k t)")).then_inc(s_route_v, 1)
            dve.tensor_copy(id_i[:, :], r1[:, 14:16, :].rearrange("p k t -> p (k t)")).then_inc(s_route_v, 1)
            dve.wait_ge(s_table, 32 + 16 * 2 * NT)
            ch.link(dve.tensor_copy(row_f[:, :], row_i[:, :]))
            ch.link(dve.tensor_scalar(tok_f[:, :], row_f[:, :], float(SEQ), -float(SEQ), ALU.is_ge, ALU.mult))
            ch.link(dve.tensor_tensor(tok_f[:, :], tok_f[:, :], row_f[:, :], ALU.add))
            dve.tensor_copy(tok_i[:, :], tok_f[:, :]).then_inc(s_route_v, 1)

            def expert_lo(j, x):
                dve.wait_ge(s_mhi, j * 12 + (x + 1))
                dve.tensor_tensor(m_raw_r[x % 12], m_raw[x % 12], m_hi[x % 4].bitcast(F32),
                                  ALU.subtract).then_inc(s_mlo, 1)

            def rows_lo(n):
                for q in range(4):
                    dve.wait_ge(s_xehi, n + (q + 1))
                    dve.tensor_tensor(xe_lo[:, 4 * q:4 * q + 4, :].rearrange("p a b -> p (a b)"), ps[2 + q % 2][:, :],
                                      xe_hi[:, 4 * q:4 * q + 4, :].bitcast(F32).rearrange("p a b -> p (a b)"),
                                      ALU.subtract).then_inc(s_xelo, 1)

            for x in range(3):
                expert_lo(0, x)
            last_block = dve.value_load(plan[0:1, MAX_OVER + 1:MAX_OVER + 2], min_val=EXPERTS - 1, max_val=NB - 1)
            rows_lo(0)
            def block_turn(j, last):
                for x in range(3, 11):
                    expert_lo(j, x)
                dve.wait_ge(s_hsig, j + 1)
                ch.link(dve.tensor_tensor(h_e, h_sig, ps[0][:, :], ALU.mult))
                dve.wait_ge(s_mused, j * 12 + 20)
                dve.tensor_tensor(h_e, h_e, ps[1][:, :], ALU.mult).then_inc(s_h, 1)
                rows_lo(j * 4 + 4)
                dve.wait_ge(s_hthi, j + 1)
                dve.tensor_tensor(ht_lo.rearrange("p a b -> p (a b)"), ps[0][:, :],
                                  ht_hi.bitcast(F32).rearrange("p a b -> p (a b)"), ALU.subtract).then_inc(s_htlo, 1)
                for x in range(11, 12 if last else 15):
                    expert_lo(j, x)
                dve.wait_ge(s_ysc, j * 16)
                for b in range(2, 4):
                    if b == 2:
                        dve.wait_ge(s_ybank, j * 3 + 3)
                    else:
                        dve.wait_ge(s_mused, j * 12 + 24)
                    dve.tensor_copy(y_e[:, b * COLS:(b + 1) * COLS], ps[4 + b][:, :]).then_inc(s_ye_v, 1)

            with ch.loop(last_block, 1) as j:
                block_turn(j, False)
            block_turn(last_block, True)

            def combine(m):
                dve.wait_ge(s_f_in[m], f_in_base[m] + 32)
                y0, y1 = f_y[m]
                ch.link(dve.tensor_scalar(y0, y0, wts[:, 0, m:m + 1], None, ALU.mult))
                dve.scalar_tensor_tensor(y0, y1, wts[:, 1, m:m + 1], y0, ALU.mult, ALU.add).then_inc(s_f_y, 1)

            def last_residual(m):
                y0 = f_y[m][0]
                dve.wait_ge(s_f_ss, m + 1)
                ch.link(dve.reciprocal(ss_f[:, m:m + 1], ss_f[:, m:m + 1]))
                ch.link(dve.scalar_tensor_tensor(y0, y0, ss_f[:, m:m + 1], row_g2, ALU.mult, ALU.mult))
                dve.tensor_tensor(f_x[m], f_x[m], y0, ALU.add).then_inc(s_f_out, 1)

            combine(0)
            dve.wait_ge(s_g2, 16 * 5)
            for m in range(NT):
                if m + 1 < NT:
                    combine(m + 1)
                last_residual(m)


def kernel(**inputs):
    import numpy as _np
    import concourse.bacc as _bacc
    from concourse import mybir as _mybir
    from concourse.bass_utils import run_bass_kernel_spmd as _run

    nc = _bacc.Bacc("TRN2", target_bir_lowering=False, num_devices=1)
    planes, small = shape_constants()
    arrays, aps = {}, {}
    for name, x in {**inputs, "planes": planes, "small": small}.items():
        x = _np.ascontiguousarray(x)
        arrays[f"in_{name}_dram"] = x
        aps[name] = nc.dram_tensor(f"in_{name}_dram", x.shape, _mybir.dt.from_np(x.dtype), kind="ExternalInput").ap()
    out = nc.dram_tensor("out_dram", (1, SEQ, D), F32, kind="ExternalOutput").ap()

    def dram(name, shape, dt=F32):
        return nc.dram_tensor(f"{name}_dram", shape, dt).ap()

    build(nc, aps, out, dram)
    r = _run(nc, [arrays], core_ids=[0])
    return r.results[0]["out_dram"]
```
